# Optimizing a Trainium2 kernel written in Bass

```python
import math
import jax, jax.numpy as jnp
from jax import lax
import numpy as np

D_MODEL = 1024
BATCH = 1
SEQ = 512
DEPTH = 1

CHUNK = 64
H_A = 8
D_A = 64
H_I = 4
D_I = 64
TOPK_MAX = 256
SPARSE_Q_BLOCK = 32
H_B = 4
D_B = 64
DENSE_Q_BLOCK = 128
D_FF = ((8 * D_MODEL + 3 * 256 - 1) // (3 * 256)) * 256
RMS_EPS = 1e-6
MASK_VALUE = -1e30

W_QA = H_A * D_A
W_KA = H_A * D_A
W_VA = H_A * D_A
W_QB = H_B * 2 * D_B
W_KB = H_B * 2 * D_B
W_VB = H_B * 2 * D_B
W_QI = H_I * D_I
W_KI = D_I
W_WI = H_I
W_G = 2 * D_MODEL
_WIDTHS = [W_QA, W_KA, W_VA, W_QB, W_KB, W_VB, W_QI, W_KI, W_WI, W_G]
SPLITS = [int(v) for v in np.cumsum(_WIDTHS)[:-1]]
W_IN = int(sum(_WIDTHS))


def rms_norm(x, g):
    xf = x.astype(jnp.float32)
    y = xf * lax.rsqrt(jnp.mean(xf * xf, axis=-1, keepdims=True) + RMS_EPS)
    return (y * g.astype(jnp.float32)).astype(x.dtype)

def alibi_slopes(n):
    return jnp.asarray(2.0 ** (-8.0 * np.arange(1, n + 1) / n), dtype=jnp.float32)

def dsa_sparse_attention(q, k, v, q_idx, k_idx, w_idx):
    B, S = q.shape[0], q.shape[1]
    n_sel = min(TOPK_MAX, S // 4)
    nblk = S // SPARSE_Q_BLOCK
    slopes = alibi_slopes(H_A)
    key_chunk = jnp.arange(S) // CHUNK
    kif = k_idx.astype(jnp.float32)

    def to_blocks(a):
        return a.reshape((B, nblk, SPARSE_Q_BLOCK) + a.shape[2:]).swapaxes(0, 1)

    def block(args):
        i, qb, qib, wb = args
        t = i * SPARSE_Q_BLOCK + jnp.arange(SPARSE_Q_BLOCK)
        t_chunk = t // CHUNK
        admissible = key_chunk[None, :] <= t_chunk[:, None]
        logits = jnp.einsum('bqhd,bsd->bqhs', qib.astype(jnp.float32), kif)
        idx_score = jnp.einsum('bqh,bqhs->bqs', wb.astype(jnp.float32), jax.nn.relu(logits))
        idx_score = jnp.where(admissible[None], idx_score, -jnp.inf)
        _, sel = lax.top_k(idx_score, n_sel)
        valid = (sel // CHUNK) <= t_chunk[None, :, None]
        k_sel = jax.vmap(lambda kk, ii: kk[ii])(k, sel)
        v_sel = jax.vmap(lambda vv, ii: vv[ii])(v, sel)
        s = jnp.einsum('bqhd,bqkhd->bhqk', qb.astype(jnp.float32),
                       k_sel.astype(jnp.float32)) * (D_A ** -0.5)
        dist = jnp.abs(t[None, :, None] - sel).astype(jnp.float32)
        s = s - slopes[None, :, None, None] * dist[:, None]
        s = jnp.where(valid[:, None], s, MASK_VALUE)
        p = jax.nn.softmax(s, axis=-1)
        o = jnp.einsum('bhqk,bqkhd->bqhd', p, v_sel.astype(jnp.float32))
        return o.astype(q.dtype)

    out = lax.map(block, (jnp.arange(nblk), to_blocks(q), to_blocks(q_idx), to_blocks(w_idx)))
    return out.swapaxes(0, 1).reshape(B, S, H_A * D_A)

def differential_attention(q, k, v, lam, subln_g, lambda_init):
    B, S = q.shape[0], q.shape[1]
    nblk = S // DENSE_Q_BLOCK
    slopes = alibi_slopes(H_B)
    key_pos = jnp.arange(S)
    key_chunk = key_pos // CHUNK
    kf = k.astype(jnp.float32)
    vf = v.astype(jnp.float32)

    def block(args):
        i, qb = args
        t = i * DENSE_Q_BLOCK + jnp.arange(DENSE_Q_BLOCK)
        s = jnp.einsum('bqhmd,bshmd->bhmqs', qb.astype(jnp.float32), kf) * (D_B ** -0.5)
        dist = jnp.abs(t[:, None] - key_pos[None, :]).astype(jnp.float32)
        bias = -slopes[:, None, None, None] * dist[None, None]
        allowed = key_chunk[None, :] <= (t // CHUNK)[:, None]
        s = jnp.where(allowed, s + bias, MASK_VALUE)
        p = jax.nn.softmax(s, axis=-1)
        a = p[:, :, 0] - lam * p[:, :, 1]
        o = jnp.einsum('bhqs,bshe->bqhe', a, vf)
        o = rms_norm(o, subln_g) * (1.0 - lambda_init)
        return o.astype(q.dtype)

    qblk = q.reshape((B, nblk, DENSE_Q_BLOCK) + q.shape[2:]).swapaxes(0, 1)
    out = lax.map(block, (jnp.arange(nblk), qblk))
    return out.swapaxes(0, 1).reshape(B, S, H_B * 2 * D_B)

def first_inputs(seed: int = 0) -> dict:
    key = jax.random.key(seed)
    ks = jax.random.split(key, 24)
    f32 = jnp.float32

    def w(k, shape, fan_in, gain=1.0):
        return jax.random.normal(k, shape, f32) * (gain * fan_in ** -0.5)

    def g(k, n):
        return 1.0 + 0.02 * jax.random.normal(k, (DEPTH, n), f32)

    return {
        'x': jax.random.normal(ks[0], (BATCH, SEQ, D_MODEL), f32),
        'c': jax.random.normal(ks[1], (BATCH, D_MODEL), f32),
        'w_ada': w(ks[2], (DEPTH, D_MODEL, 6 * D_MODEL), D_MODEL, 0.5),
        'b_ada': 0.02 * jax.random.normal(ks[3], (DEPTH, 6 * D_MODEL), f32),
        'norm1_g': g(ks[4], D_MODEL),
        'w_in': w(ks[5], (DEPTH, D_MODEL, W_IN), D_MODEL),
        'qn_a': g(ks[6], D_A),
        'kn_a': g(ks[7], D_A),
        'qn_b': g(ks[8], D_B),
        'kn_b': g(ks[9], D_B),
        'lam_q1': 0.1 * jax.random.normal(ks[10], (DEPTH, D_B), f32),
        'lam_k1': 0.1 * jax.random.normal(ks[11], (DEPTH, D_B), f32),
        'lam_q2': 0.1 * jax.random.normal(ks[12], (DEPTH, D_B), f32),
        'lam_k2': 0.1 * jax.random.normal(ks[13], (DEPTH, D_B), f32),
        'subln_g': g(ks[14], 2 * D_B),
        'w_up_a': w(ks[15], (DEPTH, H_A * D_A, D_MODEL), H_A * D_A),
        'w_up_b': w(ks[16], (DEPTH, H_B * 2 * D_B, D_MODEL), H_B * 2 * D_B),
        'w_o': w(ks[17], (DEPTH, D_MODEL, D_MODEL), D_MODEL),
        'norm2_g': g(ks[18], D_MODEL),
        'w_ff1': w(ks[19], (DEPTH, D_MODEL, D_FF), D_MODEL),
        'w_ff3': w(ks[20], (DEPTH, D_MODEL, D_FF), D_MODEL),
        'w_ff2': w(ks[21], (DEPTH, D_FF, D_MODEL), D_FF),
    }

def first_block(x, c, w_ada, b_ada, norm1_g, w_in, qn_a, kn_a, qn_b, kn_b,
              lam_q1, lam_k1, lam_q2, lam_k2, subln_g, w_up_a, w_up_b, w_o,
              norm2_g, w_ff1, w_ff3, w_ff2):
    B, S = x.shape[0], x.shape[1]
    cs = jax.nn.silu(c)
    for l in range(DEPTH):
        lambda_init = 0.8 - 0.6 * math.exp(-0.3 * l)
        mod = cs @ w_ada[l] + b_ada[l]
        shift1, scale1, gate1, shift2, scale2, gate2 = jnp.split(mod, 6, axis=-1)

        h = rms_norm(x, norm1_g[l]) * (1.0 + scale1[:, None]) + shift1[:, None]
        proj = h @ w_in[l]
        qa, ka, va, qb, kb, vb, qi, ki, wi, gates = jnp.split(proj, SPLITS, axis=-1)

        qa = rms_norm(qa.reshape(B, S, H_A, D_A), qn_a[l])
        ka = rms_norm(ka.reshape(B, S, H_A, D_A), kn_a[l])
        va = va.reshape(B, S, H_A, D_A)
        y_a = dsa_sparse_attention(qa, ka, va, qi.reshape(B, S, H_I, D_I), ki, wi)

        qb = rms_norm(qb.reshape(B, S, H_B, 2, D_B), qn_b[l])
        kb = rms_norm(kb.reshape(B, S, H_B, 2, D_B), kn_b[l])
        vb = vb.reshape(B, S, H_B, 2 * D_B)
        lam = (jnp.exp(jnp.sum(lam_q1[l].astype(jnp.float32) * lam_k1[l].astype(jnp.float32)))
               - jnp.exp(jnp.sum(lam_q2[l].astype(jnp.float32) * lam_k2[l].astype(jnp.float32)))
               + lambda_init)
        y_b = differential_attention(qb, kb, vb, lam, subln_g[l], lambda_init)

        g_a, g_b = jnp.split(jax.nn.sigmoid(gates), 2, axis=-1)
        merged = g_a * (y_a @ w_up_a[l]) + g_b * (y_b @ w_up_b[l])
        x = x + gate1[:, None] * (merged @ w_o[l])

        h2 = rms_norm(x, norm2_g[l]) * (1.0 + scale2[:, None]) + shift2[:, None]
        ff = (jax.nn.silu(h2 @ w_ff1[l]) * (h2 @ w_ff3[l])) @ w_ff2[l]
        x = x + gate2[:, None] * ff
    return x


PLE_DIM = 256
RET_HEADS = 4
RET_QK_DIM = 256
RET_V_DIM = 512
RET_CHUNK = 128
MLA_HEADS = 8
MLA_NOPE_DIM = 128
MLA_ROPE_DIM = 64
MLA_QK_DIM = MLA_NOPE_DIM + MLA_ROPE_DIM
MLA_V_DIM = 128
MLA_Q_LORA = 384
MLA_KV_LORA = 256
ATTN_BLOCK = 128
D_FF_2 = 4 * D_MODEL
ROPE_BASE = 10000.0

RET_QK_W = RET_HEADS * RET_QK_DIM
RET_V_W = RET_HEADS * RET_V_DIM
MLA_V_W = MLA_HEADS * MLA_V_DIM
IN_SIZES = (RET_QK_W, RET_QK_W, RET_V_W, RET_V_W, MLA_Q_LORA, MLA_KV_LORA, MLA_ROPE_DIM, D_MODEL, D_MODEL)
IN_WIDTH = sum(IN_SIZES)


def rms_norm_2(x, gain):
    xf = x.astype(jnp.float32)
    y = xf * lax.rsqrt(jnp.mean(xf * xf, axis=-1, keepdims=True) + RMS_EPS)
    return (y * gain.astype(jnp.float32)).astype(x.dtype)

def rope(x, pos):
    half = x.shape[-1] // 2
    inv = ROPE_BASE ** (-jnp.arange(half, dtype=jnp.float32) / half)
    ang = pos.astype(jnp.float32)[:, :, None] * inv
    cos = jnp.cos(ang)[:, :, None, :]
    sin = jnp.sin(ang)[:, :, None, :]
    xf = x.astype(jnp.float32)
    x1, x2 = xf[..., :half], xf[..., half:]
    return jnp.concatenate([x1 * cos - x2 * sin, x2 * cos + x1 * sin], axis=-1).astype(x.dtype)

def retention(q, k, v):
    B, S, H, dk = q.shape
    dv = v.shape[-1]
    C = RET_CHUNK
    N = S // C
    log_g = jnp.log1p(-jnp.exp2(-5.0 - jnp.arange(H, dtype=jnp.float32)))
    idx = jnp.arange(C, dtype=jnp.float32)
    diff = idx[:, None] - idx[None, :]
    decay_in = jnp.where(diff >= 0, jnp.exp(jnp.maximum(diff, 0.0)[None] * log_g[:, None, None]), 0.0)
    q_dec = jnp.exp((idx + 1.0)[None, :] * log_g[:, None])
    k_dec = jnp.exp((C - 1.0 - idx)[None, :] * log_g[:, None])
    chunk_dec = jnp.exp(C * log_g)

    def to_chunks(t):
        return t.astype(jnp.float32).reshape(B, N, C, H, t.shape[-1]).transpose(1, 0, 3, 2, 4)

    def step(state, inp):
        qc, kc, vc = inp
        scores = jnp.einsum('bhnd,bhmd->bhnm', qc, kc) * decay_in
        o = (jnp.einsum('bhnm,bhmv->bhnv', scores, vc)
             + jnp.einsum('bhnd,bhdv->bhnv', qc, state) * q_dec[None, :, :, None])
        state = (state * chunk_dec[None, :, None, None]
                 + jnp.einsum('bhmd,bhmv->bhdv', kc * k_dec[None, :, :, None], vc))
        return state, o

    state0 = jnp.zeros((B, H, dk, dv), jnp.float32)
    _, o = lax.scan(step, state0, (to_chunks(q), to_chunks(k), to_chunks(v)))
    return o.transpose(1, 0, 3, 2, 4).reshape(B, S, H, dv).astype(v.dtype)

def causal_block_attention(q, k, v):
    B, S, H, D = q.shape
    nb = S // ATTN_BLOCK
    scale = D ** -0.5
    qb = q.reshape(B, nb, ATTN_BLOCK, H, D).transpose(1, 0, 2, 3, 4)
    key_pos = jnp.arange(S)

    def one(args):
        qi, bi = args
        s = jnp.einsum('bqhd,bkhd->bhqk', qi, k).astype(jnp.float32) * scale
        q_pos = bi * ATTN_BLOCK + jnp.arange(ATTN_BLOCK)
        s = jnp.where(key_pos[None, :] <= q_pos[:, None], s, -1e30)
        pr = jax.nn.softmax(s, axis=-1).astype(v.dtype)
        return jnp.einsum('bhqk,bkhv->bqhv', pr, v)

    o = lax.map(one, (qb, jnp.arange(nb)))
    return o.transpose(1, 0, 2, 3, 4).reshape(B, S, H, v.shape[-1])

def hybrid_layer(x, p_l, pos, norm_mix, w_in, ret_norm, q_lat_norm, kv_lat_norm, w_uq, w_ukv,
                 q_norm, k_norm, w_br, w_bm, w_o, norm_mlp, w_up, w_down, norm_ple, w_ple_gate, w_ple):
    B, S, _ = x.shape
    h = rms_norm_2(x, norm_mix)
    proj = h @ w_in
    offsets = np.cumsum(IN_SIZES)[:-1].tolist()
    rq, rk, rv, rg, cq, ckv, krope, gr, gm = jnp.split(proj, offsets, axis=-1)

    rq = rope(rq.reshape(B, S, RET_HEADS, RET_QK_DIM), pos)
    rk = rope(rk.reshape(B, S, RET_HEADS, RET_QK_DIM), pos) * (RET_QK_DIM ** -0.5)
    rv = rv.reshape(B, S, RET_HEADS, RET_V_DIM)
    ro = retention(rq, rk, rv)
    ro = rms_norm_2(ro, ret_norm.reshape(RET_HEADS, RET_V_DIM)).reshape(B, S, RET_V_W)
    a_ret = (ro * jax.nn.silu(rg)) @ w_br

    cq = rms_norm_2(cq, q_lat_norm)
    q = (cq @ w_uq).reshape(B, S, MLA_HEADS, MLA_QK_DIM)
    ckv = rms_norm_2(ckv, kv_lat_norm)
    kv = (ckv @ w_ukv).reshape(B, S, MLA_HEADS, MLA_NOPE_DIM + MLA_V_DIM)
    k_nope, v = kv[..., :MLA_NOPE_DIM], kv[..., MLA_NOPE_DIM:]
    k_rope = jnp.broadcast_to(krope[:, :, None, :], (B, S, MLA_HEADS, MLA_ROPE_DIM))
    k = jnp.concatenate([k_nope, k_rope], axis=-1)
    q = rms_norm_2(q, q_norm)
    k = rms_norm_2(k, k_norm)
    q = jnp.concatenate([q[..., :MLA_NOPE_DIM], rope(q[..., MLA_NOPE_DIM:], pos)], axis=-1)
    k = jnp.concatenate([k[..., :MLA_NOPE_DIM], rope(k[..., MLA_NOPE_DIM:], pos)], axis=-1)
    mo = causal_block_attention(q, k, v).reshape(B, S, MLA_V_W)
    a_mla = mo @ w_bm

    mixed = jax.nn.sigmoid(gr) * a_ret + jax.nn.sigmoid(gm) * a_mla
    x = x + mixed @ w_o

    h2 = rms_norm_2(x, norm_mlp)
    x = x + jnp.square(jax.nn.relu(h2 @ w_up)) @ w_down

    gate = jax.nn.sigmoid(rms_norm_2(x, norm_ple) @ w_ple_gate)
    x = x + gate * (p_l @ w_ple)
    return x

def second_inputs(seed: int = 0) -> dict:
    key = jax.random.key(seed)
    ks = jax.random.split(key, 24)

    def dense(k, shape, fan_in):
        return jax.random.normal(k, shape, jnp.float32) * (fan_in ** -0.5)

    def gain(k, n):
        return 1.0 + 0.05 * jax.random.normal(k, (DEPTH, n), jnp.float32)

    x = jax.random.normal(ks[0], (BATCH, SEQ, D_MODEL), jnp.float32)
    p = jax.random.normal(ks[1], (DEPTH, BATCH, SEQ, PLE_DIM), jnp.float32)
    offset = jax.random.randint(ks[2], (BATCH, 1), 0, 1024, dtype=jnp.int32)
    positions = offset + jnp.arange(SEQ, dtype=jnp.int32)[None, :]
    return {
        "x": x,
        "p": p,
        "positions": positions,
        "norm_mix": gain(ks[3], D_MODEL),
        "w_in": dense(ks[4], (DEPTH, D_MODEL, IN_WIDTH), D_MODEL),
        "ret_norm": gain(ks[5], RET_V_W),
        "q_lat_norm": gain(ks[6], MLA_Q_LORA),
        "kv_lat_norm": gain(ks[7], MLA_KV_LORA),
        "w_uq": dense(ks[8], (DEPTH, MLA_Q_LORA, MLA_HEADS * MLA_QK_DIM), MLA_Q_LORA),
        "w_ukv": dense(ks[9], (DEPTH, MLA_KV_LORA, MLA_HEADS * (MLA_NOPE_DIM + MLA_V_DIM)), MLA_KV_LORA),
        "q_norm": gain(ks[10], MLA_QK_DIM),
        "k_norm": gain(ks[11], MLA_QK_DIM),
        "w_br": dense(ks[12], (DEPTH, RET_V_W, D_MODEL), RET_V_W),
        "w_bm": dense(ks[13], (DEPTH, MLA_V_W, D_MODEL), MLA_V_W),
        "w_o": dense(ks[14], (DEPTH, D_MODEL, D_MODEL), D_MODEL),
        "norm_mlp": gain(ks[15], D_MODEL),
        "w_up": dense(ks[16], (DEPTH, D_MODEL, D_FF_2), D_MODEL),
        "w_down": dense(ks[17], (DEPTH, D_FF_2, D_MODEL), D_FF_2),
        "norm_ple": gain(ks[18], D_MODEL),
        "w_ple_gate": dense(ks[19], (DEPTH, D_MODEL, D_MODEL), D_MODEL),
        "w_ple": dense(ks[20], (DEPTH, PLE_DIM, D_MODEL), PLE_DIM),
    }

def second_block(x, p, positions, norm_mix, w_in, ret_norm, q_lat_norm, kv_lat_norm, w_uq, w_ukv,
              q_norm, k_norm, w_br, w_bm, w_o, norm_mlp, w_up, w_down, norm_ple, w_ple_gate, w_ple):
    for i in range(DEPTH):
        x = hybrid_layer(x, p[i], positions, norm_mix[i], w_in[i], ret_norm[i], q_lat_norm[i],
                         kv_lat_norm[i], w_uq[i], w_ukv[i], q_norm[i], k_norm[i], w_br[i], w_bm[i],
                         w_o[i], norm_mlp[i], w_up[i], w_down[i], norm_ple[i], w_ple_gate[i], w_ple[i])
    return x


def setup_inputs(seed=0):
    out = dict(first_inputs(seed))
    for name, value in second_inputs(seed + 1).items():
        if name != "x":
            out[name + "_2"] = value
    return out


def reference(
    x, c, w_ada, b_ada, norm1_g, w_in, qn_a, kn_a, qn_b, kn_b, lam_q1, lam_k1, lam_q2, lam_k2,
    subln_g, w_up_a, w_up_b, w_o, norm2_g, w_ff1, w_ff3, w_ff2, p_2, positions_2, norm_mix_2,
    w_in_2, ret_norm_2, q_lat_norm_2, kv_lat_norm_2, w_uq_2, w_ukv_2, q_norm_2, k_norm_2,
    w_br_2, w_bm_2, w_o_2, norm_mlp_2, w_up_2, w_down_2, norm_ple_2, w_ple_gate_2, w_ple_2,
):
    x = first_block(
        x, c, w_ada, b_ada, norm1_g, w_in, qn_a, kn_a, qn_b, kn_b, lam_q1, lam_k1, lam_q2,
        lam_k2, subln_g, w_up_a, w_up_b, w_o, norm2_g, w_ff1, w_ff3, w_ff2,
    )
    return second_block(
        x, p_2, positions_2, norm_mix_2, w_in_2, ret_norm_2, q_lat_norm_2, kv_lat_norm_2,
        w_uq_2, w_ukv_2, q_norm_2, k_norm_2, w_br_2, w_bm_2, w_o_2, norm_mlp_2, w_up_2,
        w_down_2, norm_ple_2, w_ple_gate_2, w_ple_2,
    )


_drawn_inputs = setup_inputs


def setup_inputs(seed=0):
    import zlib

    import numpy as np

    out = dict(_drawn_inputs(seed))
    spreads = {}
    factors = {'norm1_g': 4.252,
     'qn_a': 8.0,
     'kn_a': 8.0,
     'qn_b': 8.0,
     'kn_b': 8.0,
     'lam_q1': 8.0,
     'lam_q2': 4.88,
     'subln_g': 8.0,
     'norm2_g': 8.0,
     'ret_norm_2': 29.816,
     'q_lat_norm_2': 8.0,
     'kv_lat_norm_2': 8.0,
     'q_norm_2': 8.0,
     'k_norm_2': 8.0,
     'norm_ple_2': 200.0,
     'norm_mlp_2': 8.0,
     'p_2': 6.482,
     'w_ple_gate_2': 8.0,
     'w_ple_2': 6.469}
    for name, (base, spread) in spreads.items():
        noise = np.random.default_rng([zlib.crc32(name.encode()), seed]).standard_normal(out[name].shape)
        drawn = base * np.exp(spread * noise) if base else spread * noise
        out[name] = __import__('jax').numpy.asarray(drawn.astype(out[name].dtype))
    for name, factor in factors.items():
        out[name] = (out[name] * factor).astype(out[name].dtype)
    return out
```

```python
import math
from contextlib import ExitStack

import numpy as np
import concourse.bass as bass
from concourse import mybir

F32 = mybir.dt.float32
F32R = mybir.dt.float32r
I32 = mybir.dt.int32
ALU = mybir.AluOpType
ACT = mybir.ActivationFunctionType
AX = mybir.AxisListType.X
ds = bass.ds

P = 128
S = 512
QT = S // P
D = 1024
KD = D // P
EPS = 1e-6
CHUNK = 64
H_A, D_A = 8, 64
H_B = 4
H_I = 4
TOPK = 128
FF = 2816
KFF = FF // P
C_QA, C_KA, C_VA, C_QB, C_KB, C_VB, C_QI, C_KI, C_WI, C_G = (
    0, 512, 1024, 1536, 2048, 2560, 3072, 3328, 3392, 3396)
LAMBDA_INIT = 0.8 - 0.6 * math.exp(0.0)
R_QK, R_V, R_H = 256, 512, 4
C_RQ, C_RK, C_RV, C_RG, C_CQ, C_CKV, C_KR, C_GR, C_GM = (
    0, 1024, 2048, 4096, 6144, 6528, 6784, 6848, 7872)
M_H = 8
FF2 = 4096
FAR = 1e32
INADMISSIBLE = -3.0e38
TAKEN = -3.3e38
UW = 2048

VROWS = {}
_at = 0
for _n, _c in (("c", 8), ("norm1_g", 8), ("norm2_g", 8), ("norm_mix", 8), ("norm_mlp", 8),
               ("norm_ple", 8), ("b_ada", 48), ("ret_norm", 16), ("q_lat", 3), ("kv_lat", 2),
               ("subln", 1), ("qn_a", 1), ("kn_a", 1), ("qn_b", 1), ("kn_b", 1),
               ("q_nope", 1), ("q_rope", 1), ("k_nope", 1), ("k_rope", 1)):
    VROWS[_n] = _at
    _at += _c
NVR = _at

STAGES = [
    ("index", [2048, 8 * 132]),
    ("values", [2048] * 4),
    ("qk", [2048] * 8),
    ("merge", [2048, 1024] * 8),
    ("out1", [2048] * 4),
    ("ff1a", [2048] * 12), ("ff2a", [12 * P] * 8),
    ("ff1b", [2048] * 10), ("ff2b", [10 * P] * 8),
    ("retention", [2048] * 32),
    ("latent", [2048, 2048, 1024, 1024]),
    ("mla", [3 * 384, 2 * 512] * 4),
    ("merge2", [2048, 1024] * 8),
    ("out2", [2048] * 4),
    ("mlp", [2048] * 32),
    ("ple", [1024, 256] * 8),
]
U0, WIDTH = {}, []
for _n, _w in STAGES:
    U0[_n] = len(WIDTH)
    WIDTH += _w


class Count:

    def __init__(self, eng, sem):
        self.eng, self.sem, self.total, self.loop = eng, sem, 0, None

    def inc(self, ins):
        ins.then_inc(self.sem, 1)
        if self.loop is None:
            self.total += 1
            return self.total
        self.loop[2] += 1
        return self.total + self.loop[1] * self.loop[0] + self.loop[2]

    def step(self, ins):
        self.eng.wait_ge(self.sem, self.inc(ins))

    def enter(self, i, per):
        self.loop = [i, per, 0]

    def leave(self, times):
        assert self.loop[2] == self.loop[1], f"{self.sem}: {self.loop[2]} steps per turn, not {self.loop[1]}"
        self.total += self.loop[1] * times
        self.loop = None


def rows(ap, parts=P):
    return ap.rearrange("(k p) n -> p k n", p=parts)


def two_layers(nc, A, out):
    ctx = ExitStack()

    def sbuf(name, shape, dt=F32, at=ctx):
        return at.enter_context(nc.sbuf_tensor(name, shape, dt))

    sems = {}

    def sem(name):
        if name not in sems:
            sems[name] = ctx.enter_context(nc.semaphore(name))
        return sems[name]

    with ctx:
        xT = sbuf("xT", [P, KD, S])
        raw = sbuf("raw", [P, 2, UW])
        w_hi = sbuf("w_hi", [P, 2, UW], F32R)
        w_lo = sbuf("w_lo", [P, 2, UW], F32R)
        h_hi = sbuf("h_hi", [P, KD, S], F32R)
        h_lo = sbuf("h_lo", [P, KD, S], F32R)
        ident = sbuf("ident", [P, P])
        ones = sbuf("ones", [P, P])
        vT = sbuf("vT", [P, NVR])
        modc = sbuf("modc", [P, 48])
        gs1 = sbuf("gs1", [P, KD])
        gs2 = sbuf("gs2", [P, KD])
        eps = sbuf("eps", [P, 1])
        small = sbuf("small", [P, 32])
        lam = sbuf("lam", [P, 1])
        tri = sbuf("tri", [P, P])
        turn = sbuf("turn", [P, P])
        consts = sbuf("consts", [P, 8])
        cs = sbuf("cs", [P, 3 * KD])
        half = sbuf("half", [P, 2])
        stat = sbuf("stat", [P, 48])

        SH1, SC1, GT1, SH2, SC2, GT2 = (modc[:, KD * n:KD * (n + 1)] for n in range(6))

        def vcol(name, n=0):
            return vT[:, VROWS[name] + n:VROWS[name] + n + 1]

        layer1 = ExitStack()
        y_a = sbuf("y_a", [P, QT, 512], at=layer1)
        y_b = sbuf("y_b", [P, QT, 512], at=layer1)
        start = ExitStack()
        x_in = sbuf("x_in", [P, QT, D], at=start)
        x_n = sbuf("x_n", [P, QT, D], at=start)
        ada = sbuf("ada", [P, UW], at=start)
        ada_w = sbuf("ada_w", [P, 4, UW], at=start)
        vrows = sbuf("vrows", [P, P], at=start)
        lrow = sbuf("lrow", [1, 4 * D_A], at=start)
        lsum = sbuf("lsum", [1, 8], at=start)
        h_t = sbuf("h_t", [P, 2, S], at=start)
        start.close()
        attn = ExitStack()
        qaT = sbuf("qaT", [P, 4, S], at=attn)
        kaT = sbuf("kaT", [P, 4, S], at=attn)
        qbT = sbuf("qbT", [P, 4, S], at=attn)
        kbT = sbuf("kbT", [P, 4, S], at=attn)
        va = sbuf("va", [P, QT, 512], at=attn)
        vb = sbuf("vb", [P, QT, 512], at=attn)
        qiT = sbuf("qiT", [P, 2, S], at=attn)
        kiT = sbuf("kiT", [P, S], at=attn)
        wi = sbuf("wi", [P, QT, H_I], at=attn)
        dist_b = sbuf("dist_b", [P, QT, S], at=attn)
        dist_a = sbuf("dist_a", [P, QT, S], at=attn)
        t1 = sbuf("t1", [P, 2, S], at=attn)
        t2 = sbuf("t2", [P, 2, S], at=attn)
        t3 = sbuf("t3", [P, 2, S], at=attn)
        top8 = sbuf("top8", [P, 8], at=attn)
        slope = sbuf("slope", [P, H_A + H_B], at=attn)
        dist_i = sbuf("dist_i", [P, S], I32, at=attn)
        halves = sbuf("halves", [P, P], at=attn)
        attn.close()
        merge = ExitStack()
        y_hi = sbuf("y_hi", [P, 8, S], F32R, at=merge)
        y_lo = sbuf("y_lo", [P, 8, S], F32R, at=merge)
        m_hi = sbuf("m_hi", [P, 8, S], F32R, at=merge)
        m_lo = sbuf("m_lo", [P, 8, S], F32R, at=merge)
        mt = sbuf("mt", [P, 3, S], at=merge)
        ada2 = sbuf("ada2", [P, 2, UW], at=merge)
        merge.close()
        layer1.close()

        nt = sbuf("nt", [P, 6, S])
        trigs = sbuf("trigs", [P, 4, S])
        ff_mem = ExitStack()
        g_hi = sbuf("g_hi", [P, 12, S], F32R, at=ff_mem)
        g_lo = sbuf("g_lo", [P, 12, S], F32R, at=ff_mem)
        ft = sbuf("ft", [P, 3, S], at=ff_mem)
        pos_i = sbuf("pos_i", [P, S], I32, at=ff_mem)
        ff_mem.close()
        aret = sbuf("aret", [P, KD, S])
        ret_mem = ExitStack()
        rqT = sbuf("rqT", [P, 2, S], at=ret_mem)
        rkT = sbuf("rkT", [P, 2, S], at=ret_mem)
        rv = sbuf("rv", [P, QT, S], at=ret_mem)
        rs_t = sbuf("rs_t", [P, QT, S], at=ret_mem)
        sg = sbuf("sg", [P, 4, S], at=ret_mem)
        yr_hi = sbuf("yr_hi", [P, 4, S], F32R, at=ret_mem)
        yr_lo = sbuf("yr_lo", [P, 4, S], F32R, at=ret_mem)
        rt = sbuf("rt", [P, 4, S], at=ret_mem)
        etab = sbuf("etab", [P, S], at=ret_mem)
        dtab = sbuf("dtab", [P, S], at=ret_mem)
        dtab_i = sbuf("dtab_i", [P, S], I32, at=ret_mem)
        ret_mem.close()
        mla_out = ExitStack()
        mo_hi = sbuf("mo_hi", [P, 8, S], F32R, at=mla_out)
        mo_lo = sbuf("mo_lo", [P, 8, S], F32R, at=mla_out)
        mla_mem = ExitStack()
        lat_hi = sbuf("lat_hi", [P, 5, S], F32R, at=mla_mem)
        lat_lo = sbuf("lat_lo", [P, 5, S], F32R, at=mla_mem)
        krr = sbuf("krr", [P, S], at=mla_mem)
        lat_mem = ExitStack()
        lat_t = sbuf("lat_t", [P, 5, S], at=lat_mem)
        krT = sbuf("krT", [P, S], at=lat_mem)
        lat_mem.close()
        qn = sbuf("qn", [P, 2, S], at=mla_mem)
        kn = sbuf("kn", [P, 2, S], at=mla_mem)
        qr = sbuf("qr", [P, S], at=mla_mem)
        vv = sbuf("vv", [P, QT, 256], at=mla_mem)
        mo_t = sbuf("mo_t", [P, QT, 256], at=mla_mem)
        kw = mo_t[:].rearrange("p t (h c) -> p (t h) c", h=2)
        cst = sbuf("cst", [P, 48], at=mla_mem)
        qrg = nt[:, 5, :]
        kr2 = trigs[:, 0:2, :]
        qt2 = nt[:, 0:2, :]
        mla_mem.close()
        m2_hi = sbuf("m2_hi", [P, 8, S], F32R, at=mla_out)
        m2_lo = sbuf("m2_lo", [P, 8, S], F32R, at=mla_out)
        mla_out.close()
        u_hi = sbuf("u_hi", [P, KD, S], F32R)
        u_lo = sbuf("u_lo", [P, KD, S], F32R)
        p_in = sbuf("p_in", [P, QT, 256])
        p_hi = sbuf("p_hi", [P, 2, S], F32R)
        p_lo = sbuf("p_lo", [P, 2, S], F32R)
        out_sb = sbuf("out_sb", [P, QT, D])

        bank = [ctx.enter_context(nc.psum_tensor(f"bank{n}", [P, 512], F32)) for n in range(8)]

        raw_in = [sem("raw_in0"), sem("raw_in1")]
        hi_done, lo_done, mm_done, banks_free = sem("hi_done"), sem("lo_done"), sem("mm_done"), sem("banks_free")

        def raw_ready(u, slot):
            return 32 * (u - slot) + 64

        tok = "p t n -> p (t n)"
        ada_in1 = [raw[:, 0, :], raw[:, 1, :]] + [ada_w[:, n, :] for n in range(4)] + [y_a[:].rearrange(tok), y_b[:].rearrange(tok)]
        ada2_all = ada2[:].rearrange("p g n -> p (g n)")
        ada_in2 = [y_a[:].rearrange(tok), y_b[:].rearrange(tok)]

        block = ctx.enter_context(nc.Block())

        @block.sync
        def _(sp):
            def load(u, slot, pieces):
                if not isinstance(u, int) or u >= 2:
                    sp.wait_ge(lo_done, u - 1)
                if not isinstance(u, int):
                    sp.sem_inc(sem("slots_seen_free"), 1)
                for dst, src in pieces:
                    sp.dma_start(dst, src).then_inc(raw_in[slot], 64 // len(pieces))

            def slot_view(slot, k, n, at=0, width=None):
                width = width or n
                v = raw[:, slot, 0:k * width].rearrange("p (k n) -> p k n", k=k)
                return v[:, :, at:at + n]

            def prologue():
                sp.dma_start(x_in[:], A["x"][0].rearrange("(t p) n -> p t n", p=P)).then_inc(sem("x_in_done"), 16)
                for k, dst in enumerate(ada_in1):
                    if k == 2:
                        sp.wait_ge(sem("vectors_in"), 16 * 13)
                        sp.wait_ge(sem("head_vectors_in"), 16 * 6)
                    sp.dma_start(dst, A["w_ada"][0, k * P:k * P + P, 0:UW]).then_inc(sem(f"ada_in{k}"), 16)
                sp.wait_ge(sem("ada_free"), 2)

            w_in = rows(A["w_in"][0])

            def index():
                u = U0["index"]
                load(u, 0, [(slot_view(0, KD, 256), w_in[:, :, C_QI:C_QI + 256])])
                load(u + 1, 1, [(slot_view(1, KD, 64, 0, 132), w_in[:, :, C_KI:C_KI + 64]),
                                (slot_view(1, KD, 68, 64, 132), w_in[:, :, C_KI:C_KI + 68])])

            def values():
                for n, c in enumerate((C_VA, C_VB)):
                    for half in range(2):
                        load(U0["values"] + 2 * n + half, half,
                             [(slot_view(half, 4, 512), w_in[:, 4 * half:4 * half + 4, c:c + 512])])

            def qk():
                with sp.Fori(0, 4) as i:
                    for slot, (c0, c1) in enumerate(((C_QA, C_KA), (C_QB, C_KB))):
                        load(U0["qk"] + 2 * i + slot, slot,
                             [(slot_view(slot, KD, P, P * n, 256), w_in[:, :, ds(i * P + c, P)])
                              for n, c in enumerate((c0, c1))])

            def merge_loads():
                up_a, up_b = rows(A["w_up_a"][0]), rows(A["w_up_b"][0])
                with sp.Fori(0, KD) as i:
                    load(U0["merge"] + 2 * i, 0,
                         [(slot_view(0, KD, P, P * n, 256), w_in[:, :, ds(i * P + (C_G + D * n), P)])
                          for n in range(2)])
                    load(U0["merge"] + 2 * i + 1, 1,
                         [(slot_view(1, 4, P, P * n, 256), w[:, :, ds(i * P, P)])
                          for n, w in enumerate((up_a, up_b))])
                    sp.wait_ge(sem("y_mm"), 8)
                    for n in range(2):
                        sp.wait_ge(sem("ada_free"), 2 * i + (KD - 1 + n))
                        sp.sem_inc(sem("slots_seen_free"), 1)
                        sp.dma_start(ada_in2[n], A["w_ada"][0][ds(i * P, P), UW * (n + 1):UW * (n + 2)]
                                     ).then_inc(sem(f"ada_in{n}"), 16)

            def out1():
                w_o = rows(A["w_o"][0])
                with sp.Fori(0, 2) as i:
                    for slot in range(2):
                        load(U0["out1"] + 2 * i + slot, slot,
                             [(slot_view(slot, KD, 256), w_o[:, :, ds(i * 512 + 256 * slot, 256)])])

            def ff():
                w1, w3, w2 = rows(A["w_ff1"][0]), rows(A["w_ff3"][0]), rows(A["w_ff2"][0])
                for part, k0, k1 in (("a", 0, 12), ("b", 12, KFF)):
                    with sp.Fori(0, (k1 - k0) // 2) as i:
                        for slot in range(2):
                            load(U0["ff1" + part] + 2 * i + slot, slot,
                                 [(slot_view(slot, KD, P, P * n, 256), w[:, :, ds(i * 256 + (k0 + slot) * P, P)])
                                  for n, w in enumerate((w1, w3))])
                    with sp.Fori(0, KD // 2) as i:
                        for slot in range(2):
                            load(U0["ff2" + part] + 2 * i + slot, slot,
                                 [(slot_view(slot, k1 - k0, P), w2[:, k0:k1, ds(i * 256 + slot * P, P)])])

            w_in2 = rows(A["w_in_2"][0])

            def retention():
                w_br = rows(A["w_br_2"][0])
                with sp.Fori(0, R_H) as i:
                    u = U0["retention"] + 8 * i
                    for n, c in ((0, C_RQ), (1, C_RK)):
                        load(u + n, n, [(slot_view(n, KD, 256), w_in2[:, :, ds(i * R_QK + c, 256)])])
                    for half in range(2):
                        load(u + 2 + half, half, [(slot_view(half, 4, 512),
                                                   w_in2[:, 4 * half:4 * half + 4, ds(i * R_V + C_RV, 512)])])
                    for half in range(2):
                        load(u + 4 + half, half, [(slot_view(half, KD, 256),
                                                   w_in2[:, :, ds(i * R_V + (C_RG + 256 * half), 256)])])
                    for half in range(2):
                        load(u + 6 + half, half, [(slot_view(half, 4, 512),
                                                   w_br[:, ds(i * 4, 4), 512 * half:512 * half + 512])])

            def latent():
                u = U0["latent"]
                load(u, 0, [(slot_view(0, KD, 256), w_in2[:, :, C_CQ:C_CQ + 256])])
                load(u + 1, 1, [(slot_view(1, KD, 256), w_in2[:, :, C_CQ + 256:C_CQ + 512])])
                load(u + 2, 0, [(slot_view(0, KD, P), w_in2[:, :, C_CKV + P:C_CKV + 256])])
                load(u + 3, 1, [(slot_view(1, KD, 64, 64 * n, P), w_in2[:, :, C_KR:C_KR + 64]) for n in range(2)])

            def mla():
                w_uq, w_ukv = rows(A["w_uq_2"][0]), rows(A["w_ukv_2"][0])
                with sp.Fori(0, M_H // 2) as i:
                    u = U0["mla"] + 2 * i
                    q = w_uq[:, :, ds(i * 384, 384)].rearrange("p k (h c) -> p k h c", h=2)
                    load(u, 0, [(slot_view(0, 3, n, at + n * hh, 384), q[:, :, hh, c:c + n])
                                for at, c, n in ((0, 0, P), (2 * P, P, 64)) for hh in range(2)])
                    load(u + 1, 1, [(slot_view(1, 2, 512), w_ukv[:, :, ds(i * 512, 512)])])

            def merge2_loads():
                w_bm = rows(A["w_bm_2"][0])
                with sp.Fori(0, KD) as i:
                    load(U0["merge2"] + 2 * i, 0,
                         [(slot_view(0, KD, P, P * n, 256), w_in2[:, :, ds(i * P + (C_GR + D * n), P)])
                          for n in range(2)])
                    load(U0["merge2"] + 2 * i + 1, 1, [(slot_view(1, KD, P), w_bm[:, :, ds(i * P, P)])])

            def out2():
                w_o = rows(A["w_o_2"][0])
                with sp.Fori(0, 2) as i:
                    for slot in range(2):
                        load(U0["out2"] + 2 * i + slot, slot,
                             [(slot_view(slot, KD, 256), w_o[:, :, ds(i * 512 + 256 * slot, 256)])])

            def mlp():
                w_up, w_down = rows(A["w_up_2"][0]), rows(A["w_down_2"][0])
                with sp.Fori(0, 4) as i:
                    u = U0["mlp"] + 8 * i
                    for k in range(4):
                        load(u + k, k % 2, [(slot_view(k % 2, KD, 256), w_up[:, :, ds(i * D + 256 * k, 256)])])
                    for k in range(4):
                        load(u + 4 + k, k % 2, [(slot_view(k % 2, KD, 256),
                                                 w_down[:, ds(i * KD, KD), 256 * k:256 * k + 256])])

            def ple():
                w_g, w_p = rows(A["w_ple_gate_2"][0]), rows(A["w_ple_2"][0])
                with sp.Fori(0, KD) as i:
                    load(U0["ple"] + 2 * i, 0, [(slot_view(0, KD, P), w_g[:, :, ds(i * P, P)])])
                    load(U0["ple"] + 2 * i + 1, 1, [(slot_view(1, 2, P), w_p[:, :, ds(i * P, P)])])
                out_v = out[0].rearrange("(t p) n -> p t n", p=P)
                for t in range(QT):
                    sp.wait_ge(sem("out_tile_ready"), 2 * t + 2)
                    sp.dma_start(out_v[:, t, :], out_sb[:, t, :]).then_inc(sem("out_written"), 16)
                sp.wait_ge(sem("out_written"), 16 * QT)

            prologue()
            index()
            values()
            qk()
            merge_loads()
            out1()
            ff()
            retention()
            latent()
            mla()
            merge2_loads()
            out2()
            mlp()
            ple()

        @block.gpsimd
        def _(pool):
            own = Count(pool, sem("pool_steps"))

            def prologue():
                row = VROWS
                for name, ap, lo in (("qn_a", A["qn_a"], 0), ("kn_a", A["kn_a"], 0), ("qn_b", A["qn_b"], 0),
                                     ("kn_b", A["kn_b"], 0), ("q_rope", A["q_norm_2"], P),
                                     ("k_rope", A["k_norm_2"], P)):
                    nc.gpsimd.dma_start(vrows[row[name]:row[name] + 1, :].rearrange("o (h n) -> o h n", h=2),
                                        ap[0:1, lo:lo + 64].unsqueeze(1).to_broadcast([1, 2, 64])
                                        ).then_inc(sem("head_vectors_in"), 16)
                own.step(nc.gpsimd.memset(ident[:], 0.0))
                own.step(nc.gpsimd.memset(halves[:], 0.0))
                nc.gpsimd.memset(ones[:], 1.0).then_inc(sem("ones_ready"), 1)
                nc.gpsimd.affine_select(out=ident[:], in_=ident[:], compare_op=ALU.not_equal, fill=1.0, base=0,
                                        pattern=[[-1, P]], channel_multiplier=1).then_inc(sem("ident_ready"), 1)
                own.step(nc.gpsimd.memset(halves[0:64, 0:64], 1.0))
                nc.gpsimd.memset(halves[64:P, 64:P], 1.0).then_inc(sem("halves_ready"), 1)

            def distances():
                pool.wait_ge(sem("h_made"), KD)
                pool.wait_ge(sem("halves_ready"), 1)
                for n in range(H_A):
                    nc.gpsimd.memset(slope[:, n:n + 1], -2.0 ** (-8.0 * (n + 1) / H_A)).then_inc(sem("slopes_ready"), 1)
                for n in range(H_B):
                    nc.gpsimd.memset(slope[:, H_A + n:H_A + n + 1], -2.0 ** (-8.0 * (n + 1) / H_B)
                                     ).then_inc(sem("slopes_ready"), 1)
                for t in range(QT):
                    own.step(nc.gpsimd.iota(dist_i[:], pattern=[[-1, S]], base=t * P, channel_multiplier=1))
                    own.step(nc.gpsimd.tensor_copy(dist_b[:, t, :], dist_i[:]))
                    own.step(nc.gpsimd.tensor_scalar(t3[:, 0, :], dist_b[:, t, :], 0.0, 2.0, ALU.max, ALU.mult))
                    own.step(nc.gpsimd.tensor_tensor(dist_b[:, t, :], t3[:, 0, :], dist_b[:, t, :], ALU.subtract))
                    nc.gpsimd.memset(dist_b[0:64, t, t * P + 64:t * P + P], FAR).then_inc(sem("dist_ready"), 1)

            def attn_copies(name, q, k, per):
                with pool.Fori(0, 4) as i:
                    pool.wait_ge(sem(name + "_scores"), per * i)
                    nc.gpsimd.tensor_copy(t3[:, 0, :], q[:, ds(i, 1), :]).then_inc(sem(name + "_pair"), 1)
                    nc.gpsimd.tensor_copy(t3[:, 1, :], k[:, ds(i, 1), :]).then_inc(sem(name + "_pair"), 1)

            def attn_a():
                pool.wait_ge(banks_free, U0["qk"] + 8)
                attn_copies("a", qaT, kaT, 8)

            def attn_b():
                pool.wait_ge(sem("a_scores"), 32)
                attn_copies("b", qbT, kbT, 8)

            def clear_ada():
                pool.wait_ge(sem("y_made"), 8)
                nc.gpsimd.memset(ada2[:], 0.0).then_inc(sem("ada_clear"), 1)

            def masks():
                pool.wait_ge(mm_done, U0["ff1a"])
                nc.gpsimd.dma_start(pos_i[:], A["positions_2"][0, :].partition_broadcast(P)).then_inc(sem("positions_in"), 16)
                nc.gpsimd.dma_start(consts[:], A["shape_constants"]).then_inc(sem("consts_in"), 16)
                own.step(nc.gpsimd.memset(tri[:], 0.0))
                own.step(nc.gpsimd.affine_select(out=tri[:], in_=tri[:], compare_op=ALU.is_ge, fill=-1e30, base=0,
                                                 pattern=[[-1, P]], channel_multiplier=1))
                own.step(nc.gpsimd.memset(turn[:], 0.0))
                own.step(nc.gpsimd.memset(half[:], 0.0))
                for n in range(2):
                    own.step(nc.gpsimd.memset(half[64 * n:64 * n + 64, n:n + 1], 1.0))
                for at, sign in ((0, 1.0), (32, -1.0), (64, 1.0), (96, -1.0)):
                    blk = turn[at:at + 32, at + 32:at + 64] if sign > 0 else turn[at:at + 32, at - 32:at]
                    own.step(nc.gpsimd.affine_select(out=blk, in_=blk, compare_op=ALU.not_equal, fill=sign, base=0,
                                                     pattern=[[-1, 32]], channel_multiplier=1))
                nc.gpsimd.memset(small[:, 30:31], 0.0).then_inc(sem("masks_ready"), 1)

            def decays():
                pool.wait_ge(sem("hidden"), KFF)
                pool.wait_ge(mm_done, U0["retention"])
                pool.wait_ge(sem("masks_ready"), 1)
                own.step(nc.gpsimd.iota(dtab_i[:], pattern=[[1, S]], base=0, channel_multiplier=-1))
                own.step(nc.gpsimd.tensor_copy(dtab[:], dtab_i[:]))
                nc.gpsimd.affine_select(out=dtab[:], in_=dtab[:], compare_op=ALU.is_ge, fill=1e30, base=0,
                                        pattern=[[1, S]], channel_multiplier=-1).then_inc(sem("dtab_ready"), 1)
                pool.wait_ge(sem("dtab_ready"), 1)
                nc.gpsimd.memset(aret[:], 0.0).then_inc(sem("aret_clear"), 1)

            def ple():
                pool.wait_ge(mm_done, U0["ple"])
                nc.gpsimd.dma_start(p_in[:], A["p_2"][0, 0].rearrange("(t p) n -> p t n", p=P)).then_inc(sem("p_in_done"), 16)

            prologue()
            distances()
            attn_a()
            attn_b()
            clear_ada()
            masks()
            decays()
            ple()

        @block.tensor
        def _(pe):
            def mm3(dst, ws, xs, cols=None):
                terms = [(a, b) for (a_hi, a_lo), (b_hi, b_lo) in zip(ws, xs)
                         for a, b in ((a_hi, b_hi), (a_hi, b_lo), (a_lo, b_hi))]
                for n, (a, b) in enumerate(terms):
                    last = nc.tensor.matmul(dst, a, b, start=n == 0, stop=n == len(terms) - 1)
                return last

            def unit_ready(u):
                pe.wait_ge(lo_done, u + 1)
                if not isinstance(u, int) or u >= 2:
                    pe.wait_ge(banks_free, u - 1)

            def w_tile(slot, k, row, col, n=P):
                a = k * row + col
                return w_hi[:, slot, a:a + n], w_lo[:, slot, a:a + n]

            h = [(h_hi[:, k, :], h_lo[:, k, :]) for k in range(KD)]

            def h_tok(k, t):
                return h_hi[:, k, t * P:t * P + P], h_lo[:, k, t * P:t * P + P]

            def pair_unit(u, slot, xs, made=None):
                unit_ready(u)
                tiles_by_k([(bank[2 * slot + n][:], P * n) for n in range(2)], slot, 256, xs, made)

            def tiles_by_k(dsts, slot, row, xs, made=None):
                last_k = len(xs) - 1
                for k, (x_hi, x_lo) in enumerate(xs):
                    if made:
                        pe.wait_ge(made[0], made[1] + k + 1)
                    for dst, col in dsts:
                        a_hi, a_lo = w_tile(slot, k, row, col)
                        for n, (a, b) in enumerate(((a_hi, x_hi), (a_hi, x_lo), (a_lo, x_hi))):
                            last = nc.tensor.matmul(dst, a, b, start=k == n == 0, stop=k == last_k and n == 2)
                last.then_inc(mm_done, 1)

            def ada_columns(dst, sums, tiles):
                for m in tiles:
                    last = nc.tensor.matmul(dst[:, m:m + 1], sums[:, m * P:m * P + P], ones[:, 0:1], start=True, stop=True)
                last.then_inc(sem("ada_mm"), 1)

            def prologue():
                pe.wait_ge(sem("ident_ready"), 1)
                pe.wait_ge(sem("vectors_in"), 16 * 13)
                pe.wait_ge(sem("head_vectors_in"), 16 * 6)
                nc.tensor.transpose(bank[4][:, 0:NVR], vrows[0:NVR, :], ident[0:NVR, 0:NVR]).then_inc(sem("vT_mm"), 1)
                pe.wait_ge(sem("x_in_done"), 16)
                def turn(which, f):
                    for t in range(QT):
                        if which and f == 0:
                            pe.wait_ge(sem("x_n_ready"), t + 1)
                        if t == 0 and which and f >= 4:
                            pe.wait_ge(sem("h_t_ready"), f - 3)
                        elif t == 0 and (which or f >= 4):
                            pe.wait_ge(sem("xT_ready"), f + 5 if which else f - 3)
                        last = nc.tensor.transpose(bank[f % 4][:, t * P:t * P + P], (x_in, x_n)[which][:, t, f * P:f * P + P],
                                                   ident[:])
                    last.then_inc(sem("x_mm"), 1)

                for f in range(KD):
                    turn(0, f)
                for f in range(4):
                    turn(1, f)
                pe.wait_ge(sem("ones_ready"), 1)
                pe.wait_ge(sem("lambda_sum"), 1)
                nc.tensor.matmul(bank[5][:, 0:1], ones[0:1, :], lsum[0:1, 4:5], start=True, stop=True
                                 ).then_inc(sem("lambda_mm"), 1)
                pe.wait_ge(sem("ada_free"), KD)
                ada_columns(bank[6], ada[:], range(2 * KD))
                for f in range(4, KD):
                    turn(1, f)

            def index():
                u = U0["index"]
                pe.wait_ge(sem("h_t_ready"), KD)
                pair_unit(u, 0, h, (sem("h_made"), 0))
                unit_ready(u + 1)
                mm3(bank[2][:], [w_tile(1, k, 132, 0) for k in range(KD)], h)
                for t in range(QT):
                    last = mm3(bank[3][:, 4 * t:4 * t + 4], [h_tok(k, t) for k in range(KD)],
                               [w_tile(1, k, 132, P, 4) for k in range(KD)])
                last.then_inc(mm_done, 1)

            def value_pair(u):
                for half in range(2):
                    pe.wait_ge(lo_done, u + half + 1)
                    if half == 0:
                        pe.wait_ge(banks_free, u)
                    for t in range(QT):
                        for k in range(4):
                            (a_hi, a_lo), (b_hi, b_lo) = h_tok(4 * half + k, t), w_tile(half, k, 512, 0, 512)
                            for n, (a, b) in enumerate(((a_hi, b_hi), (a_hi, b_lo), (a_lo, b_hi))):
                                last = nc.tensor.matmul(bank[t][:], a, b, start=half == k == n == 0,
                                                        stop=half == 1 and k == 3 and n == 2)
                    last.then_inc(mm_done, 1)

            def values():
                value_pair(U0["values"])
                value_pair(U0["values"] + 2)

            def qk():
                pe.wait_ge(sem("halves_ready"), 1)
                with pe.Fori(0, 4) as i:
                    for slot in range(2):
                        unit_ready(U0["qk"] + 2 * i + slot)
                        for n in range(2):
                            last = mm3(bank[2 * slot + n][:], [w_tile(slot, k, 256, P * n) for k in range(KD)], h)
                            if slot == 1 and n == 0:
                                head_sums(i, 0)
                        last.then_inc(mm_done, 1)
                    head_sums(i, 1)

            def head_sums(i, slot):
                for n in range(2):
                    pe.wait_ge(sem("qk_squares"), 4 * i + (2 * slot + n + 1))
                    pe.wait_ge(sem("qk_std"), 4 * i + max(2 * slot + n - 1, 0))
                    nc.tensor.matmul(bank[4 + n][:], halves[:], t1[:, n, :], start=True, stop=True
                                     ).then_inc(sem("qk_sums"), 1)

            def topk():
                pe.wait_ge(sem("index_ready"), 2)
                g = 0
                for t in range(QT):
                    w = (t + 1) * P
                    for hh in range(H_I):
                        if g >= 4:
                            pe.wait_ge(sem("logits_read"), g - 3)
                        lo = 64 * (hh % 2)
                        nc.tensor.matmul(bank[4 + g % 4][:, 0:w], qiT[lo:lo + 64, hh // 2, t * P:t * P + P],
                                         kiT[lo:lo + 64, 0:w], start=True, stop=True).then_inc(sem("logits_mm"), 1)
                        g += 1

            def prev(i, per, n):
                return per * i + max(n - 1, 0)

            def attn_a():
                pe.wait_ge(banks_free, U0["qk"] + 8)
                pe.wait_ge(sem("logits_read"), QT * H_I)
                with pe.Fori(0, 4) as i:
                    def scores(n):
                        hh, t = divmod(n, QT)
                        pe.wait_ge(sem("a_pair"), 2 * i + 2)
                        pe.wait_ge(sem("a_biased"), prev(i, 8, n))
                        lo = 64 * hh
                        nc.tensor.matmul(bank[4 + n % 2][:, 0:(t + 1) * P], t3[lo:lo + 64, 0, t * P:t * P + P],
                                         t3[lo:lo + 64, 1, 0:(t + 1) * P], start=True, stop=True
                                         ).then_inc(sem("a_scores"), 1)

                    def turn_p(n):
                        pe.wait_ge(sem("a_exp"), 8 * i + (n + 1))
                        pe.wait_ge(sem("a_pT"), prev(i, 8, n))
                        for j in range(n % QT + 1):
                            last = nc.tensor.transpose(bank[6 + n % 2][:, j * P:j * P + P], t1[:, n % 2, j * P:j * P + P], ident[:])
                        last.then_inc(sem("a_turned"), 1)

                    def weigh(n):
                        hh, t = divmod(n, QT)
                        pe.wait_ge(sem("a_pT"), 8 * i + (n + 1))
                        pe.wait_ge(sem("a_out"), prev(i, 8, n))
                        for j in range(t + 1):
                            last = nc.tensor.matmul(bank[n % 2][:, 0:D_A], t2[:, n % 2, j * P:j * P + P],
                                                    va[:, j, ds(i * P + hh * D_A, D_A)], start=j == 0, stop=j == t)
                        last.then_inc(sem("a_weighed"), 1)

                    for n in range(8 + 2):
                        if n < 8:
                            scores(n)
                        if 0 <= n - 1 < 8:
                            turn_p(n - 1)
                        if n >= 2:
                            weigh(n - 2)

            def attn_b():
                pe.wait_ge(sem("a_out"), 32)
                with pe.Fori(0, 4) as i:
                    def scores(t):
                        pe.wait_ge(sem("b_pair"), 2 * i + 2)
                        for m in range(2):
                            pe.wait_ge(sem("b_biased"), 8 * i + max(2 * t - 2, 0))
                            nc.tensor.matmul(bank[2 + 2 * (t % 2) + m][:, 0:(t + 1) * P],
                                             t3[64 * m:64 * m + 64, 0, t * P:t * P + P],
                                             t3[64 * m:64 * m + 64, 1, 0:(t + 1) * P], start=True, stop=True
                                             ).then_inc(sem("b_scores"), 1)

                    def turn_p(t):
                        pe.wait_ge(sem("b_mixed"), 4 * i + (t + 1))
                        pe.wait_ge(sem("b_pT"), prev(i, 4, t))
                        for j in range(t + 1):
                            last = nc.tensor.transpose(bank[6 + t % 2][:, j * P:j * P + P],
                                                       dist_a[:, 2 * (t % 2), j * P:j * P + P], ident[:])
                        last.then_inc(sem("b_turned"), 1)

                    def weigh(t):
                        pe.wait_ge(sem("b_pT"), 4 * i + (t + 1))
                        pe.wait_ge(sem("b_out"), prev(i, 4, t))
                        for j in range(t + 1):
                            last = nc.tensor.matmul(bank[t % 2][:, 0:P], t2[:, t % 2, j * P:j * P + P],
                                                    vb[:, j, ds(i * P, P)], start=j == 0, stop=j == t)
                        last.then_inc(sem("b_weighed"), 1)

                    for n in range(QT + 2):
                        if n < QT:
                            scores(n)
                        if n >= 2:
                            weigh(n - 2)
                        if 0 <= n - 1 < QT:
                            turn_p(n - 1)

            def turn_y():
                for f in range(8):
                    if f == 4:
                        pe.wait_ge(sem("y_b_scaled"), 1)
                    if f >= 4:
                        pe.wait_ge(sem("y_made"), f - 3)
                    elif f == 0:
                        pe.wait_ge(sem("b_out"), 16)
                    for t in range(QT):
                        last = nc.tensor.transpose(bank[f % 4][:, t * P:t * P + P],
                                                   (y_a, y_b)[f // 4][:, t, (f % 4) * P:(f % 4) * P + P], ident[:])
                    last.then_inc(sem("y_mm"), 1)

            def merge_mm():
                pe.wait_ge(sem("y_made"), 8)
                y = [(y_hi[:, k, :], y_lo[:, k, :]) for k in range(8)]
                with pe.Fori(0, KD) as i:
                    u = U0["merge"] + 2 * i
                    pair_unit(u, 0, h)
                    unit_ready(u + 1)
                    for n in range(2):
                        last = mm3(bank[2 + n][:], [w_tile(1, k, 256, P * n) for k in range(4)], y[4 * n:4 * n + 4])
                    last.then_inc(mm_done, 1)

            def out1():
                pe.wait_ge(sem("ada_free"), 3 * KD)
                ada_columns(bank[5], ada2_all, range(KD))
                m = [(m_hi[:, k, :], m_lo[:, k, :]) for k in range(KD)]
                for k in range(4):
                    pair_unit(U0["out1"] + k, k % 2, m, (sem("merged"), 0))
                    if k:
                        norm_add(0, 2 * k - 2, 2 * k)

            def norm_add(q, f0, f1):
                if q and f0 == 0:
                    pe.wait_ge(sem("norm_std"), q)
                for f in range(f0, f1):
                    pe.wait_ge(sem("norm_squares"), KD * q + f + 1)
                    nc.tensor.matmul(bank[4][:], ones[:], nt[:, f % 2, :], start=f == 0, stop=f == KD - 1
                                     ).then_inc(sem("norm_added"), 1)

            def norm2():
                norm_add(0, KD - 2, KD)
                ada_columns(bank[6], ada2_all, range(KD, 3 * KD))
                ada_columns(bank[7], ada2_all, range(3 * KD, 4 * KD))

            def ff():
                g = [(g_hi[:, k, :], g_lo[:, k, :]) for k in range(12)]
                for part, n, done in (("a", 12, 0), ("b", 10, 12)):
                    with pe.Fori(0, n // 2) as i:
                        for slot in range(2):
                            pair_unit(U0["ff1" + part] + 2 * i + slot, slot, h, (sem("h_made"), KD))
                    def down(i, slot):
                        unit_ready(U0["ff2" + part] + 2 * i + slot)
                        tiles_by_k([(bank[2 * slot][:], 0)], slot, P, g[:n], (sem("hidden"), done))

                    with pe.Fori(0, KD // 2 - 1) as i:
                        for slot in range(2):
                            down(i, slot)
                    down(KD // 2 - 1, 0)
                    if part == "b":
                        norm_add(1, 0, KD - 2)
                    down(KD // 2 - 1, 1)

            def norm_mix():
                norm_add(1, KD - 2, KD)

            def retention():
                pe.wait_ge(sem("norm_std"), 2)
                yr = [(yr_hi[:, k, :], yr_lo[:, k, :]) for k in range(4)]
                with pe.Fori(0, R_H) as i:
                    u = U0["retention"] + 8 * i
                    pair_unit(u, 0, h, (sem("h_made"), 2 * KD))
                    pair_unit(u + 1, 1, h)
                    value_pair(u + 2)
                    pe.wait_ge(sem("r_rope"), 2 * i + 2)
                    pe.wait_ge(banks_free, u)
                    for j in range(QT):
                        for d in range(2):
                            last = nc.tensor.matmul(bank[4 + j][:, 0:S - j * P], rkT[:, d, j * P:j * P + P],
                                                    rqT[:, d, j * P:S], start=d == 0, stop=d == 1)
                        last.then_inc(sem("r_scores"), 1)
                    pe.wait_ge(banks_free, u + 4)
                    pair_unit(u + 4, 0, h)
                    pe.wait_ge(sem("r_decayed"), 4 * i + 4)
                    for vt in range(4):
                        for j in range(QT):
                            last = nc.tensor.matmul(bank[4 + vt][:, j * P:S], rv[:, j, vt * P:vt * P + P],
                                                    rs_t[:, j, 0:S - j * P], start=j == 0, stop=j == QT - 1)
                        last.then_inc(sem("r_o"), 1)
                    for vt in range(4):
                        pe.wait_ge(sem("r_squares"), 4 * i + (vt + 1))
                        nc.tensor.matmul(bank[2][:], ones[:], nt[:, vt % 2, :], start=vt == 0, stop=vt == 3
                                         ).then_inc(sem("r_added"), 1)
                    pe.wait_ge(sem("r_std"), i + 1)
                    pair_unit(u + 5, 1, h)
                    for half in range(2):
                        pe.wait_ge(lo_done, u + (7 + half))
                        for n0 in (0, 2):
                            pe.wait_ge(banks_free, u + 5 + (half or n0 > 0))
                            for k, (y_h, y_l) in enumerate(yr):
                                pe.wait_ge(sem("r_y"), 4 * i + (k + 1))
                                for n in (n0, n0 + 1):
                                    a_hi, a_lo = w_tile(half, k, 512, P * n)
                                    for m, (a, b) in enumerate(((a_hi, y_h), (a_hi, y_l), (a_lo, y_h))):
                                        last = nc.tensor.matmul(bank[4 * half + n][:], a, b, start=k == m == 0,
                                                                stop=k == 3 and m == 2)
                        last.then_inc(mm_done, 1)

            def latent():
                u = U0["latent"]
                pair_unit(u, 0, h)
                pair_unit(u + 1, 1, h)
                for n in range(2):
                    unit_ready(u + 2 + n)
                    mm3(bank[2 * n][:], [w_tile(n, k, P, 0) for k in range(KD)], h).then_inc(mm_done, 1)
                for n in range(5):
                    pe.wait_ge(sem("l_squares"), n + 1)
                    nc.tensor.matmul(bank[4 + n // 3][:], ones[:], nt[:, n % 2, :], start=n in (0, 3), stop=n in (2, 4)
                                     ).then_inc(sem("l_added"), 1)
                pe.wait_ge(sem("l_squares"), 6)
                for t in range(QT):
                    last = nc.tensor.matmul(bank[6][:, t:t + 1], nt[0:64, 1, t * P:t * P + P], ones[0:64, 0:1],
                                            start=True, stop=True)
                last.then_inc(sem("l_added"), 1)
                pe.wait_ge(sem("l_kr"), 1)
                pe.wait_ge(sem("masks_ready"), 1)
                nc.tensor.matmul(bank[7][:], turn[:], krT[:], start=True, stop=True).then_inc(sem("l_turned"), 1)

            def mla():
                pe.wait_ge(sem("l_made"), 5)
                pe.wait_ge(sem("l_krr"), 1)
                lq = [(lat_hi[:, k, :], lat_lo[:, k, :]) for k in range(3)]
                lkv = [(lat_hi[:, 3 + k, :], lat_lo[:, 3 + k, :]) for k in range(2)]

                def wide(w, slot, k, row, lo, n):
                    return w[:, slot, k * row:(k + 1) * row].rearrange("p (h c) -> p h c", h=2)[:, :, lo:lo + n]

                with pe.Fori(0, M_H // 2) as i:
                    u = U0["mla"] + 2 * i
                    pe.wait_ge(sem("c_mo"), 2 * i)
                    unit_ready(u)
                    for n in range(2):
                        mm3(bank[n][:], [w_tile(0, k, 384, P * n) for k in range(3)], lq)
                    mm3(bank[2][:], [w_tile(0, k, 384, 2 * P) for k in range(3)], lq
                        ).then_inc(mm_done, 1)
                    unit_ready(u + 1)
                    for n in range(2):
                        mm3(bank[3 + n][:], [w_tile(1, k, 512, 256 * n) for k in range(2)], lkv)
                    for t in range(QT):
                        at = 256 * (t % 2)
                        last = mm3(bank[5 + t // 2][:, at:at + 256].rearrange("p (h c) -> p h c", h=2),
                                   [(a[:, t * P:t * P + P], b[:, t * P:t * P + P]) for a, b in lkv],
                                   [(wide(w_hi, 1, k, 512, P, P), wide(w_lo, 1, k, 512, P, P)) for k in range(2)])
                    last.then_inc(mm_done, 1)
                    pe.wait_ge(sem("c_squares"), 5 * i + 5)
                    for t in range(QT):
                        tok = slice(t * P, t * P + P)
                        for j in range(4):
                            dst = bank[7][:, 4 * t + j:4 * t + j + 1]
                            last = nc.tensor.matmul(dst, nt[:, j + j // 2, tok], ones[:, 0:1], start=True, stop=j >= 2)
                            if j < 2:
                                last = nc.tensor.matmul(dst, nt[:, 2, tok], half[:, j:j + 1],
                                                        start=False, stop=True)
                    last.then_inc(sem("c_sums"), 1)
                    pe.wait_ge(banks_free, u + 1)
                    pe.wait_ge(sem("c_v"), 2 * i + 2)
                    nc.tensor.matmul(bank[5][:], turn[:], qrg, start=True, stop=True).then_inc(sem("c_turned_q"), 1)
                    pe.wait_ge(sem("c_wide"), 2 * i + 2)
                    for hh in range(2):
                        for t in range(QT):
                            last = nc.tensor.transpose(bank[6 + hh][:, t * P:t * P + P], kw[:, 4 * hh + t, :], ident[:])
                        last.then_inc(sem("c_kinv"), 1)
                    pe.wait_ge(sem("c_k"), 4 * i + 4)
                    pe.wait_ge(sem("c_q"), i + 1)
                    pe.wait_ge(banks_free, u + 2)

                    def scores(n):
                        hh, t = divmod(n, QT)
                        pe.wait_ge(sem("c_exp"), prev(i, 8, n))
                        w = (t + 1) * P
                        nc.tensor.matmul(bank[n % 2][:, 0:w], qn[:, hh, t * P:t * P + P], kn[:, hh, 0:w],
                                         start=True, stop=False)
                        nc.tensor.matmul(bank[n % 2][:, 0:w], qr[:, t * P:t * P + P], kr2[:, hh, 0:w],
                                         start=False, stop=True).then_inc(sem("c_scores"), 1)

                    def turn_p(n):
                        pe.wait_ge(sem("c_exp"), 8 * i + (n + 1))
                        pe.wait_ge(sem("c_pT"), prev(i, 8, n))
                        for j in range(n % QT + 1):
                            last = nc.tensor.transpose(bank[2 + n % 2][:, j * P:j * P + P], nt[:, n % 2, j * P:j * P + P], ident[:])
                        last.then_inc(sem("c_turned"), 1)

                    def weigh(n):
                        hh, t = divmod(n, QT)
                        pe.wait_ge(sem("c_pT"), 8 * i + (n + 1))
                        pe.wait_ge(sem("c_out"), prev(i, 8, n))
                        for j in range(t + 1):
                            last = nc.tensor.matmul(bank[4 + n % 2][:, 0:P], nt[:, 2 + n % 2, j * P:j * P + P],
                                                    vv[:, j, hh * P:hh * P + P], start=j == 0, stop=j == t)
                        last.then_inc(sem("c_weighed"), 1)

                    for n in range(8 + 2):
                        if n < 8:
                            scores(n)
                        if 0 <= n - 1 < 8:
                            turn_p(n - 1)
                        if n >= 2:
                            weigh(n - 2)
                    for hh in range(2):
                        pe.wait_ge(sem("c_out"), 8 * i + 4 * hh + 4)
                        for t in range(QT):
                            last = nc.tensor.transpose(bank[6 + hh][:, t * P:t * P + P], mo_t[:, t, hh * P:hh * P + P], ident[:])
                        last.then_inc(sem("c_mo_mm"), 1)

            def merge2_mm():
                mo = [(mo_hi[:, k, :], mo_lo[:, k, :]) for k in range(8)]
                pe.wait_ge(sem("c_mo"), 8)
                with pe.Fori(0, KD) as i:
                    u = U0["merge2"] + 2 * i
                    pair_unit(u, 0, h)
                    unit_ready(u + 1)
                    mm3(bank[2][:], [w_tile(1, k, P, 0) for k in range(KD)], mo).then_inc(mm_done, 1)

            def out2():
                m = [(m2_hi[:, k, :], m2_lo[:, k, :]) for k in range(KD)]
                for k in range(4):
                    pair_unit(U0["out2"] + k, k % 2, m, (sem("merged2"), 0))
                    if k:
                        norm_add(2, 2 * k - 2, 2 * k)

            def mlp():
                norm_add(2, KD - 2, KD)
                g = [(u_hi[:, k, :], u_lo[:, k, :]) for k in range(KD)]

                def quarter(i, last):
                    u = U0["mlp"] + 8 * i
                    for k in range(4):
                        pair_unit(u + k, k % 2, h, (sem("h_made"), 3 * KD))
                    for k in range(4):
                        pair_unit(u + 4 + k, k % 2, g, (sem("mlp_made"), 8 * i))
                        if last and k:
                            norm_add(3, 2 * k - 2, 2 * k)

                with pe.Fori(0, 3) as i:
                    quarter(i, False)
                quarter(3, True)

            def ple():
                norm_add(3, KD - 2, KD)
                pe.wait_ge(sem("p_in_done"), 16)
                for k in range(2):
                    for t in range(QT):
                        last = nc.tensor.transpose(bank[5 + k][:, t * P:t * P + P], p_in[:, t, k * P:k * P + P], ident[:])
                    last.then_inc(sem("p_mm"), 1)
                pp = [(p_hi[:, k, :], p_lo[:, k, :]) for k in range(2)]
                with pe.Fori(0, KD) as i:
                    u = U0["ple"] + 2 * i
                    for slot, xs, made in ((0, h, (sem("h_made"), 4 * KD)), (1, pp, (sem("p_made"), 0))):
                        unit_ready(u + slot)
                        tiles_by_k([(bank[2 * slot][:], 0)], slot, P, xs, made)
                pe.wait_ge(banks_free, len(WIDTH))
                for n in range(2 * QT):
                    t, half = divmod(n, 2)
                    if n >= 4:
                        pe.wait_ge(sem("out_tile_ready"), n - 3)
                    for f in range(4):
                        last = nc.tensor.transpose(bank[4 + n % 4][:, f * P:f * P + P], xT[:, 4 * half + f, t * P:t * P + P], ident[:])
                    last.then_inc(sem("out_mm"), 1)

            prologue()
            index()
            topk()
            values()
            qk()
            attn_a()
            attn_b()
            turn_y()
            merge_mm()
            out1()
            norm2()
            ff()
            norm_mix()
            retention()
            latent()
            mla()
            merge2_mm()
            out2()
            mlp()
            ple()

        @block.scalar
        def _(act):
            own = Count(act, sem("act_steps"))

            def split(u, slot=None, width=None):
                if isinstance(u, int):
                    if u >= len(WIDTH):
                        return
                    slot, width = u % 2, WIDTH[u]
                act.wait_ge(raw_in[slot], raw_ready(u, slot))
                if not isinstance(u, int) or u >= 2:
                    act.wait_ge(mm_done, u - 1)
                nc.scalar.activation(w_hi[:, slot, 0:width], raw[:, slot, 0:width], ACT.Copy).then_inc(hi_done, 1)

            def ring(name, per, body, count=0):
                u0, n = U0[name], len(dict(STAGES)[name]) // per
                widths = WIDTH[u0:u0 + per]
                if n > 1:
                    with act.Fori(0, n - 1) as i:
                        own.enter(i, count)
                        body(i, u0 + per * i, lambda u, k: split(u + k, k % 2, (widths + widths[:1])[k]))
                    own.leave(n - 1)
                body(n - 1, u0 + per * (n - 1), lambda u, k: split(u + k))

            def prologue():
                row = VROWS
                for name, ap, n in (("c", A["c"], 8), ("norm1_g", A["norm1_g"], 8), ("b_ada", A["b_ada"], 48),
                                    ("norm2_g", A["norm2_g"], 8), ("norm_mix", A["norm_mix_2"], 8),
                                    ("norm_mlp", A["norm_mlp_2"], 8), ("norm_ple", A["norm_ple_2"], 8),
                                    ("ret_norm", A["ret_norm_2"], 16), ("q_lat", A["q_lat_norm_2"], 3),
                                    ("kv_lat", A["kv_lat_norm_2"], 2), ("subln", A["subln_g"], 1)):
                    nc.scalar.dma_start(vrows[row[name]:row[name] + n, :],
                                 ap[0, :].rearrange("(r n) -> r n", n=P)).then_inc(sem("vectors_in"), 16)
                for name, ap in (("q_nope", A["q_norm_2"]), ("k_nope", A["k_norm_2"])):
                    nc.scalar.dma_start(vrows[row[name]:row[name] + 1, :], ap[0:1, 0:P]).then_inc(sem("vectors_in"), 16)
                for n, name in enumerate(("lam_q1", "lam_k1", "lam_q2", "lam_k2")):
                    nc.scalar.dma_start(lrow[0:1, D_A * n:D_A * n + D_A], A[name]).then_inc(sem("lambda_in"), 16)
                act.wait_ge(sem("eps_ready"), 1)
                act.wait_ge(sem("x_in_done"), 16)
                for t in range(QT):
                    nc.scalar.activation(x_n[:, t, :], x_in[:, t, :], ACT.Square, accum_out=small[:, t:t + 1]
                                         ).then_inc(sem("x_squares"), 1)
                act.wait_ge(sem("x_squares"), QT)
                nc.scalar.activation(small[:, 4:8], small[:, 0:4], ACT.Sqrt, scale=1.0 / D, bias=eps[:]
                                     ).then_inc(sem("x_std"), 1)
                act.wait_ge(sem("vT_mm"), 1)
                nc.scalar.activation(vT[:], bank[4][:, 0:NVR], ACT.Copy).then_inc(sem("vT_ready"), 1)
                act.wait_ge(sem("vT_ready"), 1)
                nc.scalar.activation(cs[:, 0:KD], vT[:, 0:KD], ACT.Exp, scale=-1.0).then_inc(sem("silu_exp"), 1)
                act.wait_ge(sem("lambda_dots"), 2)
                nc.scalar.activation(lsum[0:1, 2:4], lsum[0:1, 0:2], ACT.Exp).then_inc(sem("lambda_exp"), 1)
                for f in range(KD):
                    act.wait_ge(sem("x_mm"), f + 1)
                    nc.scalar.activation(xT[:, f, :], bank[f % 4][:], ACT.Copy).then_inc(sem("xT_ready"), 1)
                split(0)
                split(1)
                split_h(0, "h_t_ready", h_t)

            def split_h(first, ready, tmp):
                for f in range(KD):
                    act.wait_ge(sem(ready), first + f + 1)
                    nc.scalar.activation(h_hi[:, f, :], tmp[:, f % 2, :], ACT.Copy).then_inc(sem("h_hi_ready"), 1)

            def index():
                u = U0["index"]
                act.wait_ge(mm_done, u + 1)
                act.wait_ge(sem("h_made"), KD)
                nc.scalar.activation(qiT[:, 0, :], bank[0][:], ACT.Copy).then_inc(own.sem, 1)
                nc.scalar.activation(qiT[:, 1, :], bank[1][:], ACT.Copy).then_inc(banks_free, 1)
                own.total += 1
                split(u + 2)
                act.wait_ge(mm_done, u + 2)
                nc.scalar.activation(kiT[:], bank[2][:], ACT.Copy).then_inc(sem("index_ready"), 1)
                act.wait_ge(own.sem, own.total)
                act.wait_ge(sem("index_ready"), 1)
                nc.scalar.activation(wi[:].rearrange("p t n -> p (t n)"), bank[3][:, 0:4 * QT], ACT.Copy
                                     ).then_inc(banks_free, 1)
                act.wait_ge(banks_free, u + 2)
                own.step(nc.scalar.activation(small[:, 8:9], small[:, 4:5], ACT.Copy))
                nc.scalar.activation(small[:, 9:10], small[:, 8:9], ACT.Copy).then_inc(sem("index_ready"), 1)
                split(U0["values"] + 1)

            def values():
                u = U0["values"]
                for n, dst in enumerate((va, vb)):
                    if n:
                        split(u + 2 * n + 1)
                    split(u + 2 * n + 2)
                    act.wait_ge(mm_done, u + 2 * n + 2)
                    for t in range(QT):
                        ins = nc.scalar.activation(dst[:, t, :], bank[t][:], ACT.Copy)
                        if t < QT - 1:
                            own.inc(ins)
                    act.wait_ge(own.sem, own.total)
                    ins.then_inc(banks_free, 2)

            def qk():
                act.wait_ge(sem("logits_added"), QT * H_I)

                def body(i, u, nxt):
                    for slot in range(2):
                        nxt(u, slot + 1)
                        act.wait_ge(mm_done, u + slot + 1)
                        for n in range(2):
                            c = 2 * slot + n
                            nc.scalar.activation(t1[:, n, :], bank[c][:], ACT.Square).then_inc(sem("qk_squares"), 1)
                        act.wait_ge(banks_free, u + slot)
                        for n in range(2):
                            c = 2 * slot + n
                            act.wait_ge(sem("qk_sums"), 4 * i + (c + 1))
                            nc.scalar.activation(t2[:, n, :], bank[4 + n][:], ACT.Sqrt, scale=1.0 / D_A, bias=eps[:]
                                                 ).then_inc(sem("qk_std"), 1)
                ring("qk", 2, body)

            def topk():
                g = 0
                for t in range(QT):
                    w = (t + 1) * P
                    for hh in range(H_I):
                        act.wait_ge(sem("logits_mm"), g + 1)
                        if g >= 2:
                            act.wait_ge(sem("logits_added"), g - 1)
                        nc.scalar.activation(t1[:, g % 2, 0:w], bank[4 + g % 4][:, 0:w], ACT.Relu
                                             ).then_inc(sem("logits_read"), 1)
                        g += 1

            def attn_a():
                act.wait_ge(banks_free, U0["qk"] + 8)
                with act.Fori(0, 4) as i:
                    def exp(n):
                        act.wait_ge(sem("a_max"), 8 * i + (n + 1))
                        w = (n % QT + 1) * P
                        nc.scalar.activation(t1[:, n % 2, 0:w], t1[:, n % 2, 0:w], ACT.Exp, bias=stat[:, n:n + 1],
                                             accum_out=stat[:, 8 + n:9 + n]).then_inc(sem("a_exp"), 1)

                    def fetch(n):
                        act.wait_ge(sem("a_turned"), 8 * i + (n + 1))
                        act.wait_ge(sem("a_weighed"), 8 * i + max(n - 1, 0))
                        w = (n % QT + 1) * P
                        nc.scalar.activation(t2[:, n % 2, 0:w], bank[6 + n % 2][:, 0:w], ACT.Copy).then_inc(sem("a_pT"), 1)

                    for n in range(8 + 1):
                        if n < 8:
                            exp(n)
                        if n >= 1:
                            fetch(n - 1)

            def attn_b():
                act.wait_ge(sem("a_out"), 32)
                with act.Fori(0, 4) as i:
                    def exp(t):
                        w = (t + 1) * P
                        for m in range(2):
                            act.wait_ge(sem("b_max"), 8 * i + (2 * t + m + 1))
                            p = dist_a[:, 2 * (t % 2) + m, 0:w]
                            nc.scalar.activation(p, p, ACT.Exp, bias=stat[:, 2 * t + m:2 * t + m + 1],
                                                 accum_out=stat[:, 8 + 2 * t + m:9 + 2 * t + m]).then_inc(sem("b_exp"), 1)

                    def fetch(t):
                        act.wait_ge(sem("b_turned"), 4 * i + (t + 1))
                        act.wait_ge(sem("b_weighed"), 4 * i + max(t - 1, 0))
                        w = (t + 1) * P
                        nc.scalar.activation(t2[:, t % 2, 0:w], bank[6 + t % 2][:, 0:w], ACT.Copy).then_inc(sem("b_pT"), 1)

                    for n in range(QT + 1):
                        if n < QT:
                            exp(n)
                        if n >= 1:
                            fetch(n - 1)

            def turn_y():
                act.wait_ge(sem("b_out"), 16)
                for n in range(16):
                    nc.scalar.activation(t1[:, 0, 0:P], y_b[:, n // 4, (n % 4) * P:(n % 4) * P + P], ACT.Square,
                                         accum_out=stat[:, 32 + n:33 + n]).then_inc(sem("y_b_squares"), 1)
                    act.wait_ge(sem("y_b_squares"), n + 1)
                nc.scalar.activation(stat[:, 0:16], stat[:, 32:48], ACT.Sqrt, scale=1.0 / P, bias=eps[:]
                                     ).then_inc(sem("y_b_std"), 1)
                for f in range(8):
                    act.wait_ge(sem("y_mm"), f + 1)
                    if f < 4:
                        nc.scalar.activation(y_hi[:, f, :], bank[f % 4][:], ACT.Copy).then_inc(sem("y_hi_ready"), 1)
                    else:
                        nc.scalar.activation(y_hi[:, f, :], bank[f % 4][:], ACT.Copy, scale=vcol("subln")
                                             ).then_inc(sem("y_hi_ready"), 1)

            def merge_epi():
                def body(i, u, nxt):
                    nxt(u, 1)
                    act.wait_ge(mm_done, u + 1)
                    act.wait_ge(banks_free, u)
                    own.step(nc.scalar.activation(mt[:, 0, :], bank[0][:], ACT.Sigmoid))
                    nc.scalar.activation(mt[:, 1, :], bank[1][:], ACT.Sigmoid).then_inc(banks_free, 1)
                    nxt(u, 2)
                    act.wait_ge(sem("mixed"), i + 1)
                    nc.scalar.activation(m_hi[:, ds(i, 1), :], mt[:, 2, :], ACT.Copy).then_inc(sem("m_hi_ready"), 1)
                ring("merge", 2, body, 1)

            def out_units(name, q):
                def body(i, u, nxt):
                    for k in range(4):
                        nxt(u, k + 1)
                        if k:
                            act.wait_ge(banks_free, u + k)
                            norm_squares(q, 2 * k - 2, 2 * k)
                ring(name, 4, body)

            def out1():
                out_units("out1", 0)

            def norm_squares(q, f0, f1):
                for f in range(f0, f1):
                    if f >= 2 or q:
                        act.wait_ge(sem("norm_added"), KD * q + max(f - 1, 0))
                    nc.scalar.activation(nt[:, f % 2, :], xT[:, f, :], ACT.Square).then_inc(sem("norm_squares"), 1)

            def norm(q):
                norm_squares(q, KD - 2, KD)
                act.wait_ge(sem("norm_added"), KD * q + KD)
                nc.scalar.activation(nt[:, 2, :], bank[4][:], ACT.Sqrt, scale=1.0 / D, bias=eps[:]).then_inc(sem("norm_std"), 1)
                for f in range(KD):
                    act.wait_ge(sem("h_t_ready"), KD * (q + 1) + f + 1)
                    nc.scalar.activation(h_hi[:, f, :], nt[:, 4 + f % 2, :], ACT.Copy).then_inc(sem("h_hi_ready"), 1)

            def norm2():
                act.wait_ge(banks_free, U0["out1"] + 4)
                norm(0)

            def ff():
                at = 0
                for part, n in (("a", 12), ("b", 10)):
                    def epi(i, u, nxt, at=at):
                        for slot in range(2):
                            nxt(u, slot + 1)
                            act.wait_ge(mm_done, u + slot + 1)
                            act.wait_ge(sem("hidden"), 2 * i + (at + slot))
                            nc.scalar.activation(ft[:, 0, :], bank[2 * slot][:], ACT.Sigmoid).then_inc(sem("ff_sigmoid"), 1)
                            act.wait_ge(sem("ff_t_ready"), 2 * i + (at + slot + 1))
                            nc.scalar.activation(g_hi[:, ds(2 * i + slot, 1), :], ft[:, 1, :], ACT.Copy
                                                 ).then_inc(sem("ff_hi_ready"), 1)
                    ring("ff1" + part, 2, epi)
                    at += n
                    if part == "b":
                        sines(2)

                    def down(i, u, nxt):
                        nxt(u, 1)
                        if part == "b" and isinstance(i, int):
                            act.wait_ge(banks_free, u)
                            norm_squares(1, 0, KD - 2)
                        nxt(u, 2)
                    ring("ff2" + part, 2, down)
                    if part == "a":
                        sines(0)

            def sines(at):
                for n in (at, at + 1):
                    act.wait_ge(sem("angles"), n + 1)
                    nc.scalar.activation(trigs[:, n, :], nt[:, 4 + n % 2, :], ACT.Sin).then_inc(sem("trig_ready"), 1)

            def norm_mix():
                act.wait_ge(banks_free, U0["retention"])
                norm(1)

            def retention():
                act.wait_ge(sem("consts_in"), 16)
                act.wait_ge(sem("dtab_ready"), 1)

                def body(i, u, nxt):
                    act.wait_ge(sem("r_decayed"), 4 * i)
                    nc.scalar.activation(etab[:], dtab[:], ACT.Exp, scale=consts[:, ds(i + 2, 1)]).then_inc(sem("r_table"), 1)
                    for k in range(1, 5):
                        nxt(u, k)
                    act.wait_ge(mm_done, u + 4)
                    act.wait_ge(sem("r_o"), 4 * i)
                    act.wait_ge(banks_free, u + 2)
                    for t in range(QT):
                        ins = nc.scalar.activation(rv[:, t, :], bank[t][:], ACT.Copy)
                        if t < QT - 1:
                            own.step(ins)
                    ins.then_inc(banks_free, 2)
                    nxt(u, 5)
                    act.wait_ge(mm_done, u + 5)
                    act.wait_ge(sem("r_gated"), 4 * i)
                    for n in range(2):
                        nc.scalar.activation(sg[:, n, :], bank[n][:], ACT.Sigmoid).then_inc(sem("r_sigmoid"), 1)
                    nxt(u, 6)
                    for vt in range(4):
                        act.wait_ge(sem("r_o"), 4 * i + (vt + 1))
                        act.wait_ge(sem("r_added"), 4 * i + max(vt - 1, 0))
                        nc.scalar.activation(nt[:, vt % 2, :], bank[4 + vt][:], ACT.Square).then_inc(sem("r_squares"), 1)
                    act.wait_ge(sem("r_added"), 4 * i + 4)
                    nc.scalar.activation(nt[:, 2, :], bank[2][:], ACT.Sqrt, scale=1.0 / R_V, bias=eps[:]).then_inc(sem("r_std"), 1)
                    for vt in range(4):
                        if vt == 2:
                            act.wait_ge(mm_done, u + 6)
                            for n in range(2):
                                nc.scalar.activation(sg[:, 2 + n, :], bank[2 + n][:], ACT.Sigmoid).then_inc(sem("r_sigmoid"), 1)
                        act.wait_ge(sem("r_gated"), 4 * i + (vt + 1))
                        nc.scalar.activation(yr_hi[:, vt, :], nt[:, 4 + vt % 2, :], ACT.Copy).then_inc(sem("r_y_hi"), 1)
                    nxt(u, 7)
                    nxt(u, 8)
                ring("retention", 8, body, 3)

            def latent():
                u = U0["latent"]
                for k, tiles in enumerate(((0, 1), (2, 3), (4,))):
                    split(u + k + 1)
                    act.wait_ge(mm_done, u + k + 1)
                    act.wait_ge(banks_free, u + k)
                    for n, f in enumerate(tiles):
                        ins = nc.scalar.activation(lat_t[:, f, :], bank[2 * (k % 2) + n][:], ACT.Copy)
                        if f != tiles[-1]:
                            own.step(ins)
                    ins.then_inc(banks_free, 1)
                split(u + 4)
                act.wait_ge(mm_done, u + 4)
                nc.scalar.activation(krr[:], bank[2][:], ACT.Copy).then_inc(banks_free, 1)
                act.wait_ge(banks_free, u + 4)
                for n in range(5):
                    if n >= 2:
                        act.wait_ge(sem("l_added"), n - 1)
                    nc.scalar.activation(nt[:, n % 2, :], lat_t[:, n, :], ACT.Square).then_inc(sem("l_squares"), 1)
                act.wait_ge(sem("l_added"), 4)
                nc.scalar.activation(nt[:, 1, :], krr[:], ACT.Square).then_inc(sem("l_squares"), 1)
                act.wait_ge(sem("l_added"), 5)
                nc.scalar.activation(nt[:, 2, :], bank[4][:], ACT.Sqrt, scale=1.0 / 384, bias=eps[:]).then_inc(sem("l_std"), 1)
                act.wait_ge(sem("l_inverse"), 1)
                nc.scalar.activation(nt[:, 2, :], bank[5][:], ACT.Sqrt, scale=1.0 / 256, bias=eps[:]).then_inc(sem("l_std"), 1)
                for n in range(5):
                    act.wait_ge(sem("l_t"), n + 1)
                    nc.scalar.activation(lat_hi[:, n, :], nt[:, 4 + n % 2, :], ACT.Copy).then_inc(sem("l_hi"), 1)

            def mla():
                def body(i, u, nxt):
                    nxt(u, 1)
                    act.wait_ge(mm_done, u + 1)
                    act.wait_ge(banks_free, u)
                    act.wait_ge(sem("c_mo"), 2 * i)
                    for n in range(3):
                        nc.scalar.activation(nt[:, n, :], bank[n][:], ACT.Square).then_inc(sem("c_squares"), 1)
                    for n in range(2):
                        own.step(nc.scalar.activation(qn[:, n, :], bank[n][:], ACT.Copy, scale=vcol("q_nope")))
                    nc.scalar.activation(qrg[:], bank[2][:], ACT.Copy, scale=vcol("q_rope")).then_inc(banks_free, 1)
                    nxt(u, 2)
                    act.wait_ge(mm_done, u + 2)
                    for n in range(2):
                        nc.scalar.activation(nt[:, 3 + n, :], bank[3 + n][:], ACT.Square).then_inc(sem("c_squares"), 1)
                    for n in range(2):
                        nc.scalar.activation(vv[:, 2 * n:2 * n + 2, :].rearrange("p t c -> p (t c)"), bank[5 + n][:], ACT.Copy
                                             ).then_inc(sem("c_v"), 1)
                    act.wait_ge(sem("c_sums_out"), i + 1)
                    nc.scalar.activation(stat[:, 16:32], stat[:, 0:16], ACT.Sqrt, scale=1.0 / 192, bias=eps[:]
                                         ).then_inc(sem("c_std"), 1)
                    for hh in range(2):
                        act.wait_ge(sem("c_kinv"), 2 * i + (hh + 1))
                        nc.scalar.activation(nt[:, 3 + hh, :], bank[6 + hh][:], ACT.Copy).then_inc(sem("c_kinv_out"), 1)

                    def exp(n):
                        hh, t = divmod(n, QT)
                        act.wait_ge(sem("c_max"), 8 * i + (n + 1))
                        act.wait_ge(sem("c_turned"), 8 * i + max(n - 1, 0))
                        w = (t + 1) * P
                        nc.scalar.activation(nt[:, n % 2, 0:w], bank[n % 2][:, 0:w], ACT.Exp, bias=cst[:, 24 + n:25 + n],
                                             scale=cst[:, 4 * t + hh:4 * t + hh + 1], accum_out=cst[:, 32 + n:33 + n]
                                             ).then_inc(sem("c_exp"), 1)

                    def fetch(n):
                        act.wait_ge(sem("c_turned"), 8 * i + (n + 1))
                        act.wait_ge(sem("c_weighed"), 8 * i + max(n - 1, 0))
                        w = (n % QT + 1) * P
                        nc.scalar.activation(nt[:, 2 + n % 2, 0:w], bank[2 + n % 2][:, 0:w], ACT.Copy).then_inc(sem("c_pT"), 1)

                    act.wait_ge(sem("c_k"), 4 * i + 4)
                    for n in range(8 + 1):
                        if n < 8:
                            exp(n)
                        if n >= 1:
                            fetch(n - 1)
                    for hh in range(2):
                        act.wait_ge(sem("c_mo_mm"), 2 * i + (hh + 1))
                        nc.scalar.activation(mo_hi[:, ds(2 * i + hh, 1), :], bank[6 + hh][:], ACT.Copy).then_inc(sem("c_mo_hi"), 1)
                ring("mla", 2, body, 2)

            def merge2_epi():
                def body(i, u, nxt):
                    nxt(u, 1)
                    act.wait_ge(mm_done, u + 1)
                    act.wait_ge(banks_free, u)
                    act.wait_ge(sem("merged2"), i)
                    own.step(nc.scalar.activation(nt[:, 0, :], bank[0][:], ACT.Sigmoid))
                    nc.scalar.activation(nt[:, 1, :], bank[1][:], ACT.Sigmoid).then_inc(banks_free, 1)
                    nxt(u, 2)
                    act.wait_ge(sem("mixed2"), i + 1)
                    nc.scalar.activation(m2_hi[:, ds(i, 1), :], nt[:, 2, :], ACT.Copy).then_inc(sem("m2_hi_ready"), 1)
                ring("merge2", 2, body, 1)

            def out2():
                out_units("out2", 2)

            def mlp():
                act.wait_ge(banks_free, U0["mlp"])
                norm(2)

                def body(i, u, nxt):
                    for k in range(4):
                        nxt(u, k + 1)
                        act.wait_ge(mm_done, u + k + 1)
                        act.wait_ge(banks_free, u + k)
                        for n in range(2):
                            act.wait_ge(sem("mlp_squared"), 8 * i + max(2 * k + n - 1, 0))
                            ins = nc.scalar.activation(nt[:, n, :], bank[2 * (k % 2) + n][:], ACT.Relu)
                            ins.then_inc(sem("mlp_relu"), 1)
                        act.wait_ge(sem("mlp_relu"), 8 * i + (2 * k + 2))
                        own.step(nc.scalar.activation(small[:, 20:21], eps[:], ACT.Copy))
                        nc.scalar.activation(small[:, 21:22], eps[:], ACT.Copy).then_inc(banks_free, 1)
                        for n in range(2):
                            act.wait_ge(sem("mlp_squared"), 8 * i + (2 * k + n + 1))
                            nc.scalar.activation(u_hi[:, 2 * k + n, :], nt[:, 4 + n, :], ACT.Copy).then_inc(sem("mlp_hi"), 1)
                    for k in range(4, 8):
                        nxt(u, k + 1)
                        if k > 4 and isinstance(i, int):
                            act.wait_ge(banks_free, u + k)
                            norm_squares(3, 2 * k - 10, 2 * k - 8)
                ring("mlp", 8, body, 4)

            def ple():
                act.wait_ge(banks_free, U0["ple"])
                norm(3)
                for k in range(2):
                    act.wait_ge(sem("p_mm"), k + 1)
                    nc.scalar.activation(p_hi[:, k, :], bank[5 + k][:], ACT.Copy).then_inc(sem("p_hi_ready"), 1)

                def body(i, u, nxt):
                    nxt(u, 1)
                    act.wait_ge(mm_done, u + 1)
                    act.wait_ge(banks_free, u)
                    nc.scalar.activation(nt[:, 0, :], bank[0][:], ACT.Sigmoid).then_inc(banks_free, 1)
                    nxt(u, 2)
                ring("ple", 2, body)
                for n in range(0, 2 * QT, 2):
                    act.wait_ge(sem("out_mm"), n + 1)
                    if n:
                        act.wait_ge(sem("out_tile_ready"), n)
                    nc.scalar.activation(out_sb[:, n // 2, 0:512], bank[4 + n % 4][:], ACT.Copy).then_inc(sem("out_tile_ready"), 1)

            prologue()
            index()
            topk()
            values()
            qk()
            attn_a()
            attn_b()
            turn_y()
            merge_epi()
            out1()
            norm2()
            ff()
            norm_mix()
            retention()
            latent()
            mla()
            merge2_epi()
            out2()
            mlp()
            ple()

        @block.vector
        def _(dve):
            own = Count(dve, sem("dve_steps"))
            v = nc.vector

            def split(u, slot=None, width=None):
                if isinstance(u, int):
                    if u >= len(WIDTH):
                        return
                    slot, width = u % 2, WIDTH[u]
                dve.wait_ge(hi_done, u + 1)
                v.tensor_tensor(w_lo[:, slot, 0:width], raw[:, slot, 0:width],
                                w_hi[:, slot, 0:width].bitcast(F32), ALU.subtract).then_inc(lo_done, 1)

            def ring(name, per, body, count=0):
                u0, n = U0[name], len(dict(STAGES)[name]) // per
                widths = WIDTH[u0:u0 + per]
                if n > 1:
                    with dve.Fori(0, n - 1) as i:
                        own.enter(i, count)
                        body(i, u0 + per * i, lambda u, k: split(u + k, k % 2, (widths + widths[:1])[k]))
                    own.leave(n - 1)
                body(n - 1, u0 + per * (n - 1), lambda u, k: split(u + k))

            def prologue():
                v.memset(eps[:], EPS).then_inc(sem("eps_ready"), 1)
                dve.wait_ge(sem("x_std"), 1)
                own.step(v.reciprocal(small[:, 0:4], small[:, 4:8]))
                for t in range(QT):
                    v.tensor_scalar(x_n[:, t, :], x_in[:, t, :], small[:, t:t + 1], None, ALU.mult
                                    ).then_inc(sem("x_n_ready"), 1)
                dve.wait_ge(sem("lambda_in"), 64)
                for n in range(2):
                    own.step(v.tensor_tensor(vrows_l(n), lrow[0:1, 128 * n:128 * n + 64],
                                             lrow[0:1, 128 * n + 64:128 * n + 128], ALU.mult))
                    v.reduce_sum(lsum[0:1, n:n + 1], vrows_l(n), axis=AX).then_inc(sem("lambda_dots"), 1)
                dve.wait_ge(sem("silu_exp"), 1)
                own.step(v.tensor_scalar(cs[:, KD:2 * KD], cs[:, 0:KD], 1.0, None, ALU.add))
                own.step(v.reciprocal(cs[:, 0:KD], cs[:, KD:2 * KD]))
                own.step(v.tensor_tensor(cs[:, 2 * KD:3 * KD], cs[:, 0:KD], vT[:, 0:KD], ALU.mult))
                dve.wait_ge(sem("lambda_exp"), 1)
                own.step(v.tensor_tensor(lsum[0:1, 5:6], lsum[0:1, 2:3], lsum[0:1, 3:4], ALU.subtract))
                v.tensor_scalar(lsum[0:1, 4:5], lsum[0:1, 5:6], LAMBDA_INIT, None, ALU.add
                                ).then_inc(sem("lambda_sum"), 1)
                for k, w in enumerate(ada_in1):
                    dve.wait_ge(sem(f"ada_in{k}"), 16)
                    scale = cs[:, 2 * KD + k:2 * KD + k + 1]
                    if k == 0:
                        ins = v.tensor_scalar(ada[:], w, scale, None, ALU.mult)
                    else:
                        dve.wait_ge(sem("ada_free"), k)
                        ins = v.scalar_tensor_tensor(ada[:], w, scale, ada[:], ALU.mult, ALU.add)
                    ins.then_inc(sem("ada_free"), 1)
                split(0)
                split(1)
                dve.wait_ge(sem("lambda_mm"), 1)
                own.step(v.tensor_copy(lam[:], bank[5][:, 0:1]))
                make_h1()
                v.tensor_scalar(vT[:, VROWS["qn_a"]:VROWS["qn_a"] + 1], vcol("qn_a"), D_A ** -0.5, None, ALU.mult
                                ).then_inc(own.sem, 1)
                own.total += 1
                v.tensor_scalar(vT[:, VROWS["qn_b"]:VROWS["qn_b"] + 1], vcol("qn_b"), D_A ** -0.5, None, ALU.mult
                                ).then_inc(own.sem, 1)
                own.total += 1
                own.step(v.tensor_scalar(vT[:, VROWS["subln"]:VROWS["subln"] + 1], vcol("subln"), 1.0 - LAMBDA_INIT,
                                         None, ALU.mult))

            def vrows_l(n):
                return h_t[0:1, n, 0:64]

            def make_h1():
                dve.wait_ge(sem("ada_mm"), 1)
                own.step(v.tensor_tensor(modc[:, 0:16], bank[6][:, 0:16], vT[:, VROWS["b_ada"]:VROWS["b_ada"] + 16], ALU.add))
                own.step(v.tensor_scalar(gs1[:], SC1, 1.0, None, ALU.add))
                own.step(v.tensor_tensor(gs1[:], gs1[:], vT[:, VROWS["norm1_g"]:VROWS["norm1_g"] + KD], ALU.mult))
                for f in range(KD):
                    dve.wait_ge(sem("x_mm"), KD + f + 1)
                    if f >= 2:
                        dve.wait_ge(sem("h_made"), f - 1)
                    v.tensor_scalar(h_t[:, f % 2, :], bank[f % 4][:], gs1[:, f:f + 1], modc[:, f:f + 1],
                                    ALU.mult, ALU.add).then_inc(sem("h_t_ready"), 1)
                    if f:
                        h_rest(0, f - 1, h_t)
                h_rest(0, KD - 1, h_t)

            def h_rest(first, f, tmp):
                dve.wait_ge(sem("h_hi_ready"), first + f + 1)
                v.tensor_tensor(h_lo[:, f, :], tmp[:, f % 2, :], h_hi[:, f, :].bitcast(F32), ALU.subtract
                                ).then_inc(sem("h_made"), 1)

            def index():
                split(U0["index"] + 2)
                split(U0["values"] + 1)

            def values():
                u = U0["values"]
                index_scores()
                rounds(1, 16)
                split(u + 2)
                rounds(2, 8)
                split(u + 3)
                rounds(2, 8)
                split(u + 4)

            def qk():
                dve.wait_ge(sem("dist_ready"), QT)

                def body(i, u, nxt):
                    for slot in range(2):
                        nxt(u, slot + 1)
                        rounds(3, TOPK // 8 // 8)
                        for n, (dst, g) in enumerate((((qaT, "qn_a"), (kaT, "kn_a")), ((qbT, "qn_b"), (kbT, "kn_b")))[slot]):
                            c = 2 * slot + n
                            dve.wait_ge(sem("qk_std"), 4 * i + (c + 1))
                            own.step(v.reciprocal(t3[:, n, :], t2[:, n, :]))
                            ins = v.scalar_tensor_tensor(dst[:, ds(i, 1), :], bank[c][:], vcol(g), t3[:, n, :],
                                                         ALU.mult, ALU.mult)
                            if n == 0:
                                own.step(ins)
                        ins.then_inc(banks_free, 1)
                ring("qk", 2, body, 14)

            def index_scores():
                dve.wait_ge(sem("index_ready"), 2)
                g = 0
                for t in range(QT):
                    w = (t + 1) * P
                    for hh in range(H_I):
                        dve.wait_ge(sem("logits_read"), g + 1)
                        if hh == 0:
                            ins = v.tensor_scalar(dist_a[:, t, 0:w], t1[:, g % 2, 0:w], wi[:, t, 0:1], None, ALU.mult)
                        else:
                            ins = v.scalar_tensor_tensor(dist_a[:, t, 0:w], t1[:, g % 2, 0:w], wi[:, t, hh:hh + 1],
                                                         dist_a[:, t, 0:w], ALU.mult, ALU.add)
                        ins.then_inc(sem("logits_added"), 1)
                        g += 1
                        dve.wait_ge(sem("logits_added"), g)
                    own.step(v.memset(dist_a[0:64, t, w - 64:w], INADMISSIBLE))

            def rounds(t, n):
                w = (t + 1) * P
                for _ in range(n):
                    if own.loop:
                        dve.sem_inc(sem("rounds_seen"), 1)
                    own.step(v.max(top8[:], dist_a[:, t, 0:w]))
                    if own.loop:
                        dve.sem_inc(sem("rounds_seen"), 1)
                    own.step(v.match_replace(out=dist_a[:, t, 0:w], in_to_replace=top8[:], in_values=dist_a[:, t, 0:w],
                                             imm_value=TAKEN))

            def topk():
                own.step(v.tensor_copy(dist_a[:, 0, 0:P], dist_b[:, 0, 0:P]))
                for t in range(1, QT):
                    w = (t + 1) * P
                    own.step(v.tensor_scalar(dist_a[:, t, 0:w], dist_a[:, t, 0:w], TAKEN, FAR, ALU.is_gt, ALU.mult))
                    own.step(v.tensor_tensor(dist_a[:, t, 0:w], dist_a[:, t, 0:w], dist_b[:, t, 0:w], ALU.add))

            def attn_a():
                dve.wait_ge(sem("slopes_ready"), H_A + H_B)
                with dve.Fori(0, 4) as i:
                    own.enter(i, 8)

                    def bias(n):
                        hh, t = divmod(n, QT)
                        w = (t + 1) * P
                        dve.wait_ge(sem("a_scores"), 8 * i + (n + 1))
                        dve.wait_ge(sem("a_turned"), 8 * i + max(n - 1, 0))
                        v.scalar_tensor_tensor(t1[:, n % 2, 0:w], dist_a[:, t, 0:w], slope[:, ds(2 * i + hh, 1)],
                                               bank[4 + n % 2][:, 0:w], ALU.mult, ALU.add).then_inc(sem("a_biased"), 1)
                        dve.wait_ge(sem("a_biased"), 8 * i + (n + 1))
                        v.tensor_reduce(stat[:, n:n + 1], t1[:, n % 2, 0:w], axis=AX, op=ALU.max, negate=True
                                        ).then_inc(sem("a_max"), 1)

                    def out_(n):
                        hh, t = divmod(n, QT)
                        dve.wait_ge(sem("a_exp"), 8 * i + (n + 1))
                        own.step(v.reciprocal(stat[:, 16 + n:17 + n], stat[:, 8 + n:9 + n]))
                        dve.wait_ge(sem("a_weighed"), 8 * i + (n + 1))
                        v.tensor_scalar(y_a[:, t, ds(i * P + hh * D_A, D_A)], bank[n % 2][:, 0:D_A],
                                        stat[:, 16 + n:17 + n], None, ALU.mult).then_inc(sem("a_out"), 1)

                    for n in range(8 + 2):
                        if n < 8:
                            bias(n)
                        if n >= 2:
                            out_(n - 2)
                own.leave(4)

            def attn_b():
                with dve.Fori(0, 4) as i:
                    own.enter(i, 12)

                    def bias(t):
                        w = (t + 1) * P
                        for m in range(2):
                            n = 2 * t + m
                            dve.wait_ge(sem("b_scores"), 8 * i + (n + 1))
                            dve.wait_ge(sem("b_turned"), 4 * i + max(t - 1, 0))
                            p = dist_a[:, 2 * (t % 2) + m, 0:w]
                            v.scalar_tensor_tensor(p, dist_b[:, t, 0:w], slope[:, ds(i + H_A, 1)],
                                                   bank[2 + 2 * (t % 2) + m][:, 0:w], ALU.mult, ALU.add
                                                   ).then_inc(sem("b_biased"), 1)
                            dve.wait_ge(sem("b_biased"), 8 * i + (n + 1))
                            v.tensor_reduce(stat[:, n:n + 1], p, axis=AX, op=ALU.max, negate=True
                                            ).then_inc(sem("b_max"), 1)

                    def mix(t):
                        w = (t + 1) * P
                        c = 16 + 2 * t
                        dve.wait_ge(sem("b_exp"), 8 * i + (2 * t + 2))
                        own.step(v.reciprocal(stat[:, c:c + 2], stat[:, c - 8:c - 6]))
                        own.step(v.tensor_tensor(stat[:, 24 + t:25 + t], stat[:, c + 1:c + 2], lam[:], ALU.mult))
                        p0, p1 = (dist_a[:, 2 * (t % 2) + m, 0:w] for m in range(2))
                        own.step(v.tensor_scalar(p1, p1, stat[:, 24 + t:25 + t], None, ALU.mult))
                        v.scalar_tensor_tensor(p0, p0, stat[:, c:c + 1], p1, ALU.mult, ALU.subtract
                                               ).then_inc(sem("b_mixed"), 1)

                    def out_(t):
                        dve.wait_ge(sem("b_weighed"), 4 * i + (t + 1))
                        v.tensor_copy(y_b[:, t, ds(i * P, P)], bank[t % 2][:, 0:P]).then_inc(sem("b_out"), 1)

                    for n in range(QT + 2):
                        if n < QT:
                            bias(n)
                        if 0 <= n - 1 < QT:
                            mix(n - 1)
                        if n >= 2:
                            out_(n - 2)
                own.leave(4)

            def turn_y():
                dve.wait_ge(sem("y_b_std"), 1)
                own.step(v.reciprocal(stat[:, 16:32], stat[:, 0:16]))
                for n in range(16):
                    blk = y_b[:, n // 4, (n % 4) * P:(n % 4) * P + P]
                    ins = v.tensor_scalar(blk, blk, stat[:, 16 + n:17 + n], None, ALU.mult)
                    if n < 15:
                        own.step(ins)
                ins.then_inc(sem("y_b_scaled"), 1)
                for f in range(8):
                    dve.wait_ge(sem("y_hi_ready"), f + 1)
                    if f < 4:
                        ins = v.tensor_tensor(y_lo[:, f, :], bank[f % 4][:], y_hi[:, f, :].bitcast(F32), ALU.subtract)
                    else:
                        ins = v.scalar_tensor_tensor(y_lo[:, f, :], bank[f % 4][:], vcol("subln"), y_hi[:, f, :].bitcast(F32),
                                                     ALU.mult, ALU.subtract)
                    ins.then_inc(sem("y_made"), 1)

            def merge_epi():
                dve.wait_ge(sem("ada_clear"), 1)

                def body(i, u, nxt):
                    for n in range(2):
                        nxt(u, n + 1)
                        dve.wait_ge(sem(f"ada_in{n}"), 16 * i + 32)
                        dve.wait_ge(sem("ada_free"), 2 * i + (KD - 1 + n))
                        v.scalar_tensor_tensor(ada2[:, n, :], ada_in2[n], cs[:, ds(i + 2 * KD, 1)], ada2[:, n, :],
                                               ALU.mult, ALU.add).then_inc(sem("ada_free"), 1)
                    dve.wait_ge(mm_done, u + 2)
                    dve.wait_ge(banks_free, u + 1)
                    own.step(v.tensor_tensor(mt[:, 0, :], bank[2][:], mt[:, 0, :], ALU.mult))
                    v.tensor_tensor(mt[:, 1, :], bank[3][:], mt[:, 1, :], ALU.mult).then_inc(sem("gated"), 1)
                    dve.wait_ge(sem("gated"), i + 1)
                    v.tensor_tensor(mt[:, 2, :], mt[:, 0, :], mt[:, 1, :], ALU.add).then_inc(sem("mixed"), 1)
                    v.memset(small[:, 18:19], 0.0).then_inc(banks_free, 1)
                    dve.wait_ge(sem("m_hi_ready"), i + 1)
                    v.tensor_tensor(m_lo[:, ds(i, 1), :], mt[:, ds(2, 1), :], m_hi[:, ds(i, 1), :].bitcast(F32), ALU.subtract
                                    ).then_inc(sem("merged"), 1)
                ring("merge", 2, body, 1)

            def add_gated(i, u, nxt, gate, per_unit):
                for slot in range(2):
                    nxt(u, slot + 1)
                    dve.wait_ge(mm_done, u + slot + 1)
                    for n in range(per_unit):
                        f = ds(2 * per_unit * i + (per_unit * slot + n), 1)
                        ins = v.scalar_tensor_tensor(xT[:, f, :], bank[2 * slot + n][:], gate[:, f], xT[:, f, :],
                                                     ALU.mult, ALU.add)
                        if n < per_unit - 1:
                            own.step(ins)
                    ins.then_inc(banks_free, 1)

            def modulation(b, tiles, count):
                dve.wait_ge(sem("ada_mm"), count)
                lo, hi = tiles[0], tiles[-1] + 1
                at = VROWS["b_ada"]
                own.step(v.tensor_tensor(modc[:, lo:hi], bank[b][:, lo - 2 * KD:hi - 2 * KD], vT[:, at + lo:at + hi], ALU.add))

            def out1():
                modulation(5, range(2 * KD, 3 * KD), 2)
                ring("out1", 2, lambda i, u, nxt: add_gated(i, u, nxt, GT1, 2), 2)

            def norm(q, gains, shift=None):
                dve.wait_ge(sem("norm_std"), q + 1)
                own.step(v.reciprocal(nt[:, 3, :], nt[:, 2, :]))
                norm_tiles(q, gains, shift)

            def norm_tiles(q, gains, shift=None):
                for f in range(KD):
                    if f >= 2:
                        dve.wait_ge(sem("h_made"), KD * (q + 1) + f - 1)
                    ins = v.scalar_tensor_tensor(nt[:, 4 + f % 2, :], xT[:, f, :], gains[:, f:f + 1], nt[:, 3, :],
                                                 ALU.mult, ALU.mult)
                    if shift is not None:
                        own.step(ins)
                        ins = v.tensor_scalar(nt[:, 4 + f % 2, :], nt[:, 4 + f % 2, :], shift[:, f:f + 1], None, ALU.add)
                    ins.then_inc(sem("h_t_ready"), 1)
                    if f:
                        rest(q, f - 1)
                rest(q, KD - 1)

            def rest(q, f):
                dve.wait_ge(sem("h_hi_ready"), KD * (q + 1) + f + 1)
                v.tensor_tensor(h_lo[:, f, :], nt[:, 4 + f % 2, :], h_hi[:, f, :].bitcast(F32), ALU.subtract
                                ).then_inc(sem("h_made"), 1)

            def norm2():
                dve.wait_ge(sem("norm_std"), 1)
                own.step(v.reciprocal(nt[:, 3, :], nt[:, 2, :]))
                modulation(6, range(3 * KD, 5 * KD), 3)
                own.step(v.tensor_scalar(gs2[:], SC2, 1.0, None, ALU.add))
                own.step(v.tensor_tensor(gs2[:], gs2[:], vT[:, VROWS["norm2_g"]:VROWS["norm2_g"] + KD], ALU.mult))
                norm_tiles(0, gs2, SH2)
                modulation(7, range(5 * KD, 6 * KD), 4)

            def ff():
                at = 0
                for part, n in (("a", 12), ("b", 10)):
                    def epi(i, u, nxt, at=at):
                        for slot in range(2):
                            nxt(u, slot + 1)
                            dve.wait_ge(sem("ff_sigmoid"), 2 * i + (at + slot + 1))
                            own.step(v.tensor_tensor(ft[:, 2, :], bank[2 * slot][:], ft[:, 0, :], ALU.mult))
                            v.tensor_tensor(ft[:, 1, :], bank[2 * slot + 1][:], ft[:, 2, :], ALU.mult
                                            ).then_inc(sem("ff_t_ready"), 1)
                            dve.wait_ge(sem("ff_t_ready"), 2 * i + (at + slot + 1))
                            v.memset(small[:, 19:20], 0.0).then_inc(banks_free, 1)
                            dve.wait_ge(sem("ff_hi_ready"), 2 * i + (at + slot + 1))
                            v.tensor_tensor(g_lo[:, ds(2 * i + slot, 1), :], ft[:, ds(1, 1), :],
                                            g_hi[:, ds(2 * i + slot, 1), :].bitcast(F32), ALU.subtract).then_inc(sem("hidden"), 1)
                    ring("ff1" + part, 2, epi, 2)
                    at += n
                    if part == "a":
                        angles(0)
                    ring("ff2" + part, 2, lambda i, u, nxt: add_gated(i, u, nxt, GT2, 1))
                    if part == "a":
                        angles(1)

            def angles(s):
                two_pi = 2.0 * math.pi
                c1 = 6.28125
                c2 = float(np.float32(two_pi - c1).view(np.uint32).__and__(np.uint32(0xFFFFF000)).view(np.float32))
                c3 = two_pi - c1 - c2
                magic = 1.5 * 2.0 ** 23
                edge = float(np.nextafter(np.float32(math.pi), np.float32(0)))
                dve.wait_ge(sem("positions_in"), 16)
                dve.wait_ge(sem("consts_in"), 16)
                a, k, x, y = (nt[:, n, :] for n in range(4))
                own.step(v.tensor_copy(a, pos_i[:]))
                own.step(v.tensor_scalar(a, a, consts[:, s:s + 1], None, ALU.mult))
                own.step(v.tensor_scalar(k, a, 1.0 / two_pi, magic, ALU.mult, ALU.add))
                own.step(v.tensor_scalar(k, k, magic, None, ALU.subtract))
                own.step(v.scalar_tensor_tensor(x, k, -c1, a, ALU.mult, ALU.add))
                own.step(v.scalar_tensor_tensor(x, k, -c2, x, ALU.mult, ALU.add))
                own.step(v.scalar_tensor_tensor(x, k, -c3, x, ALU.mult, ALU.add))
                own.step(v.tensor_scalar(y, x, math.pi / 2, None, ALU.add))
                own.step(v.tensor_scalar(k, y, math.pi, -two_pi, ALU.is_gt, ALU.mult))
                own.step(v.tensor_tensor(y, y, k, ALU.add))
                if s:
                    dve.wait_ge(sem("trig_ready"), 2)
                v.tensor_scalar(nt[:, 4, :], y, edge, -edge, ALU.min, ALU.max).then_inc(sem("angles"), 1)
                v.tensor_scalar(nt[:, 5, :], x, edge, -edge, ALU.min, ALU.max).then_inc(sem("angles"), 1)

            def norm_mix():
                norm(1, vT[:, VROWS["norm_mix"]:VROWS["norm_mix"] + KD])

            def rope_tile(dst, x1, x2, cos, sin):
                own.step(v.tensor_tensor(rt[:, 0, :], x1, cos, ALU.mult))
                own.step(v.tensor_tensor(rt[:, 1, :], x2, sin, ALU.mult))
                own.step(v.tensor_tensor(rt[:, 2, :], x2, cos, ALU.mult))
                own.step(v.tensor_tensor(rt[:, 3, :], x1, sin, ALU.mult))
                v.tensor_tensor(dst[:, 0, :], rt[:, 0, :], rt[:, 1, :], ALU.subtract).then_inc(banks_free, 1)
                v.tensor_tensor(dst[:, 1, :], rt[:, 2, :], rt[:, 3, :], ALU.add).then_inc(sem("r_rope"), 1)

            def retention():
                cos, sin = trigs[:, 0, :], trigs[:, 1, :]
                dve.wait_ge(sem("aret_clear"), 1)

                def body(i, u, nxt):
                    for k, dst in enumerate((rqT, rkT)):
                        nxt(u, k + 1)
                        dve.wait_ge(mm_done, u + k + 1)
                        dve.wait_ge(sem("r_scores"), 4 * i)
                        rope_tile(dst, bank[2 * k][:], bank[2 * k + 1][:], cos, sin)
                        dve.wait_ge(sem("r_rope"), 2 * i + (k + 1))
                        dve.wait_ge(banks_free, u + k + 1)
                    nxt(u, 3)
                    nxt(u, 4)
                    dve.wait_ge(sem("r_table"), i + 1)
                    for j in range(QT):
                        dve.wait_ge(sem("r_scores"), 4 * i + (j + 1))
                        w = S - j * P
                        v.scalar_tensor_tensor(rs_t[:, j, 0:w], bank[4 + j][:, 0:w], R_QK ** -0.5, etab[:, 0:w],
                                               ALU.mult, ALU.mult).then_inc(sem("r_decayed"), 1)
                    nxt(u, 5)
                    dve.wait_ge(banks_free, u + 4)
                    for n in range(2):
                        dve.wait_ge(sem("r_sigmoid"), 4 * i + (n + 1))
                        ins = v.tensor_tensor(sg[:, n, :], bank[n][:], sg[:, n, :], ALU.mult)
                        if n == 0:
                            own.step(ins)
                    ins.then_inc(banks_free, 1)
                    nxt(u, 6)
                    dve.wait_ge(sem("r_std"), i + 1)
                    own.step(v.reciprocal(nt[:, 3, :], nt[:, 2, :]))
                    for vt in range(4):
                        if vt == 2:
                            y_lo_tile(i, 1)
                            for n in range(2, 4):
                                dve.wait_ge(sem("r_sigmoid"), 4 * i + (n + 1))
                                ins = v.tensor_tensor(sg[:, n, :], bank[n][:], sg[:, n, :], ALU.mult)
                                if n == 2:
                                    own.step(ins)
                            ins.then_inc(banks_free, 1)
                            dve.wait_ge(banks_free, u + 6)
                        own.step(v.scalar_tensor_tensor(rt[:, vt, :], bank[4 + vt][:],
                                                        vT[:, ds(4 * i + (VROWS["ret_norm"] + vt), 1)], nt[:, 3, :],
                                                        ALU.mult, ALU.mult))
                        v.tensor_tensor(nt[:, 4 + vt % 2, :], rt[:, vt, :], sg[:, vt, :], ALU.mult).then_inc(sem("r_gated"), 1)
                        if vt in (1, 3):
                            y_lo_tile(i, vt - 1)
                    y_lo_tile(i, 3)
                    nxt(u, 7)
                    for half in range(2):
                        dve.wait_ge(mm_done, u + (7 + half))
                        for n in range(4):
                            f = 4 * half + n
                            ins = v.tensor_tensor(aret[:, f, :], bank[f][:], aret[:, f, :], ALU.add)
                            if n < 3:
                                own.step(ins)
                        ins.then_inc(banks_free, 1)
                        if half == 0:
                            nxt(u, 8)
                    if not isinstance(i, int):
                        dve.wait_ge(banks_free, u + 8)

                def y_lo_tile(i, vt):
                    dve.wait_ge(sem("r_y_hi"), 4 * i + (vt + 1))
                    v.tensor_tensor(yr_lo[:, vt, :], nt[:, 4 + vt % 2, :], yr_hi[:, vt, :].bitcast(F32), ALU.subtract
                                    ).then_inc(sem("r_y"), 1)
                    dve.wait_ge(sem("r_y"), 4 * i + (vt + 1))
                ring("retention", 8, body, 21)

            def latent():
                u = U0["latent"]
                for k in range(4):
                    split(u + k + 1)
                dve.wait_ge(banks_free, u + 4)
                v.tensor_scalar(krT[:], krr[:], vcol("k_rope"), None, ALU.mult).then_inc(sem("l_kr"), 1)
                for n in range(2):
                    dve.wait_ge(sem("l_std"), n + 1)
                    v.reciprocal(nt[:, 3, :], nt[:, 2, :]).then_inc(sem("l_inverse"), 1)
                    dve.wait_ge(sem("l_inverse"), n + 1)
                    for f in ((0, 1, 2), (3, 4))[n]:
                        name, at = (("q_lat", f), ("kv_lat", f - 3))[n]
                        if f >= 2:
                            dve.wait_ge(sem("l_made"), f - 1)
                        v.scalar_tensor_tensor(nt[:, 4 + f % 2, :], lat_t[:, f, :], vcol(name, at), nt[:, 3, :],
                                               ALU.mult, ALU.mult).then_inc(sem("l_t"), 1)
                        dve.wait_ge(sem("l_hi"), f + 1)
                        v.tensor_tensor(lat_lo[:, f, :], nt[:, 4 + f % 2, :], lat_hi[:, f, :].bitcast(F32), ALU.subtract
                                        ).then_inc(sem("l_made"), 1)
                dve.wait_ge(sem("l_added"), 6)
                own.step(v.tensor_copy(stat[:, 32:36], bank[6][:, 0:4]))
                dve.wait_ge(sem("l_turned"), 1)
                dve.wait_ge(sem("l_made"), 5)
                own.step(v.tensor_tensor(nt[:, 4, :], bank[7][:], trigs[:, 3, :], ALU.mult))
                own.step(v.tensor_tensor(nt[:, 5, :], krT[:], trigs[:, 2, :], ALU.mult))
                v.tensor_tensor(krr[:], nt[:, 4, :], nt[:, 5, :], ALU.add).then_inc(sem("l_krr"), 1)
                dve.wait_ge(sem("l_krr"), 1)

            def mla():
                for hh in range(2):
                    own.step(v.memset(kr2[64 - 64 * hh:128 - 64 * hh, hh, :], 0.0))

                def body(i, u, nxt):
                    nxt(u, 1)
                    nxt(u, 2)
                    dve.wait_ge(sem("c_sums"), i + 1)
                    own.step(v.tensor_copy(stat[:, 0:16], bank[7][:, 0:16]))
                    by = stat[:, 0:16].rearrange("p (t c) -> p c t", c=4)
                    own.step(v.tensor_tensor(by[:, 2, :], by[:, 2, :], stat[:, 32:36], ALU.add))
                    v.tensor_tensor(by[:, 3, :], by[:, 3, :], stat[:, 32:36], ALU.add).then_inc(sem("c_sums_out"), 1)
                    dve.wait_ge(sem("c_std"), i + 1)
                    own.step(v.reciprocal(cst[:, 0:16], stat[:, 16:32]))
                    for hh in range(2):
                        for t in range(QT):
                            ins = v.tensor_scalar(kw[:, 4 * hh + t, :], ones[:], cst[:, 4 * t + 2 + hh:4 * t + 3 + hh], None, ALU.mult)
                            if t < QT - 1:
                                own.step(ins)
                        ins.then_inc(sem("c_wide"), 1)
                    dve.wait_ge(sem("c_wide"), 2 * i + 2)
                    own.step(v.tensor_scalar(cst[:, 0:16], cst[:, 0:16], 192.0 ** -0.5, None, ALU.mult))
                    dve.wait_ge(sem("c_turned_q"), i + 1)
                    own.step(v.tensor_tensor(qt2[:, 0, :], bank[5][:], trigs[:, 3, :], ALU.mult))
                    own.step(v.tensor_tensor(qt2[:, 1, :], qrg[:], trigs[:, 2, :], ALU.mult))
                    v.tensor_tensor(qr[:], qt2[:, 0, :], qt2[:, 1, :], ALU.add).then_inc(sem("c_q"), 1)
                    for hh in range(2):
                        lo = 64 * hh
                        dve.wait_ge(sem("c_kinv_out"), 2 * i + (hh + 1))
                        v.scalar_tensor_tensor(kn[:, hh, :], bank[3 + hh][:], vcol("k_nope"), nt[:, 3 + hh, :],
                                               ALU.mult, ALU.mult).then_inc(sem("c_k"), 1)
                        v.tensor_tensor(kr2[lo:lo + 64, hh, :], krr[lo:lo + 64, :], nt[lo:lo + 64, 3 + hh, :], ALU.mult
                                        ).then_inc(sem("c_k"), 1)
                    dve.wait_ge(sem("c_k"), 4 * i + 4)
                    dve.wait_ge(sem("c_v"), 2 * i + 2)
                    dve.wait_ge(banks_free, u + 1)
                    v.memset(small[:, 22:23], 0.0).then_inc(banks_free, 1)

                    def peak(n):
                        hh, t = divmod(n, QT)
                        w = (t + 1) * P
                        dve.wait_ge(sem("c_scores"), 8 * i + (n + 1))
                        own.step(v.tensor_tensor(bank[n % 2][:, t * P:w], bank[n % 2][:, t * P:w], tri[:], ALU.add))
                        own.step(v.tensor_reduce(cst[:, 16 + n:17 + n], bank[n % 2][:, 0:w], axis=AX, op=ALU.max, negate=True))
                        v.tensor_tensor(cst[:, 24 + n:25 + n], cst[:, 16 + n:17 + n], cst[:, 4 * t + hh:4 * t + hh + 1], ALU.mult
                                        ).then_inc(sem("c_max"), 1)

                    def out_(n):
                        hh, t = divmod(n, QT)
                        dve.wait_ge(sem("c_exp"), 8 * i + (n + 1))
                        own.step(v.reciprocal(cst[:, 40 + n:41 + n], cst[:, 32 + n:33 + n]))
                        dve.wait_ge(sem("c_weighed"), 8 * i + (n + 1))
                        v.tensor_scalar(mo_t[:, t, hh * P:hh * P + P], bank[4 + n % 2][:, 0:P], cst[:, 40 + n:41 + n], None,
                                        ALU.mult).then_inc(sem("c_out"), 1)

                    for n in range(8 + 2):
                        if n < 8:
                            peak(n)
                        if n >= 2:
                            out_(n - 2)
                    for hh in range(2):
                        dve.wait_ge(sem("c_mo_hi"), 2 * i + (hh + 1))
                        v.tensor_tensor(mo_lo[:, ds(2 * i + hh, 1), :], bank[6 + hh][:].unsqueeze(1),
                                        mo_hi[:, ds(2 * i + hh, 1), :].bitcast(F32), ALU.subtract).then_inc(sem("c_mo"), 1)
                ring("mla", 2, body, 36)

            def merge2_epi():
                def body(i, u, nxt):
                    nxt(u, 1)
                    nxt(u, 2)
                    dve.wait_ge(mm_done, u + 2)
                    dve.wait_ge(banks_free, u + 1)
                    own.step(v.tensor_tensor(nt[:, 3, :], bank[2][:], nt[:, 1, :], ALU.mult))
                    own.step(v.tensor_tensor(nt[:, ds(4, 1), :], aret[:, ds(i, 1), :], nt[:, ds(0, 1), :], ALU.mult))
                    v.tensor_tensor(nt[:, 2, :], nt[:, 3, :], nt[:, 4, :], ALU.add).then_inc(sem("mixed2"), 1)
                    v.memset(small[:, 23:24], 0.0).then_inc(banks_free, 1)
                    dve.wait_ge(sem("m2_hi_ready"), i + 1)
                    v.tensor_tensor(m2_lo[:, ds(i, 1), :], nt[:, ds(2, 1), :], m2_hi[:, ds(i, 1), :].bitcast(F32), ALU.subtract
                                    ).then_inc(sem("merged2"), 1)
                ring("merge2", 2, body, 2)

            def out2():
                def body(i, u, nxt):
                    for slot in range(2):
                        nxt(u, slot + 1)
                        dve.wait_ge(mm_done, u + slot + 1)
                        for n in range(2):
                            f = ds(4 * i + (2 * slot + n), 1)
                            ins = v.tensor_tensor(xT[:, f, :], bank[2 * slot + n][:].unsqueeze(1), xT[:, f, :], ALU.add)
                            if n == 0:
                                own.step(ins)
                        ins.then_inc(banks_free, 1)
                ring("out2", 2, body, 2)

            def mlp():
                norm(2, vT[:, VROWS["norm_mlp"]:VROWS["norm_mlp"] + KD])

                def body(i, u, nxt):
                    for k in range(4):
                        nxt(u, k + 1)
                        for n in range(2):
                            dve.wait_ge(sem("mlp_relu"), 8 * i + (2 * k + n + 1))
                            dve.wait_ge(sem("mlp_made"), 8 * i + max(2 * k + n - 1, 0))
                            v.tensor_tensor(nt[:, 4 + n, :], nt[:, n, :], nt[:, n, :], ALU.mult).then_inc(sem("mlp_squared"), 1)
                        for n in range(2):
                            dve.wait_ge(sem("mlp_hi"), 8 * i + (2 * k + n + 1))
                            v.tensor_tensor(u_lo[:, 2 * k + n, :], nt[:, 4 + n, :], u_hi[:, 2 * k + n, :].bitcast(F32), ALU.subtract
                                            ).then_inc(sem("mlp_made"), 1)
                    for k in range(4):
                        nxt(u, 4 + k + 1)
                        dve.wait_ge(mm_done, u + (5 + k))
                        dve.wait_ge(banks_free, u + (4 + k))
                        for n in range(2):
                            f = 2 * k + n
                            ins = v.tensor_tensor(xT[:, f, :], bank[2 * (k % 2) + n][:], xT[:, f, :], ALU.add)
                            if n == 0:
                                own.step(ins)
                        ins.then_inc(banks_free, 1)
                    dve.wait_ge(banks_free, u + 8)
                ring("mlp", 8, body, 4)

            def ple():
                norm(3, vT[:, VROWS["norm_ple"]:VROWS["norm_ple"] + KD])
                for k in range(2):
                    dve.wait_ge(sem("p_hi_ready"), k + 1)
                    v.tensor_tensor(p_lo[:, k, :], bank[5 + k][:], p_hi[:, k, :].bitcast(F32), ALU.subtract).then_inc(sem("p_made"), 1)

                def body(i, u, nxt):
                    nxt(u, 1)
                    nxt(u, 2)
                    dve.wait_ge(mm_done, u + 2)
                    dve.wait_ge(banks_free, u + 1)
                    own.step(v.tensor_tensor(nt[:, 1, :], bank[2][:], nt[:, 0, :], ALU.mult))
                    v.tensor_tensor(xT[:, ds(i, 1), :], nt[:, ds(1, 1), :], xT[:, ds(i, 1), :], ALU.add).then_inc(banks_free, 1)
                ring("ple", 2, body, 1)
                for n in range(1, 2 * QT, 2):
                    dve.wait_ge(sem("out_mm"), n + 1)
                    dve.wait_ge(sem("out_tile_ready"), n)
                    v.tensor_copy(out_sb[:, n // 2, 512:1024], bank[4 + n % 4][:]).then_inc(sem("out_tile_ready"), 1)

            prologue()
            index()
            values()
            qk()
            topk()
            attn_a()
            attn_b()
            turn_y()
            merge_epi()
            out1()
            norm2()
            ff()
            norm_mix()
            retention()
            latent()
            mla()
            merge2_epi()
            out2()
            mlp()
            ple()


NAMES = ['x', 'c', 'w_ada', 'b_ada', 'norm1_g', 'w_in', 'qn_a', 'kn_a', 'qn_b', 'kn_b', 'lam_q1', 'lam_k1',
         'lam_q2', 'lam_k2', 'subln_g', 'w_up_a', 'w_up_b', 'w_o', 'norm2_g', 'w_ff1', 'w_ff3', 'w_ff2',
         'p_2', 'positions_2', 'norm_mix_2', 'w_in_2', 'ret_norm_2', 'q_lat_norm_2', 'kv_lat_norm_2',
         'w_uq_2', 'w_ukv_2', 'q_norm_2', 'k_norm_2', 'w_br_2', 'w_bm_2', 'w_o_2', 'norm_mlp_2', 'w_up_2',
         'w_down_2', 'norm_ple_2', 'w_ple_gate_2', 'w_ple_2']


def shape_constants():
    p = np.arange(P, dtype=np.float32)
    table = np.zeros((P, 8), np.float32)
    table[:, 0] = np.float32(10000.0) ** (-p / np.float32(128))
    table[:, 1] = np.float32(10000.0) ** (-(p % 32) / np.float32(32))
    table[:, 2:2 + R_H] = np.log1p(-np.exp2(-5.0 - np.arange(R_H, dtype=np.float32)))
    return table


def kernel(**inputs):
    import concourse.bacc as bacc
    from concourse.bass_utils import run_bass_kernel_spmd

    nc = bacc.Bacc("TRN2", target_bir_lowering=False, num_devices=1)
    arrays, aps = {}, {}
    for name in NAMES:
        a = np.ascontiguousarray(inputs[name])
        arrays[f"in_{name}"] = a
        aps[name] = nc.dram_tensor(f"in_{name}", a.shape, mybir.dt.from_np(a.dtype), kind="ExternalInput").ap()
    arrays["in_shape_constants"] = shape_constants()
    aps["shape_constants"] = nc.dram_tensor("in_shape_constants", (P, 8), F32, kind="ExternalInput").ap()
    out = nc.dram_tensor("out", (1, S, D), F32, kind="ExternalOutput").ap()
    two_layers(nc, aps, out)
    r = run_bass_kernel_spmd(nc, [arrays], core_ids=[0])
    return r.results[0]["out"]
```

```python
import math
from contextlib import ExitStack

import numpy as np
import concourse.bass as bass
from concourse import mybir

F32 = mybir.dt.float32
F32R = mybir.dt.float32r
I32 = mybir.dt.int32
ALU = mybir.AluOpType
ACT = mybir.ActivationFunctionType
AX = mybir.AxisListType.X
ds = bass.ds

P = 128
S = 512
QT = S // P
D = 1024
KD = D // P
EPS = 1e-6
CHUNK = 64
H_A, D_A = 8, 64
H_B = 4
H_I = 4
TOPK = 128
FF = 2816
KFF = FF // P
C_QA, C_KA, C_VA, C_QB, C_KB, C_VB, C_QI, C_KI, C_WI, C_G = (
    0, 512, 1024, 1536, 2048, 2560, 3072, 3328, 3392, 3396)
LAMBDA_INIT = 0.8 - 0.6 * math.exp(0.0)
R_QK, R_V, R_H = 256, 512, 4
C_RQ, C_RK, C_RV, C_RG, C_CQ, C_CKV, C_KR, C_GR, C_GM = (
    0, 1024, 2048, 4096, 6144, 6528, 6784, 6848, 7872)
M_H = 8
FF2 = 4096
FAR = 1e32
INADMISSIBLE = -3.0e38
TAKEN = -3.3e38
SCORE_BANKS = (0, 1, 6, 7)
UW = 2048

VROWS = {}
_at = 0
for _n, _c in (("c", 8), ("norm1_g", 8), ("norm2_g", 8), ("norm_mix", 8), ("norm_mlp", 8),
               ("norm_ple", 8), ("b_ada", 48), ("ret_norm", 16), ("q_lat", 3), ("kv_lat", 2),
               ("subln", 1), ("qn_a", 1), ("kn_a", 1), ("qn_b", 1), ("kn_b", 1),
               ("q_nope", 1), ("q_rope", 1), ("k_nope", 1), ("k_rope", 1)):
    VROWS[_n] = _at
    _at += _c
NVR = _at

STAGES = [
    ("index", [2048, 8 * 132]),
    ("values", [2048] * 4),
    ("qk", [2048] * 8),
    ("merge", [2048, 1024] * 8),
    ("out1", [2048] * 4),
    ("ff1a", [2048] * 12), ("ff2a", [12 * P] * 8),
    ("ff1b", [2048] * 10), ("ff2b", [10 * P] * 8),
    ("retention", [2048] * 32),
    ("latent", [2048, 2048, 1024, 1024]),
    ("mla", [2 * 512, 3 * 384] * 4),
    ("merge2", [2048, 1024] * 8),
    ("out2", [2048] * 4),
    ("ple_in", [1024] * 2),
    ("mlp", [2048] * 32),
    ("ple", [2048] * 4),
]
U0, WIDTH = {}, []
for _n, _w in STAGES:
    U0[_n] = len(WIDTH)
    WIDTH += _w


class Count:

    def __init__(self, eng, sem):
        self.eng, self.sem, self.total, self.loop = eng, sem, 0, None

    def inc(self, ins):
        ins.then_inc(self.sem, 1)
        if self.loop is None:
            self.total += 1
            return self.total
        self.loop[2] += 1
        return self.total + self.loop[1] * self.loop[0] + self.loop[2]

    def settle(self):
        self.eng.wait_ge(self.sem, self.total if self.loop is None else self.total + self.loop[1] * self.loop[0] + self.loop[2])

    def step(self, ins):
        self.eng.wait_ge(self.sem, self.inc(ins))

    def enter(self, i, per):
        self.loop = [i, per, 0]

    def leave(self, times):
        assert self.loop[2] == self.loop[1], f"{self.sem}: {self.loop[2]} steps per turn, not {self.loop[1]}"
        self.total += self.loop[1] * times
        self.loop = None


def rows(ap, parts=P):
    return ap.rearrange("(k p) n -> p k n", p=parts)


def two_layers(nc, A, out):
    ctx = ExitStack()

    def sbuf(name, shape, dt=F32, at=ctx):
        return at.enter_context(nc.sbuf_tensor(name, shape, dt))

    sems = {}

    def sem(name):
        if name not in sems:
            sems[name] = ctx.enter_context(nc.semaphore(name))
        return sems[name]

    with ctx:
        xT = sbuf("xT", [P, KD, S])
        raw = sbuf("raw", [P, 2, UW])
        w_hi = sbuf("w_hi", [P, 2, UW], F32R)
        w_lo = sbuf("w_lo", [P, 2, UW], F32R)
        h_hi = sbuf("h_hi", [P, KD, S], F32R)
        h_lo = sbuf("h_lo", [P, KD, S], F32R)
        ident = sbuf("ident", [P, P])
        ones = sbuf("ones", [P, P])
        vT = sbuf("vT", [P, NVR])
        modc = sbuf("modc", [P, 48])
        gs1 = sbuf("gs1", [P, KD])
        gs2 = sbuf("gs2", [P, KD])
        eps = sbuf("eps", [P, 1])
        small = sbuf("small", [P, 32])
        minus_lam = sbuf("minus_lam", [P, 1])
        tri = sbuf("tri", [P, P])
        turn = sbuf("turn", [P, P])
        consts = sbuf("consts", [P, 8])
        cs = sbuf("cs", [P, 3 * KD])
        half = sbuf("half", [P, 2])
        stat = sbuf("stat", [P, 48])

        SH1, SC1, GT1, SH2, SC2, GT2 = (modc[:, KD * n:KD * (n + 1)] for n in range(6))

        def vcol(name, n=0):
            return vT[:, VROWS[name] + n:VROWS[name] + n + 1]

        layer1 = ExitStack()
        y_a = sbuf("y_a", [P, QT, 512], at=layer1)
        y_b = sbuf("y_b", [P, QT, 512], at=layer1)
        start = ExitStack()
        x_in = sbuf("x_in", [P, QT, D], at=start)
        x_n = sbuf("x_n", [P, QT, D], at=start)
        ada = sbuf("ada", [P, UW], at=start)
        ada_w = sbuf("ada_w", [P, 4, UW], at=start)
        vrows = sbuf("vrows", [P, P], at=start)
        lrow = sbuf("lrow", [1, 4 * D_A], at=start)
        lsum = sbuf("lsum", [1, 8], at=start)
        h_t = sbuf("h_t", [P, 2, S], at=start)
        start.close()
        attn = ExitStack()
        qaT = sbuf("qaT", [P, 4, S], at=attn)
        kaT = sbuf("kaT", [P, 4, S], at=attn)
        qbT = sbuf("qbT", [P, 4, S], at=attn)
        kbT = sbuf("kbT", [P, 4, S], at=attn)
        va = sbuf("va", [P, QT, 512], at=attn)
        vb = sbuf("vb", [P, QT, 512], at=attn)
        qiT = sbuf("qiT", [P, 2, S], at=attn)
        kiT = sbuf("kiT", [P, S], at=attn)
        wi = sbuf("wi", [P, QT, H_I], at=attn)
        dist_b = sbuf("dist_b", [P, QT, S], at=attn)
        dist_a = sbuf("dist_a", [P, QT, S], at=attn)
        t1 = sbuf("t1", [P, 2, S], at=attn)
        t2 = sbuf("t2", [P, 2, S], at=attn)
        t3 = sbuf("t3", [P, 2, S], at=attn)
        top8 = sbuf("top8", [P, 8], at=attn)
        slope = sbuf("slope", [P, H_A + H_B], at=attn)
        dist_i = sbuf("dist_i", [P, S], I32, at=attn)
        pair = sbuf("pair", [P, 2, S], at=attn)
        pairs = (pair, t3)
        halves = sbuf("halves", [P, P], at=attn)
        attn.close()
        merge = ExitStack()
        y_hi = sbuf("y_hi", [P, 8, S], F32R, at=merge)
        y_lo = sbuf("y_lo", [P, 8, S], F32R, at=merge)
        m_hi = sbuf("m_hi", [P, 8, S], F32R, at=merge)
        m_lo = sbuf("m_lo", [P, 8, S], F32R, at=merge)
        mt = sbuf("mt", [P, 3, S], at=merge)
        ada2 = sbuf("ada2", [P, 2, UW], at=merge)
        merge.close()
        layer1.close()

        nt = sbuf("nt", [P, 6, S])
        trigs = sbuf("trigs", [P, 4, S])
        ff_mem = ExitStack()
        g_hi = sbuf("g_hi", [P, 12, S], F32R, at=ff_mem)
        g_lo = sbuf("g_lo", [P, 12, S], F32R, at=ff_mem)
        ft = sbuf("ft", [P, 3, S], at=ff_mem)
        pos_i = sbuf("pos_i", [P, S], I32, at=ff_mem)
        ff_mem.close()
        aret = sbuf("aret", [P, KD, S])
        ret_mem = ExitStack()
        rqT = sbuf("rqT", [P, 2, S], at=ret_mem)
        rkT = sbuf("rkT", [P, 2, S], at=ret_mem)
        rv = sbuf("rv", [P, QT, S], at=ret_mem)
        rs_t = sbuf("rs_t", [P, QT, S], at=ret_mem)
        sg = sbuf("sg", [P, 4, S], at=ret_mem)
        yr_hi = sbuf("yr_hi", [P, 4, S], F32R, at=ret_mem)
        yr_lo = sbuf("yr_lo", [P, 4, S], F32R, at=ret_mem)
        rt = sbuf("rt", [P, 4, S], at=ret_mem)
        etab = sbuf("etab", [P, S], at=ret_mem)
        dtab = sbuf("dtab", [P, S], at=ret_mem)
        dtab_i = sbuf("dtab_i", [P, S], I32, at=ret_mem)
        ret_mem.close()
        mla_out = ExitStack()
        mo_hi = sbuf("mo_hi", [P, 8, S], F32R, at=mla_out)
        mo_lo = sbuf("mo_lo", [P, 8, S], F32R, at=mla_out)
        mla_mem = ExitStack()
        lat_hi = sbuf("lat_hi", [P, 5, S], F32R, at=mla_mem)
        lat_lo = sbuf("lat_lo", [P, 5, S], F32R, at=mla_mem)
        krr = sbuf("krr", [P, S], at=mla_mem)
        lat_mem = ExitStack()
        lat_t = sbuf("lat_t", [P, 5, S], at=lat_mem)
        lat_mem.close()
        qn = sbuf("qn", [P, 2, S], at=mla_mem)
        kn = sbuf("kn", [P, 2, S], at=mla_mem)
        qr = sbuf("qr", [P, S], at=mla_mem)
        vv = sbuf("vv", [P, QT, 256], at=mla_mem)
        mo_t = sbuf("mo_t", [P, QT, 256], at=mla_mem)
        kw = mo_t[:].rearrange("p t (h c) -> p (t h) c", h=2)
        cst = sbuf("cst", [P, 48], at=mla_mem)
        qrg = nt[:, 5, :]
        kr2 = trigs[:, 0:2, :]
        krT = trigs[:, 0, :]
        lat_tmp = mo_t[:].rearrange("p (a b) c -> p a (b c)", a=2)
        mla_mem.close()
        m2_hi = sbuf("m2_hi", [P, 8, S], F32R, at=mla_out)
        m2_lo = sbuf("m2_lo", [P, 8, S], F32R, at=mla_out)
        mla_out.close()
        p_in = sbuf("p_in", [P, QT, 256])
        p_hi = sbuf("p_hi", [P, 2, S], F32R)
        p_lo = sbuf("p_lo", [P, 2, S], F32R)
        u_hi = sbuf("u_hi", [P, KD, S], F32R)
        u_lo = sbuf("u_lo", [P, KD, S], F32R)
        out_sb = sbuf("out_sb", [P, QT, D])

        bank = [ctx.enter_context(nc.psum_tensor(f"bank{n}", [P, 512], F32)) for n in range(8)]

        raw_in = [sem("raw_in0"), sem("raw_in1")]
        hi_done, lo_done, mm_done, banks_free = sem("hi_done"), sem("lo_done"), sem("mm_done"), sem("banks_free")

        def raw_ready(u, slot):
            return 32 * (u - slot) + 64

        tok = "p t n -> p (t n)"
        ada_in1 = [raw[:, 0, :], raw[:, 1, :]] + [ada_w[:, n, :] for n in range(4)] + [y_a[:].rearrange(tok), y_b[:].rearrange(tok)]
        ada2_all = ada2[:].rearrange("p g n -> p (g n)")
        ada_in2 = [y_a[:].rearrange(tok), y_b[:].rearrange(tok)]

        block = ctx.enter_context(nc.Block())

        @block.sync
        def _(sp):
            def load(u, slot, pieces):
                if not isinstance(u, int) or u >= 2:
                    sp.wait_ge(lo_done, u - 1)
                if not isinstance(u, int):
                    sp.sem_inc(sem("slots_seen_free"), 1)
                for dst, src in pieces:
                    sp.dma_start(dst, src).then_inc(raw_in[slot], 64 // len(pieces))

            def slot_view(slot, k, n, at=0, width=None):
                width = width or n
                v = raw[:, slot, 0:k * width].rearrange("p (k n) -> p k n", k=k)
                return v[:, :, at:at + n]

            def prologue():
                sp.dma_start(x_in[:], A["x"][0].rearrange("(t p) n -> p t n", p=P)).then_inc(sem("x_in_done"), 16)
                for k, dst in enumerate(ada_in1):
                    if k == 2:
                        sp.wait_ge(sem("vectors_in"), 16 * 17)
                        sp.wait_ge(sem("head_vectors_in"), 16 * 6)
                    sp.dma_start(dst, A["w_ada"][0, k * P:k * P + P, 0:UW]).then_inc(sem(f"ada_in{k}"), 16)
                sp.wait_ge(sem("ada_free"), 2)

            w_in = rows(A["w_in"][0])

            def index():
                u = U0["index"]
                load(u, 0, [(slot_view(0, KD, 256), w_in[:, :, C_QI:C_QI + 256])])
                load(u + 1, 1, [(slot_view(1, KD, 64, 0, 132), w_in[:, :, C_KI:C_KI + 64]),
                                (slot_view(1, KD, 68, 64, 132), w_in[:, :, C_KI:C_KI + 68])])

            def values():
                for n, c in enumerate((C_VA, C_VB)):
                    for half in range(2):
                        load(U0["values"] + 2 * n + half, half,
                             [(slot_view(half, 4, 512), w_in[:, 4 * half:4 * half + 4, c:c + 512])])

            def qk():
                with sp.Fori(0, 4) as i:
                    for slot, (c0, c1) in enumerate(((C_QA, C_KA), (C_QB, C_KB))):
                        load(U0["qk"] + 2 * i + slot, slot,
                             [(slot_view(slot, KD, P, P * n, 256), w_in[:, :, ds(i * P + c, P)])
                              for n, c in enumerate((c0, c1))])

            def merge_loads():
                up_a, up_b = rows(A["w_up_a"][0]), rows(A["w_up_b"][0])
                with sp.Fori(0, KD) as i:
                    load(U0["merge"] + 2 * i, 0,
                         [(slot_view(0, KD, P, P * n, 256), w_in[:, :, ds(i * P + (C_G + D * n), P)])
                          for n in range(2)])
                    load(U0["merge"] + 2 * i + 1, 1,
                         [(slot_view(1, 4, P, P * n, 256), w[:, :, ds(i * P, P)])
                          for n, w in enumerate((up_a, up_b))])
                    sp.wait_ge(sem("y_mm"), 8)
                    for n in range(2):
                        sp.wait_ge(sem("ada_free"), 2 * i + (KD - 1 + n))
                        sp.sem_inc(sem("slots_seen_free"), 1)
                        sp.dma_start(ada_in2[n], A["w_ada"][0][ds(i * P, P), UW * (n + 1):UW * (n + 2)]
                                     ).then_inc(sem(f"ada_in{n}"), 16)

            def out1():
                w_o = rows(A["w_o"][0])
                with sp.Fori(0, 2) as i:
                    for slot in range(2):
                        load(U0["out1"] + 2 * i + slot, slot,
                             [(slot_view(slot, KD, 256), w_o[:, :, ds(i * 512 + 256 * slot, 256)])])

            def ff():
                w1, w3, w2 = rows(A["w_ff1"][0]), rows(A["w_ff3"][0]), rows(A["w_ff2"][0])
                for part, k0, k1 in (("a", 0, 12), ("b", 12, KFF)):
                    with sp.Fori(0, (k1 - k0) // 2) as i:
                        for slot in range(2):
                            load(U0["ff1" + part] + 2 * i + slot, slot,
                                 [(slot_view(slot, KD, P, P * n, 256), w[:, :, ds(i * 256 + (k0 + slot) * P, P)])
                                  for n, w in enumerate((w1, w3))])
                    with sp.Fori(0, KD // 2) as i:
                        for slot in range(2):
                            load(U0["ff2" + part] + 2 * i + slot, slot,
                                 [(slot_view(slot, k1 - k0, P), w2[:, k0:k1, ds(i * 256 + slot * P, P)])])

            w_in2 = rows(A["w_in_2"][0])

            def retention():
                w_br = rows(A["w_br_2"][0])
                with sp.Fori(0, R_H) as i:
                    u = U0["retention"] + 8 * i
                    for n, c in ((0, C_RQ), (1, C_RK)):
                        load(u + n, n, [(slot_view(n, KD, 256), w_in2[:, :, ds(i * R_QK + c, 256)])])
                    for half in range(2):
                        load(u + 2 + half, half, [(slot_view(half, 4, 512),
                                                   w_in2[:, 4 * half:4 * half + 4, ds(i * R_V + C_RV, 512)])])
                    for half in range(2):
                        load(u + 4 + half, half, [(slot_view(half, KD, 256),
                                                   w_in2[:, :, ds(i * R_V + (C_RG + 256 * half), 256)])])
                    for half in range(2):
                        load(u + 6 + half, half, [(slot_view(half, 4, 512),
                                                   w_br[:, ds(i * 4, 4), 512 * half:512 * half + 512])])

            def latent():
                u = U0["latent"]
                load(u, 0, [(slot_view(0, KD, 256), w_in2[:, :, C_CKV:C_CKV + 256])])
                load(u + 1, 1, [(slot_view(1, KD, 256), w_in2[:, :, C_CQ:C_CQ + 256])])
                load(u + 2, 0, [(slot_view(0, KD, P), w_in2[:, :, C_CQ + 256:C_CQ + 384])])
                load(u + 3, 1, [(slot_view(1, KD, 64, 64 * n, P), w_in2[:, :, C_KR:C_KR + 64]) for n in range(2)])

            def mla():
                w_uq, w_ukv = rows(A["w_uq_2"][0]), rows(A["w_ukv_2"][0])
                with sp.Fori(0, M_H // 2) as i:
                    u = U0["mla"] + 2 * i
                    load(u, 0, [(slot_view(0, 2, 512), w_ukv[:, :, ds(i * 512, 512)])])
                    q = w_uq[:, :, ds(i * 384, 384)].rearrange("p k (h c) -> p k h c", h=2)
                    load(u + 1, 1, [(slot_view(1, 3, n, at + n * hh, 384), q[:, :, hh, c:c + n])
                                    for at, c, n in ((0, 0, P), (2 * P, P, 64)) for hh in range(2)])

            def merge2_loads():
                w_bm = rows(A["w_bm_2"][0])
                with sp.Fori(0, KD) as i:
                    load(U0["merge2"] + 2 * i, 0,
                         [(slot_view(0, KD, P, P * n, 256), w_in2[:, :, ds(i * P + (C_GR + D * n), P)])
                          for n in range(2)])
                    load(U0["merge2"] + 2 * i + 1, 1, [(slot_view(1, KD, P), w_bm[:, :, ds(i * P, P)])])

            def out2():
                w_o = rows(A["w_o_2"][0])
                with sp.Fori(0, 2) as i:
                    for slot in range(2):
                        load(U0["out2"] + 2 * i + slot, slot,
                             [(slot_view(slot, KD, 256), w_o[:, :, ds(i * 512 + 256 * slot, 256)])])

            def mlp2():
                ple_in()
                mlp()

            def mlp():
                w_up, w_down = rows(A["w_up_2"][0]), rows(A["w_down_2"][0])
                with sp.Fori(0, 4) as i:
                    u = U0["mlp"] + 8 * i
                    for k in range(4):
                        load(u + k, k % 2, [(slot_view(k % 2, KD, 256), w_up[:, :, ds(i * D + 256 * k, 256)])])
                    for k in range(4):
                        load(u + 4 + k, k % 2, [(slot_view(k % 2, KD, 256),
                                                 w_down[:, ds(i * KD, KD), 256 * k:256 * k + 256])])

            def ple_in():
                w_p = rows(A["w_ple_2"][0])
                for half in range(2):
                    load(U0["ple_in"] + half, half, [(slot_view(half, 2, 512), w_p[:, :, 512 * half:512 * half + 512])])

            def ple():
                w_g = rows(A["w_ple_gate_2"][0])
                with sp.Fori(0, 2) as i:
                    for slot in range(2):
                        load(U0["ple"] + 2 * i + slot, slot,
                             [(slot_view(slot, KD, 256), w_g[:, :, ds(i * 512 + 256 * slot, 256)])])
                out_v = out[0].rearrange("(t p) n -> p t n", p=P)
                sp.wait_ge(sem("out_left"), QT)
                sp.dma_start(out_v[:, :, 0:512], out_sb[:, :, 0:512]).then_inc(sem("out_written"), 16)
                for n in range(2):
                    sp.wait_ge(sem("out_even"), n + 1)
                    sp.wait_ge(sem("out_odd"), n + 1)
                    sp.dma_start(out_v[:, 2 * n:2 * n + 2, 512:D], out_sb[:, 2 * n:2 * n + 2, 512:D]
                                 ).then_inc(sem("out_written"), 16)
                sp.wait_ge(sem("out_written"), 16 * 3)

            prologue()
            index()
            values()
            qk()
            merge_loads()
            out1()
            ff()
            retention()
            latent()
            mla()
            merge2_loads()
            out2()
            mlp2()
            ple()

        @block.gpsimd
        def _(pool):
            own = Count(pool, sem("pool_steps"))

            def prologue():
                row = VROWS
                for name, ap, lo in (("qn_a", A["qn_a"], 0), ("kn_a", A["kn_a"], 0), ("qn_b", A["qn_b"], 0),
                                     ("kn_b", A["kn_b"], 0), ("q_rope", A["q_norm_2"], P),
                                     ("k_rope", A["k_norm_2"], P)):
                    nc.gpsimd.dma_start(vrows[row[name]:row[name] + 1, :].rearrange("o (h n) -> o h n", h=2),
                                        ap[0:1, lo:lo + 64].unsqueeze(1).to_broadcast([1, 2, 64])
                                        ).then_inc(sem("head_vectors_in"), 16)
                own.step(nc.gpsimd.memset(ident[:], 0.0))
                own.step(nc.gpsimd.memset(halves[:], 0.0))
                nc.gpsimd.memset(ones[:], 1.0).then_inc(sem("ones_ready"), 1)
                nc.gpsimd.affine_select(out=ident[:], in_=ident[:], compare_op=ALU.not_equal, fill=1.0, base=0,
                                        pattern=[[-1, P]], channel_multiplier=1).then_inc(sem("ident_ready"), 1)
                own.step(nc.gpsimd.memset(halves[0:64, 0:64], 1.0))
                nc.gpsimd.memset(halves[64:P, 64:P], 1.0).then_inc(sem("halves_ready"), 1)

            def distances():
                pool.wait_ge(sem("h_made"), KD)
                pool.wait_ge(sem("halves_ready"), 1)
                for n in range(H_A):
                    own.inc(nc.gpsimd.memset(slope[:, n:n + 1], -2.0 ** (-8.0 * (n + 1) / H_A)))
                for n in range(H_B):
                    own.inc(nc.gpsimd.memset(slope[:, H_A + n:H_A + n + 1], -2.0 ** (-8.0 * (n + 1) / H_B)))
                own.settle()
                for t in range(QT):
                    own.step(nc.gpsimd.iota(dist_i[:], pattern=[[-1, S]], base=t * P, channel_multiplier=1))
                    own.step(nc.gpsimd.tensor_copy(dist_b[:, t, :], dist_i[:]))
                    own.step(nc.gpsimd.tensor_scalar(t3[:, 0, :], dist_b[:, t, :], 0.0, 2.0, ALU.max, ALU.mult))
                    own.step(nc.gpsimd.tensor_tensor(dist_b[:, t, :], t3[:, 0, :], dist_b[:, t, :], ALU.subtract))
                    nc.gpsimd.memset(dist_b[0:64, t, t * P + 64:t * P + P], FAR).then_inc(sem("dist_ready"), 1)

            def attn_copies(name, q, k, per):
                with pool.Fori(0, 2) as i:
                    for n in range(2):
                        pool.wait_ge(sem(name + "_scores"), 2 * per * i)
                        if n:
                            pool.wait_ge(banks_free, U0["qk"] + 8)
                        for m, src in enumerate((q, k)):
                            nc.gpsimd.tensor_copy(pairs[n][:, m, :], src[:, ds(2 * i + n, 1), :]
                                                  ).then_inc(sem(name + "_pair"), 1)

            def attn_a():
                pool.wait_ge(banks_free, U0["qk"] + 2)
                attn_copies("a", qaT, kaT, 8)

            def attn_b():
                pool.wait_ge(sem("a_scores"), 32)
                attn_copies("b", qbT, kbT, 8)

            def clear_ada():
                pool.wait_ge(sem("y_made"), 8)
                nc.gpsimd.memset(ada2[:], 0.0).then_inc(sem("ada_clear"), 1)

            def norm_sum(q):
                for f in range(1, KD - 2):
                    pool.wait_ge(sem("norm_squares"), KD * q + f + 1)
                    if f == 1:
                        nc.gpsimd.tensor_tensor(nt[:, 2, :], nt[:, 0, :], nt[:, 1, :], ALU.add).then_inc(sem("norm_added"), 2)
                    else:
                        pool.wait_ge(sem("norm_added"), (KD - 2) * q + f)
                        nc.gpsimd.tensor_tensor(nt[:, 2, :], nt[:, 2, :], nt[:, f % 2, :], ALU.add
                                                ).then_inc(sem("norm_added"), 1)

            def before_ff():
                norm_sum(0)
                masks()
                norm_sum(1)

            def before_mlp():
                ple()
                norm_sum(2)
                norm_sum(3)

            def masks():
                pool.wait_ge(mm_done, U0["ff1a"])
                nc.gpsimd.dma_start(pos_i[:], A["positions_2"][0, :].partition_broadcast(P)).then_inc(sem("positions_in"), 16)
                nc.gpsimd.dma_start(consts[:], A["shape_constants"]).then_inc(sem("positions_in"), 16)
                own.step(nc.gpsimd.memset(tri[:], 0.0))
                own.step(nc.gpsimd.affine_select(out=tri[:], in_=tri[:], compare_op=ALU.is_ge, fill=-1e30, base=0,
                                                 pattern=[[-1, P]], channel_multiplier=1))
                own.step(nc.gpsimd.memset(turn[:], 0.0))
                own.step(nc.gpsimd.memset(half[:], 0.0))
                for n in range(2):
                    own.step(nc.gpsimd.memset(half[64 * n:64 * n + 64, n:n + 1], 1.0))
                for at, sign in ((0, 1.0), (32, -1.0), (64, 1.0), (96, -1.0)):
                    blk = turn[at:at + 32, at + 32:at + 64] if sign > 0 else turn[at:at + 32, at - 32:at]
                    own.step(nc.gpsimd.affine_select(out=blk, in_=blk, compare_op=ALU.not_equal, fill=sign, base=0,
                                                     pattern=[[-1, 32]], channel_multiplier=1))
                nc.gpsimd.memset(small[:, 30:31], 0.0).then_inc(sem("masks_ready"), 1)

            def decays():
                pool.wait_ge(sem("hidden"), KFF)
                pool.wait_ge(mm_done, U0["retention"])
                pool.wait_ge(sem("masks_ready"), 1)
                own.step(nc.gpsimd.iota(dtab_i[:], pattern=[[1, S]], base=0, channel_multiplier=-1))
                own.step(nc.gpsimd.tensor_copy(dtab[:], dtab_i[:]))
                nc.gpsimd.affine_select(out=dtab[:], in_=dtab[:], compare_op=ALU.is_ge, fill=1e30, base=0,
                                        pattern=[[1, S]], channel_multiplier=-1).then_inc(sem("dtab_ready"), 1)
                pool.wait_ge(sem("dtab_ready"), 1)
                nc.gpsimd.memset(aret[:], 0.0).then_inc(sem("aret_clear"), 1)

            def ple():
                pool.wait_ge(mm_done, U0["out2"])
                nc.gpsimd.dma_start(p_in[:], A["p_2"][0, 0].rearrange("(t p) n -> p t n", p=P)).then_inc(sem("p_in_done"), 16)

            prologue()
            distances()
            attn_a()
            attn_b()
            clear_ada()
            before_ff()
            decays()
            before_mlp()

        @block.tensor
        def _(pe):
            def mm3(dst, ws, xs, cols=None):
                terms = [(a, b) for (a_hi, a_lo), (b_hi, b_lo) in zip(ws, xs)
                         for a, b in ((a_hi, b_hi), (a_hi, b_lo), (a_lo, b_hi))]
                for n, (a, b) in enumerate(terms):
                    last = nc.tensor.matmul(dst, a, b, start=n == 0, stop=n == len(terms) - 1)
                return last

            def unit_ready(u):
                pe.wait_ge(lo_done, u + 1)
                if not isinstance(u, int) or u >= 2:
                    pe.wait_ge(banks_free, u - 1)

            def w_tile(slot, k, row, col, n=P):
                a = k * row + col
                return w_hi[:, slot, a:a + n], w_lo[:, slot, a:a + n]

            h = [(h_hi[:, k, :], h_lo[:, k, :]) for k in range(KD)]

            def h_tok(k, t):
                return h_hi[:, k, t * P:t * P + P], h_lo[:, k, t * P:t * P + P]

            def pair_unit(u, slot, xs, made=None):
                unit_ready(u)
                tiles_by_k([(bank[2 * slot + n][:], P * n) for n in range(2)], slot, 256, xs, made)

            def tiles_by_k(dsts, slot, row, xs, made=None):
                last_k = len(xs) - 1
                for k, (x_hi, x_lo) in enumerate(xs):
                    if made:
                        pe.wait_ge(made[0], made[1] + k + 1)
                    for dst, col in dsts:
                        a_hi, a_lo = w_tile(slot, k, row, col)
                        for n, (a, b) in enumerate(((a_hi, x_hi), (a_hi, x_lo), (a_lo, x_hi))):
                            last = nc.tensor.matmul(dst, a, b, start=k == n == 0, stop=k == last_k and n == 2)
                last.then_inc(mm_done, 1)

            def ada_columns(dst, sums, tiles):
                for m in tiles:
                    last = nc.tensor.matmul(dst[:, m:m + 1], sums[:, m * P:m * P + P], ones[:, 0:1], start=True, stop=True)
                last.then_inc(sem("ada_mm"), 1)

            def prologue():
                pe.wait_ge(sem("ident_ready"), 1)
                pe.wait_ge(sem("vectors_in"), 16 * 17)
                pe.wait_ge(sem("head_vectors_in"), 16 * 6)
                nc.tensor.transpose(bank[4][:, 0:NVR], vrows[0:NVR, :], ident[0:NVR, 0:NVR]).then_inc(sem("vT_mm"), 1)
                pe.wait_ge(sem("x_in_done"), 16)
                def turn(which, f):
                    for t in range(QT):
                        if which and f == 0:
                            pe.wait_ge(sem("x_n_ready"), t + 1)
                        if t == 0 and which and f >= 4:
                            pe.wait_ge(sem("h_t_ready"), f - 3)
                        elif t == 0 and (which or f >= 4):
                            pe.wait_ge(sem("xT_ready"), f + 5 if which else f - 3)
                        last = nc.tensor.transpose(bank[f % 4][:, t * P:t * P + P], (x_in, x_n)[which][:, t, f * P:f * P + P],
                                                   ident[:])
                    last.then_inc(sem("x_mm"), 1)

                for f in range(KD):
                    turn(0, f)
                for f in range(4):
                    turn(1, f)
                pe.wait_ge(sem("ones_ready"), 1)
                pe.wait_ge(sem("lambda_sum"), 1)
                nc.tensor.matmul(bank[5][:, 0:1], ones[0:1, :], lsum[0:1, 4:5], start=True, stop=True
                                 ).then_inc(sem("lambda_mm"), 1)
                pe.wait_ge(sem("ada_free"), KD)
                ada_columns(bank[6], ada[:], range(2 * KD))
                for f in range(4, KD):
                    turn(1, f)

            def index():
                u = U0["index"]
                pe.wait_ge(sem("h_t_ready"), KD)
                pair_unit(u, 0, h, (sem("h_made"), 0))
                unit_ready(u + 1)
                mm3(bank[2][:], [w_tile(1, k, 132, 0) for k in range(KD)], h)
                for t in range(QT):
                    last = mm3(bank[3][:, 4 * t:4 * t + 4], [h_tok(k, t) for k in range(KD)],
                               [w_tile(1, k, 132, P, 4) for k in range(KD)])
                last.then_inc(mm_done, 1)

            def value_pair(u):
                for half in range(2):
                    pe.wait_ge(lo_done, u + half + 1)
                    for t in range(QT):
                        if half == 0 and t % 2 == 0:
                            pe.wait_ge(banks_free, u - 1 + t // 2)
                        for k in range(4):
                            (a_hi, a_lo), (b_hi, b_lo) = h_tok(4 * half + k, t), w_tile(half, k, 512, 0, 512)
                            for n, (a, b) in enumerate(((a_hi, b_hi), (a_hi, b_lo), (a_lo, b_hi))):
                                last = nc.tensor.matmul(bank[t][:], a, b, start=half == k == n == 0,
                                                        stop=half == 1 and k == 3 and n == 2)
                    last.then_inc(mm_done, 1)

            def values():
                value_pair(U0["values"])
                value_pair(U0["values"] + 2)

            def qk():
                pe.wait_ge(sem("halves_ready"), 1)
                with pe.Fori(0, 4) as i:
                    for slot in range(2):
                        unit_ready(U0["qk"] + 2 * i + slot)
                        for n in range(2):
                            last = mm3(bank[2 * slot + n][:], [w_tile(slot, k, 256, P * n) for k in range(KD)], h)
                            if slot == 1 and n == 0:
                                head_sums(i, 0)
                        last.then_inc(mm_done, 1)
                    head_sums(i, 1)

            def head_sums(i, slot):
                for n in range(2):
                    pe.wait_ge(sem("qk_squares"), 4 * i + (2 * slot + n + 1))
                    pe.wait_ge(sem("qk_std"), 4 * i + max(2 * slot + n - 1, 0))
                    nc.tensor.matmul(bank[4 + n][:], halves[:], t1[:, n, :], start=True, stop=True
                                     ).then_inc(sem("qk_sums"), 1)

            def topk():
                pe.wait_ge(sem("index_ready"), 2)
                g = 0
                for t in range(QT):
                    w = (t + 1) * P
                    for hh in range(H_I):
                        if g >= 4:
                            pe.wait_ge(sem("logits_read"), g - 3)
                        lo = 64 * (hh % 2)
                        nc.tensor.matmul(bank[4 + g % 4][:, 0:w], qiT[lo:lo + 64, hh // 2, t * P:t * P + P],
                                         kiT[lo:lo + 64, 0:w], start=True, stop=True).then_inc(sem("logits_mm"), 1)
                        g += 1

            def prev(i, per, n):
                return per * i + max(n - 1, 0)

            def attn_a():
                pe.wait_ge(banks_free, U0["qk"] + 8)
                pe.wait_ge(sem("logits_read"), QT * H_I)
                with pe.Fori(0, 2) as i:
                    def scores(n):
                        head, t = divmod(n, QT)
                        q_k = pairs[head // 2]
                        pe.wait_ge(sem("a_pair"), 4 * i + (head // 2 * 2 + 2))
                        pe.wait_ge(sem("a_biased"), 16 * i + max(n - 3, 0))
                        lo = 64 * (head % 2)
                        nc.tensor.matmul(bank[2 + n % 4][:, 0:(t + 1) * P], q_k[lo:lo + 64, 0, t * P:t * P + P],
                                         q_k[lo:lo + 64, 1, 0:(t + 1) * P], start=True, stop=True
                                         ).then_inc(sem("a_scores"), 1)

                    def turn_p(n):
                        pe.wait_ge(sem("a_exp"), 16 * i + (n + 1))
                        pe.wait_ge(sem("a_pT"), prev(i, 16, n))
                        for j in range(n % QT + 1):
                            last = nc.tensor.transpose(bank[6 + n % 2][:, j * P:j * P + P], t1[:, n % 2, j * P:j * P + P], ident[:])
                        last.then_inc(sem("a_turned"), 1)

                    def weigh(n):
                        head, t = divmod(n, QT)
                        pe.wait_ge(sem("a_pT"), 16 * i + (n + 1))
                        pe.wait_ge(sem("a_out"), prev(i, 16, n))
                        for j in range(t + 1):
                            last = nc.tensor.matmul(bank[n % 2][:, 0:D_A], t2[:, n % 2, j * P:j * P + P],
                                                    va[:, j, ds(2 * P * i + head * D_A, D_A)], start=j == 0, stop=j == t)
                        last.then_inc(sem("a_weighed"), 1)

                    scores(0)
                    for n in range(16 + 2):
                        if n + 1 < 16:
                            scores(n + 1)
                        if 0 <= n - 1 < 16:
                            turn_p(n - 1)
                        if n >= 2:
                            weigh(n - 2)

            def attn_b():
                pe.wait_ge(sem("a_out"), 32)
                with pe.Fori(0, 2) as i:
                    def scores(n):
                        head, t = divmod(n, QT)
                        q_k = pairs[head]
                        pe.wait_ge(sem("b_pair"), 4 * i + (2 * head + 2))
                        for m in range(2):
                            pe.wait_ge(sem("b_biased"), 16 * i + max(2 * n - 2, 0))
                            nc.tensor.matmul(bank[2 + 2 * (t % 2) + m][:, 0:(t + 1) * P],
                                             q_k[64 * m:64 * m + 64, 0, t * P:t * P + P],
                                             q_k[64 * m:64 * m + 64, 1, 0:(t + 1) * P], start=True, stop=True
                                             ).then_inc(sem("b_scores"), 1)

                    def turn_p(n):
                        t = n % QT
                        pe.wait_ge(sem("b_mixed"), 8 * i + (n + 1))
                        pe.wait_ge(sem("b_pT"), prev(i, 8, n))
                        for j in range(t + 1):
                            last = nc.tensor.transpose(bank[6 + t % 2][:, j * P:j * P + P],
                                                       dist_a[:, 2 * (t % 2), j * P:j * P + P], ident[:])
                        last.then_inc(sem("b_turned"), 1)

                    def weigh(n):
                        head, t = divmod(n, QT)
                        pe.wait_ge(sem("b_pT"), 8 * i + (n + 1))
                        pe.wait_ge(sem("b_out"), prev(i, 8, n))
                        for j in range(t + 1):
                            last = nc.tensor.matmul(bank[t % 2][:, 0:P], t2[:, t % 2, j * P:j * P + P],
                                                    vb[:, j, ds(2 * P * i + head * P, P)], start=j == 0, stop=j == t)
                        last.then_inc(sem("b_weighed"), 1)

                    scores(0)
                    for n in range(2 * QT + 2):
                        if n + 1 < 2 * QT:
                            scores(n + 1)
                        if 0 <= n - 1 < 2 * QT:
                            turn_p(n - 1)
                        if n >= 2:
                            weigh(n - 2)

            def turn_y():
                for f in range(8):
                    if f >= 4:
                        pe.wait_ge(sem("y_b_scaled"), QT * (f - 3))
                    if f >= 4:
                        pe.wait_ge(sem("y_made"), f - 3)
                    elif f == 0:
                        pe.wait_ge(sem("b_out"), 16)
                    for t in range(QT):
                        last = nc.tensor.transpose(bank[f % 4][:, t * P:t * P + P],
                                                   (y_a, y_b)[f // 4][:, t, (f % 4) * P:(f % 4) * P + P], ident[:])
                    last.then_inc(sem("y_mm"), 1)

            def merge_mm():
                pe.wait_ge(sem("y_made"), 8)
                y = [(y_hi[:, k, :], y_lo[:, k, :]) for k in range(8)]
                with pe.Fori(0, KD) as i:
                    u = U0["merge"] + 2 * i
                    pair_unit(u, 0, h)
                    unit_ready(u + 1)
                    for n in range(2):
                        last = mm3(bank[2 + n][:], [w_tile(1, k, 256, P * n) for k in range(4)], y[4 * n:4 * n + 4])
                    last.then_inc(mm_done, 1)

            def out1():
                pe.wait_ge(sem("ada_free"), 3 * KD)
                ada_columns(bank[5], ada2_all, range(KD))
                m = [(m_hi[:, k, :], m_lo[:, k, :]) for k in range(KD)]
                for k in range(4):
                    pair_unit(U0["out1"] + k, k % 2, m, (sem("merged"), 0))

            def norm_sum(q):
                pe.wait_ge(sem("norm_added"), (KD - 2) * (q + 1))
                nc.tensor.matmul(bank[4][:], ones[:], nt[:, 2, :], start=True, stop=False)
                for n in range(2):
                    pe.wait_ge(sem("norm_squares"), KD * (q + 1) - 1 + n)
                    last = nc.tensor.matmul(bank[4][:], ones[:], nt[:, n, :], start=False, stop=n == 1)
                last.then_inc(sem("norm_sums"), 1)

            def norm2():
                norm_sum(0)
                ada_columns(bank[6], ada2_all, range(KD, 3 * KD))
                ada_columns(bank[7], ada2_all, range(3 * KD, 4 * KD))

            def ff():
                g = [(g_hi[:, k, :], g_lo[:, k, :]) for k in range(12)]
                for part, n, done in (("a", 12, 0), ("b", 10, 12)):
                    with pe.Fori(0, n // 2) as i:
                        for slot in range(2):
                            pair_unit(U0["ff1" + part] + 2 * i + slot, slot, h, (sem("h_made"), KD))
                    def down(i, slot):
                        unit_ready(U0["ff2" + part] + 2 * i + slot)
                        tiles_by_k([(bank[2 * slot][:], 0)], slot, P, g[:n], (sem("hidden"), done))

                    with pe.Fori(0, KD // 2) as i:
                        for slot in range(2):
                            down(i, slot)

            def norm_mix():
                norm_sum(1)

            def retention():
                pe.wait_ge(sem("norm_std"), 2)
                yr = [(yr_hi[:, k, :], yr_lo[:, k, :]) for k in range(4)]
                with pe.Fori(0, R_H) as i:
                    u = U0["retention"] + 8 * i
                    pair_unit(u, 0, h, (sem("h_made"), 2 * KD))
                    pair_unit(u + 1, 1, h)
                    value_pair(u + 2)
                    pe.wait_ge(sem("r_rope"), 2 * i + 2)
                    pe.wait_ge(banks_free, u)
                    for j in range(QT):
                        for d in range(2):
                            last = nc.tensor.matmul(bank[4 + j][:, 0:S - j * P], rkT[:, d, j * P:j * P + P],
                                                    rqT[:, d, j * P:S], start=d == 0, stop=d == 1)
                        last.then_inc(sem("r_scores"), 1)
                    pe.wait_ge(banks_free, u + 4)
                    pair_unit(u + 4, 0, h)
                    pe.wait_ge(sem("r_decayed"), 4 * i + 4)
                    for vt in range(4):
                        for j in range(QT):
                            last = nc.tensor.matmul(bank[4 + vt][:, j * P:S], rv[:, j, vt * P:vt * P + P],
                                                    rs_t[:, j, 0:S - j * P], start=j == 0, stop=j == QT - 1)
                        last.then_inc(sem("r_o"), 1)
                    for vt in range(4):
                        pe.wait_ge(sem("r_squares"), 4 * i + (vt + 1))
                        nc.tensor.matmul(bank[2][:], ones[:], nt[:, vt % 2, :], start=vt == 0, stop=vt == 3
                                         ).then_inc(sem("r_added"), 1)
                    unit_ready(u + 5)
                    mm3(bank[3][:], [w_tile(1, k, 256, P) for k in range(KD)], h)
                    pe.wait_ge(sem("r_std"), i + 1)
                    mm3(bank[2][:], [w_tile(1, k, 256, 0) for k in range(KD)], h).then_inc(mm_done, 1)
                    for half in range(2):
                        pe.wait_ge(lo_done, u + (7 + half))
                        for k0, n0 in ((0, 0), (0, 2), (2, 0), (2, 2)):
                            pe.wait_ge(banks_free, u + 5 + (half or n0 > 0))
                            for k in (k0, k0 + 1):
                                pe.wait_ge(sem("r_y"), 4 * i + (k + 1))
                                for n in (n0, n0 + 1):
                                    a_hi, a_lo = w_tile(half, k, 512, P * n)
                                    for m, (a, b) in enumerate(((a_hi, yr[k][0]), (a_hi, yr[k][1]), (a_lo, yr[k][0]))):
                                        last = nc.tensor.matmul(bank[4 * half + n][:], a, b, start=k == m == 0,
                                                                stop=k == 3 and m == 2)
                        last.then_inc(mm_done, 1)

            def latent():
                def add(n):
                    pe.wait_ge(sem("l_squares"), n + 1)
                    nc.tensor.matmul(bank[4 + (n >= 2)][:], ones[:], nt[:, n, :], start=n in (0, 2), stop=n in (1, 4)
                                     ).then_inc(sem("l_added"), 1)

                u = U0["latent"]
                pair_unit(u, 0, h)
                pair_unit(u + 1, 1, h)
                add(0)
                add(1)
                for n in range(2):
                    unit_ready(u + 2 + n)
                    mm3(bank[2 * n][:], [w_tile(n, k, P, 0) for k in range(KD)], h).then_inc(mm_done, 1)
                    for m in ((2, 3), (4,))[n]:
                        add(m)
                pe.wait_ge(sem("l_squares"), 6)
                for t in range(QT):
                    last = nc.tensor.matmul(bank[6][:, t:t + 1], nt[0:64, 5, t * P:t * P + P], ones[0:64, 0:1],
                                            start=True, stop=True)
                last.then_inc(sem("l_added"), 1)
                pe.wait_ge(sem("l_kr"), 1)
                pe.wait_ge(sem("masks_ready"), 1)
                nc.tensor.matmul(bank[7][:], turn[:], krT, start=True, stop=True).then_inc(sem("l_turned"), 1)

            def mla():
                lq = [(lat_hi[:, k, :], lat_lo[:, k, :]) for k in range(3)]
                lkv = [(lat_hi[:, 3 + k, :], lat_lo[:, 3 + k, :]) for k in range(2)]

                def wide(w, k, lo):
                    return w[:, 0, k * 512:(k + 1) * 512].rearrange("p (h c) -> p h c", h=2)[:, :, lo:lo + P]

                with pe.Fori(0, M_H // 2) as i:
                    u = U0["mla"] + 2 * i
                    pe.wait_ge(sem("c_mo"), 2 * i)
                    pe.wait_ge(sem("l_made"), 2)
                    unit_ready(u)
                    for n in range(2):
                        last = mm3(bank[3 + n][:], [w_tile(0, k, 512, 256 * n) for k in range(2)], lkv)
                    last.then_inc(sem("c_k_mm"), 1)
                    pe.wait_ge(sem("l_std"), 2)
                    pe.wait_ge(sem("l_kr_sums"), 1)
                    for t in range(QT):
                        at = 256 * (t % 2)
                        last = mm3(bank[5 + t // 2][:, at:at + 256].rearrange("p (h c) -> p h c", h=2),
                                   [(a[:, t * P:t * P + P], b[:, t * P:t * P + P]) for a, b in lkv],
                                   [(wide(w_hi, k, P), wide(w_lo, k, P)) for k in range(2)])
                    last.then_inc(mm_done, 1)
                    pe.wait_ge(sem("l_krr"), 1)
                    pe.wait_ge(sem("c_squares"), 5 * i + 2)
                    for t in range(QT):
                        for hh in range(2):
                            last = nc.tensor.matmul(bank[7][:, 2 * t + hh:2 * t + hh + 1], nt[:, 3 + hh, t * P:t * P + P],
                                                    ones[:, 0:1], start=True, stop=True)
                    last.then_inc(sem("c_sums"), 1)
                    unit_ready(u + 1)
                    pe.wait_ge(sem("l_made"), 5)
                    mm3(bank[2][:], [w_tile(1, k, 384, 2 * P) for k in range(3)], lq).then_inc(sem("c_qr_mm"), 1)
                    for n in range(2):
                        last = mm3(bank[n][:], [w_tile(1, k, 384, P * n) for k in range(3)], lq)
                    last.then_inc(mm_done, 1)
                    pe.wait_ge(sem("c_qrg"), i + 1)
                    pe.wait_ge(sem("c_v"), 2 * i + 2)
                    nc.tensor.matmul(bank[5][:], turn[:], qrg, start=True, stop=True).then_inc(sem("c_turned_q"), 1)
                    for hh in range(2):
                        pe.wait_ge(sem("c_wide"), 2 * i + (hh + 1))
                        for t in range(QT):
                            last = nc.tensor.transpose(bank[6 + hh][:, t * P:t * P + P], kw[:, 4 * hh + t, :], ident[:])
                        last.then_inc(sem("c_kinv"), 1)
                    pe.wait_ge(sem("c_squares"), 5 * i + 5)
                    for t in range(QT):
                        tok = slice(t * P, t * P + P)
                        for hh in range(2):
                            dst = bank[2][:, 2 * t + hh:2 * t + hh + 1]
                            nc.tensor.matmul(dst, nt[:, hh, tok], ones[:, 0:1], start=True, stop=False)
                            last = nc.tensor.matmul(dst, nt[:, 2, tok], half[:, hh:hh + 1], start=False, stop=True)
                    last.then_inc(sem("c_sums"), 1)
                    pe.wait_ge(banks_free, u + 2)
                    pe.wait_ge(sem("c_sums_out"), 2 * i + 2)

                    def scores(n):
                        hh, t = divmod(n, QT)
                        pe.wait_ge(sem("c_exp"), 8 * i + max(n - 3, 0))
                        w = (t + 1) * P
                        nc.tensor.matmul(bank[SCORE_BANKS[n % 4]][:, 0:w], qn[:, hh, t * P:t * P + P], kn[:, hh, 0:w],
                                         start=True, stop=False)
                        nc.tensor.matmul(bank[SCORE_BANKS[n % 4]][:, 0:w], qr[:, t * P:t * P + P], kr2[:, hh, 0:w],
                                         start=False, stop=True).then_inc(sem("c_scores"), 1)

                    def turn_p(n):
                        pe.wait_ge(sem("c_exp"), 8 * i + (n + 1))
                        pe.wait_ge(sem("c_pT"), prev(i, 8, n))
                        for j in range(n % QT + 1):
                            last = nc.tensor.transpose(bank[2 + n % 2][:, j * P:j * P + P], nt[:, n % 2, j * P:j * P + P], ident[:])
                        last.then_inc(sem("c_turned"), 1)

                    def weigh(n):
                        hh, t = divmod(n, QT)
                        pe.wait_ge(sem("c_pT"), 8 * i + (n + 1))
                        pe.wait_ge(sem("c_out"), prev(i, 8, n))
                        for j in range(t + 1):
                            last = nc.tensor.matmul(bank[4 + n % 2][:, 0:P], nt[:, 2 + n % 2, j * P:j * P + P],
                                                    vv[:, j, hh * P:hh * P + P], start=j == 0, stop=j == t)
                        last.then_inc(sem("c_weighed"), 1)

                    scores(0)
                    for n in range(8 + 2):
                        if n + 1 < 8:
                            scores(n + 1)
                        if 0 <= n - 1 < 8:
                            turn_p(n - 1)
                        if n >= 2:
                            weigh(n - 2)
                    pe.wait_ge(sem("c_exp"), 8 * i + 8)
                    for hh in range(2):
                        pe.wait_ge(sem("c_out"), 8 * i + 4 * hh + 4)
                        for t in range(QT):
                            last = nc.tensor.transpose(bank[6 + hh][:, t * P:t * P + P], mo_t[:, t, hh * P:hh * P + P], ident[:])
                        last.then_inc(sem("c_mo_mm"), 1)

            def merge2_mm():
                mo = [(mo_hi[:, k, :], mo_lo[:, k, :]) for k in range(8)]
                pe.wait_ge(sem("c_mo"), 8)
                with pe.Fori(0, KD) as i:
                    u = U0["merge2"] + 2 * i
                    pair_unit(u, 0, h)
                    unit_ready(u + 1)
                    mm3(bank[2][:], [w_tile(1, k, P, 0) for k in range(KD)], mo).then_inc(mm_done, 1)

            def out2():
                m = [(m2_hi[:, k, :], m2_lo[:, k, :]) for k in range(KD)]
                for k in range(4):
                    pair_unit(U0["out2"] + k, k % 2, m, (sem("merged2"), 0))
                    if k == 1:
                        pe.wait_ge(sem("p_in_done"), 16)
                        for n in range(2):
                            for t in range(QT):
                                last = nc.tensor.transpose(bank[5 + n][:, t * P:t * P + P], p_in[:, t, n * P:n * P + P], ident[:])
                            last.then_inc(sem("p_mm"), 1)

            def mlp():
                norm_sum(2)
                ple_in()
                g = [(u_hi[:, k, :], u_lo[:, k, :]) for k in range(KD)]

                pe.wait_ge(banks_free, U0["mlp"])

                def quarter(i):
                    u = U0["mlp"] + 8 * i
                    for k in range(4):
                        pair_unit(u + k, k % 2, h, (sem("h_made"), 3 * KD))
                    for k in range(4):
                        pair_unit(u + 4 + k, k % 2, g, (sem("mlp_made"), 8 * i))

                with pe.Fori(0, 4) as i:
                    quarter(i)

            def ple():
                norm_sum(3)
                for k in range(4):
                    pair_unit(U0["ple"] + k, k % 2, h, (sem("h_made"), 4 * KD))
                    if k == 2:
                        turn_out(0)
                turn_out(1)

            def ple_in():
                u = U0["ple_in"]
                pe.wait_ge(sem("p_made"), 2)
                for half in range(2):
                    pe.wait_ge(lo_done, u + half + 1)
                    for n in range(4):
                        if half == 0:
                            pe.wait_ge(banks_free, u)
                        elif n < 3:
                            pe.wait_ge(sem("p_copied"), n + 1)
                        else:
                            pe.wait_ge(banks_free, u + 1)
                        last = mm3(bank[n][:], [w_tile(half, k, 512, P * n) for k in range(2)],
                                   [(p_hi[:, k, :], p_lo[:, k, :]) for k in range(2)])
                    last.then_inc(mm_done, 1)

            def turn_out(half):
                pe.wait_ge(sem("x_done"), 4 * half + 4)
                for t in range(QT):
                    if half:
                        pe.wait_ge(sem("out_left"), t + 1)
                    for f in range(4):
                        last = nc.tensor.transpose(bank[4 + t][:, f * P:f * P + P], xT[:, 4 * half + f, t * P:t * P + P], ident[:])
                    last.then_inc(sem("out_mm"), 1)

            prologue()
            index()
            topk()
            values()
            qk()
            attn_a()
            attn_b()
            turn_y()
            merge_mm()
            out1()
            norm2()
            ff()
            norm_mix()
            retention()
            latent()
            mla()
            merge2_mm()
            out2()
            mlp()
            ple()

        @block.scalar
        def _(act):
            own = Count(act, sem("act_steps"))

            def split(u, slot=None, width=None):
                if isinstance(u, int):
                    if u >= len(WIDTH):
                        return
                    slot, width = u % 2, WIDTH[u]
                act.wait_ge(raw_in[slot], raw_ready(u, slot))
                if not isinstance(u, int) or u >= 2:
                    act.wait_ge(mm_done, u - 1)
                nc.scalar.activation(w_hi[:, slot, 0:width], raw[:, slot, 0:width], ACT.Copy).then_inc(hi_done, 1)

            def ring(name, per, body, count=0):
                u0, n = U0[name], len(dict(STAGES)[name]) // per
                widths = WIDTH[u0:u0 + per]
                if n > 1:
                    with act.Fori(0, n - 1) as i:
                        own.enter(i, count)
                        body(i, u0 + per * i, lambda u, k: split(u + k, k % 2, (widths + widths[:1])[k]))
                    own.leave(n - 1)
                body(n - 1, u0 + per * (n - 1), lambda u, k: split(u + k))

            def prologue():
                row = VROWS
                for name, ap, n in (("c", A["c"], 8), ("norm1_g", A["norm1_g"], 8), ("b_ada", A["b_ada"], 48),
                                    ("norm2_g", A["norm2_g"], 8), ("norm_mix", A["norm_mix_2"], 8),
                                    ("norm_mlp", A["norm_mlp_2"], 8), ("norm_ple", A["norm_ple_2"], 8),
                                    ("ret_norm", A["ret_norm_2"], 16), ("q_lat", A["q_lat_norm_2"], 3),
                                    ("kv_lat", A["kv_lat_norm_2"], 2), ("subln", A["subln_g"], 1)):
                    nc.scalar.dma_start(vrows[row[name]:row[name] + n, :],
                                 ap[0, :].rearrange("(r n) -> r n", n=P)).then_inc(sem("vectors_in"), 16)
                for name, ap in (("q_nope", A["q_norm_2"]), ("k_nope", A["k_norm_2"])):
                    nc.scalar.dma_start(vrows[row[name]:row[name] + 1, :], ap[0:1, 0:P]).then_inc(sem("vectors_in"), 16)
                for n, name in enumerate(("lam_q1", "lam_k1", "lam_q2", "lam_k2")):
                    nc.scalar.dma_start(lrow[0:1, D_A * n:D_A * n + D_A], A[name]).then_inc(sem("vectors_in"), 16)
                act.wait_ge(sem("eps_ready"), 1)
                act.wait_ge(sem("x_in_done"), 16)
                for t in range(QT):
                    own.inc(nc.scalar.activation(x_n[:, t, :], x_in[:, t, :], ACT.Square, accum_out=small[:, t:t + 1]))
                own.settle()
                nc.scalar.activation(small[:, 4:8], small[:, 0:4], ACT.Sqrt, scale=1.0 / D, bias=eps[:]
                                     ).then_inc(sem("x_std"), 1)
                act.wait_ge(sem("vT_mm"), 1)
                nc.scalar.activation(vT[:], bank[4][:, 0:NVR], ACT.Copy).then_inc(sem("vT_ready"), 1)
                act.wait_ge(sem("vT_ready"), 1)
                nc.scalar.activation(cs[:, 0:KD], vT[:, 0:KD], ACT.Exp, scale=-1.0).then_inc(sem("silu_exp"), 1)
                act.wait_ge(sem("lambda_dots"), 2)
                nc.scalar.activation(lsum[0:1, 2:4], lsum[0:1, 0:2], ACT.Exp).then_inc(sem("lambda_exp"), 1)
                for f in range(KD):
                    act.wait_ge(sem("x_mm"), f + 1)
                    nc.scalar.activation(xT[:, f, :], bank[f % 4][:], ACT.Copy).then_inc(sem("xT_ready"), 1)
                split(0)
                split(1)
                split_h(0, "h_t_ready", h_t)

            def split_h(first, ready, tmp):
                for f in range(KD):
                    act.wait_ge(sem(ready), first + f + 1)
                    nc.scalar.activation(h_hi[:, f, :], tmp[:, f % 2, :], ACT.Copy).then_inc(sem("h_hi_ready"), 1)

            def index():
                u = U0["index"]
                act.wait_ge(mm_done, u + 1)
                act.wait_ge(sem("h_made"), KD)
                nc.scalar.activation(qiT[:, 0, :], bank[0][:], ACT.Copy).then_inc(own.sem, 1)
                nc.scalar.activation(qiT[:, 1, :], bank[1][:], ACT.Copy).then_inc(banks_free, 1)
                own.total += 1
                split(u + 2)
                act.wait_ge(mm_done, u + 2)
                nc.scalar.activation(kiT[:], bank[2][:], ACT.Copy).then_inc(sem("index_ready"), 1)
                act.wait_ge(own.sem, own.total)
                act.wait_ge(sem("index_ready"), 1)
                nc.scalar.activation(wi[:].rearrange("p t n -> p (t n)"), bank[3][:, 0:4 * QT], ACT.Copy
                                     ).then_inc(banks_free, 1)
                act.wait_ge(banks_free, u + 2)
                own.step(nc.scalar.activation(small[:, 8:9], small[:, 4:5], ACT.Copy))
                nc.scalar.activation(small[:, 9:10], small[:, 8:9], ACT.Copy).then_inc(sem("index_ready"), 1)
                split(U0["values"] + 1)

            def values():
                u = U0["values"]
                for n, dst in enumerate((va, vb)):
                    if n:
                        split(u + 2 * n + 1)
                    split(u + 2 * n + 2)
                    act.wait_ge(mm_done, u + 2 * n + 2)
                    for t in range(QT):
                        ins = nc.scalar.activation(dst[:, t, :], bank[t][:], ACT.Copy)
                        if t < QT - 1:
                            own.inc(ins)
                    act.wait_ge(own.sem, own.total)
                    ins.then_inc(banks_free, 2)

            def qk():
                act.wait_ge(sem("logits_added"), QT * H_I)

                def body(i, u, nxt):
                    for slot in range(2):
                        nxt(u, slot + 1)
                        act.wait_ge(mm_done, u + slot + 1)
                        for n in range(2):
                            c = 2 * slot + n
                            nc.scalar.activation(t1[:, n, :], bank[c][:], ACT.Square).then_inc(sem("qk_squares"), 1)
                        act.wait_ge(banks_free, u + slot)
                        for n in range(2):
                            c = 2 * slot + n
                            act.wait_ge(sem("qk_sums"), 4 * i + (c + 1))
                            nc.scalar.activation(t2[:, n, :], bank[4 + n][:], ACT.Sqrt, scale=1.0 / D_A, bias=eps[:]
                                                 ).then_inc(sem("qk_std"), 1)
                ring("qk", 2, body)

            def topk():
                g = 0
                for t in range(QT):
                    w = (t + 1) * P
                    for hh in range(H_I):
                        act.wait_ge(sem("logits_mm"), g + 1)
                        if g >= 2:
                            act.wait_ge(sem("logits_added"), g - 1)
                        nc.scalar.activation(t1[:, g % 2, 0:w], bank[4 + g % 4][:, 0:w], ACT.Relu
                                             ).then_inc(sem("logits_read"), 1)
                        g += 1

            def attn_a():
                act.wait_ge(banks_free, U0["qk"] + 8)
                with act.Fori(0, 2) as i:
                    def exp(n):
                        act.wait_ge(sem("a_max"), 16 * i + (n + 1))
                        w = (n % QT + 1) * P
                        nc.scalar.activation(t1[:, n % 2, 0:w], t1[:, n % 2, 0:w], ACT.Exp, bias=stat[:, n % 8:n % 8 + 1],
                                             accum_out=stat[:, 8 + n % 8:9 + n % 8]).then_inc(sem("a_exp"), 1)

                    def fetch(n):
                        act.wait_ge(sem("a_turned"), 16 * i + (n + 1))
                        act.wait_ge(sem("a_weighed"), 16 * i + max(n - 1, 0))
                        w = (n % QT + 1) * P
                        nc.scalar.activation(t2[:, n % 2, 0:w], bank[6 + n % 2][:, 0:w], ACT.Copy).then_inc(sem("a_pT"), 1)

                    for n in range(16 + 1):
                        if n < 16:
                            exp(n)
                        if n >= 1:
                            fetch(n - 1)

            def attn_b():
                act.wait_ge(sem("a_out"), 32)
                with act.Fori(0, 2) as i:
                    def exp(n):
                        t = n % QT
                        w = (t + 1) * P
                        for m in range(2):
                            act.wait_ge(sem("b_max"), 16 * i + (2 * n + m + 1))
                            p = dist_a[:, 2 * (t % 2) + m, 0:w]
                            nc.scalar.activation(p, p, ACT.Exp, bias=stat[:, 2 * t + m:2 * t + m + 1],
                                                 accum_out=stat[:, 8 + 2 * t + m:9 + 2 * t + m]).then_inc(sem("b_exp"), 1)

                    def fetch(n):
                        t = n % QT
                        act.wait_ge(sem("b_turned"), 8 * i + (n + 1))
                        act.wait_ge(sem("b_weighed"), 8 * i + max(n - 1, 0))
                        w = (t + 1) * P
                        nc.scalar.activation(t2[:, t % 2, 0:w], bank[6 + t % 2][:, 0:w], ACT.Copy).then_inc(sem("b_pT"), 1)

                    def squares(n):
                        head, t = divmod(n, QT)
                        act.wait_ge(sem("b_out"), 8 * i + (n + 1))
                        act.wait_ge(sem("y_b_squares"), 8 * i + n)
                        nc.scalar.activation(t1[:, 0, 0:P], y_b[:, t, ds(2 * P * i + head * P, P)], ACT.Square,
                                             accum_out=stat[:, ds(8 * i + (32 + n), 1)]).then_inc(sem("y_b_squares"), 1)

                    for n in range(2 * QT + 2):
                        if n < 2 * QT:
                            exp(n)
                        if 1 <= n <= 2 * QT:
                            fetch(n - 1)
                        if n >= 2:
                            squares(n - 2)

            def turn_y():
                act.wait_ge(sem("b_out"), 16)
                act.wait_ge(sem("y_b_squares"), 16)
                nc.scalar.activation(stat[:, 0:16], stat[:, 32:48], ACT.Sqrt, scale=1.0 / P, bias=eps[:]
                                     ).then_inc(sem("y_b_std"), 1)
                for f in range(8):
                    act.wait_ge(sem("y_mm"), f + 1)
                    if f < 4:
                        nc.scalar.activation(y_hi[:, f, :], bank[f % 4][:], ACT.Copy).then_inc(sem("y_hi_ready"), 1)
                    else:
                        nc.scalar.activation(y_hi[:, f, :], bank[f % 4][:], ACT.Copy, scale=vcol("subln")
                                             ).then_inc(sem("y_hi_ready"), 1)

            def merge_epi():
                def body(i, u, nxt):
                    nxt(u, 1)
                    act.wait_ge(mm_done, u + 1)
                    act.wait_ge(banks_free, u)
                    own.step(nc.scalar.activation(mt[:, 0, :], bank[0][:], ACT.Sigmoid))
                    nc.scalar.activation(mt[:, 1, :], bank[1][:], ACT.Sigmoid).then_inc(banks_free, 1)
                    nxt(u, 2)
                    act.wait_ge(sem("mixed"), i + 1)
                    nc.scalar.activation(m_hi[:, ds(i, 1), :], mt[:, 2, :], ACT.Copy).then_inc(sem("m_hi_ready"), 1)
                ring("merge", 2, body, 1)

            def out_units(name, q):
                def body(i, u, nxt):
                    for k in range(4):
                        nxt(u, k + 1)
                        if k:
                            act.wait_ge(banks_free, u + k)
                            norm_squares(q, 2 * k - 2, 2 * k)
                        if k == 2 and q == 2:
                            for n in range(2):
                                act.wait_ge(sem("p_mm"), n + 1)
                                nc.scalar.activation(p_hi[:, n, :], bank[5 + n][:], ACT.Copy).then_inc(sem("p_hi_ready"), 1)
                ring(name, 4, body)

            def out1():
                out_units("out1", 0)

            def norm_squares(q, f0, f1):
                for f in range(f0, f1):
                    if f >= 2:
                        act.wait_ge(sem("norm_added"), (KD - 2) * q + f - 1)
                    elif q:
                        act.wait_ge(sem("norm_sums"), q)
                    nc.scalar.activation(nt[:, f % 2, :], xT[:, f, :], ACT.Square).then_inc(sem("norm_squares"), 1)

            def norm(q, early=None, then=None):
                norm_squares(q, KD - 2, KD)
                act.wait_ge(sem("norm_sums"), q + 1)
                nc.scalar.activation(nt[:, 2, :], bank[4][:], ACT.Sqrt, scale=1.0 / D, bias=eps[:]).then_inc(sem("norm_std"), 1)
                if early:
                    early()
                for f in range(KD):
                    act.wait_ge(sem("h_t_ready"), KD * (q + 1) + f + 1)
                    nc.scalar.activation(h_hi[:, f, :], nt[:, 4 + f % 2, :], ACT.Copy).then_inc(sem("h_hi_ready"), 1)
                    if then and f in then:
                        then[f]()

            def norm2():
                act.wait_ge(banks_free, U0["out1"] + 4)
                norm(0)

            def ff():
                at = 0
                for part, n in (("a", 12), ("b", 10)):
                    def epi(i, u, nxt, at=at):
                        for slot in range(2):
                            nxt(u, slot + 1)
                            act.wait_ge(mm_done, u + slot + 1)
                            act.wait_ge(sem("hidden"), 2 * i + (at + slot))
                            nc.scalar.activation(ft[:, 0, :], bank[2 * slot][:], ACT.Sigmoid).then_inc(sem("ff_sigmoid"), 1)
                            act.wait_ge(sem("ff_t_ready"), 2 * i + (at + slot + 1))
                            nc.scalar.activation(g_hi[:, ds(2 * i + slot, 1), :], ft[:, 1, :], ACT.Copy
                                                 ).then_inc(sem("ff_hi_ready"), 1)
                    ring("ff1" + part, 2, epi)
                    at += n
                    if part == "b":
                        sines(2)

                    def down(i, u, nxt):
                        nxt(u, 1)
                        if part == "b" and isinstance(i, int):
                            act.wait_ge(banks_free, u)
                            norm_squares(1, 0, KD - 2)
                        nxt(u, 2)
                    ring("ff2" + part, 2, down)
                    if part == "a":
                        sines(0)

            def sines(at):
                for n in (at, at + 1):
                    act.wait_ge(sem("angles"), n + 1)
                    nc.scalar.activation(trigs[:, n, :], nt[:, 4 + n % 2, :], ACT.Sin).then_inc(sem("trig_ready"), 1)

            def norm_mix():
                act.wait_ge(banks_free, U0["retention"])
                norm(1)

            def retention():
                act.wait_ge(sem("positions_in"), 32)
                act.wait_ge(sem("dtab_ready"), 1)

                def body(i, u, nxt):
                    act.wait_ge(sem("r_decayed"), 4 * i)
                    nc.scalar.activation(etab[:], dtab[:], ACT.Exp, scale=consts[:, ds(i + 2, 1)]).then_inc(sem("r_table"), 1)
                    for k in range(1, 5):
                        nxt(u, k)
                    act.wait_ge(mm_done, u + 4)
                    act.wait_ge(sem("r_o"), 4 * i)
                    act.wait_ge(banks_free, u + 2)
                    for t in range(QT):
                        ins = nc.scalar.activation(rv[:, t, :], bank[t][:], ACT.Copy)
                        if t < QT - 1:
                            own.step(ins)
                    ins.then_inc(banks_free, 2)
                    nxt(u, 5)
                    act.wait_ge(mm_done, u + 5)
                    act.wait_ge(sem("r_gated"), 4 * i)
                    for n in range(2):
                        nc.scalar.activation(sg[:, n, :], bank[n][:], ACT.Sigmoid).then_inc(sem("r_sigmoid"), 1)
                    nxt(u, 6)
                    for vt in range(4):
                        act.wait_ge(sem("r_o"), 4 * i + (vt + 1))
                        act.wait_ge(sem("r_added"), 4 * i + max(vt - 1, 0))
                        nc.scalar.activation(nt[:, vt % 2, :], bank[4 + vt][:], ACT.Square).then_inc(sem("r_squares"), 1)
                    act.wait_ge(sem("r_added"), 4 * i + 4)
                    nc.scalar.activation(nt[:, 2, :], bank[2][:], ACT.Sqrt, scale=1.0 / R_V, bias=eps[:]).then_inc(sem("r_std"), 1)
                    for vt in range(4):
                        if vt == 2:
                            act.wait_ge(mm_done, u + 6)
                            for n in range(2):
                                nc.scalar.activation(sg[:, 2 + n, :], bank[2 + n][:], ACT.Sigmoid).then_inc(sem("r_sigmoid"), 1)
                        act.wait_ge(sem("r_gated"), 4 * i + (vt + 1))
                        nc.scalar.activation(yr_hi[:, vt, :], nt[:, 4 + vt % 2, :], ACT.Copy).then_inc(sem("r_y_hi"), 1)
                    nxt(u, 7)
                    nxt(u, 8)
                ring("retention", 8, body, 3)

            def latent():
                u = U0["latent"]

                def unit(k, tiles, n):
                    act.wait_ge(mm_done, u + k + 1)
                    act.wait_ge(banks_free, u + k)
                    for m, f in enumerate(tiles):
                        ins = nc.scalar.activation(lat_t[:, f, :], bank[2 * (k % 2) + m][:], ACT.Copy)
                        if f != tiles[-1]:
                            own.step(ins)
                    ins.then_inc(banks_free, 1)
                    act.wait_ge(banks_free, u + k + 1)
                    for m, f in enumerate(tiles):
                        nc.scalar.activation(nt[:, n + m, :], lat_t[:, f, :], ACT.Square).then_inc(sem("l_squares"), 1)

                def root(which, added, width):
                    act.wait_ge(sem("l_added"), added)
                    nc.scalar.activation(trigs[:, which, :], bank[4 + which][:], ACT.Sqrt, scale=1.0 / width, bias=eps[:]
                                         ).then_inc(sem("l_std"), 1)

                def rounded(tiles, at):
                    for n, f in enumerate(tiles):
                        act.wait_ge(sem("l_t"), at + n + 1)
                        nc.scalar.activation(lat_hi[:, f, :], lat_tmp[:, (at + n) % 2, :], ACT.Copy).then_inc(sem("l_hi"), 1)

                split(u + 1)
                unit(0, (3, 4), 0)
                split(u + 2)
                unit(1, (0, 1), 2)
                root(0, 2, 256)
                split(u + 3)
                rounded((3, 4), 0)
                unit(2, (2,), 4)
                split(u + 4)
                act.wait_ge(mm_done, u + 4)
                act.wait_ge(banks_free, u + 3)
                nc.scalar.activation(krr[:], bank[2][:], ACT.Copy).then_inc(banks_free, 1)
                act.wait_ge(banks_free, u + 4)
                nc.scalar.activation(nt[:, 5, :], krr[:], ACT.Square).then_inc(sem("l_squares"), 1)
                root(1, 5, 384)
                rounded((0, 1, 2), 2)

            def mla():
                def body(i, u, nxt):
                    nxt(u, 1)
                    act.wait_ge(sem("c_k_mm"), i + 1)
                    act.wait_ge(sem("c_mo"), 2 * i)
                    for n in range(2):
                        nc.scalar.activation(nt[:, 3 + n, :], bank[3 + n][:], ACT.Square).then_inc(sem("c_squares"), 1)
                    act.wait_ge(mm_done, u + 1)
                    for n in range(2):
                        nc.scalar.activation(vv[:, 2 * n:2 * n + 2, :].rearrange("p t c -> p (t c)"), bank[5 + n][:], ACT.Copy
                                             ).then_inc(sem("c_v"), 1)

                    def root(which):
                        act.wait_ge(sem("c_sums_out"), 2 * i + (which + 1))
                        at = 8 * which
                        nc.scalar.activation(stat[:, 16 + at:24 + at], stat[:, at:8 + at], ACT.Sqrt, scale=1.0 / 192,
                                             bias=eps[:]).then_inc(sem("c_std"), 1)

                    root(0)
                    act.wait_ge(sem("c_qr_mm"), i + 1)
                    nc.scalar.activation(qrg, bank[2][:], ACT.Copy, scale=vcol("q_rope")).then_inc(sem("c_qrg"), 1)
                    nc.scalar.activation(nt[:, 2, :], bank[2][:], ACT.Square).then_inc(sem("c_squares"), 1)
                    act.wait_ge(mm_done, u + 2)
                    for n in range(2):
                        nc.scalar.activation(nt[:, n, :], bank[n][:], ACT.Square).then_inc(sem("c_squares"), 1)
                    for hh in range(2):
                        act.wait_ge(sem("c_kinv"), 2 * i + (hh + 1))
                        nc.scalar.activation(nt[:, 3 + hh, :], bank[6 + hh][:], ACT.Copy).then_inc(sem("c_kinv_out"), 1)
                    for n in range(2):
                        nc.scalar.activation(qn[:, n, :], bank[n][:], ACT.Copy, scale=vcol("q_nope")).then_inc(sem("c_qn"), 1)
                    root(1)
                    nxt(u, 2)

                    def exp(n):
                        hh, t = divmod(n, QT)
                        act.wait_ge(sem("c_max"), 8 * i + (n + 1))
                        act.wait_ge(sem("c_turned"), 8 * i + max(n - 1, 0))
                        w = (t + 1) * P
                        nc.scalar.activation(nt[:, n % 2, 0:w], bank[SCORE_BANKS[n % 4]][:, 0:w], ACT.Exp, bias=cst[:, 24 + n:25 + n],
                                             scale=cst[:, 8 + 2 * t + hh:9 + 2 * t + hh], accum_out=cst[:, 32 + n:33 + n]
                                             ).then_inc(sem("c_exp"), 1)

                    def fetch(n):
                        act.wait_ge(sem("c_turned"), 8 * i + (n + 1))
                        act.wait_ge(sem("c_weighed"), 8 * i + max(n - 1, 0))
                        w = (n % QT + 1) * P
                        nc.scalar.activation(nt[:, 2 + n % 2, 0:w], bank[2 + n % 2][:, 0:w], ACT.Copy).then_inc(sem("c_pT"), 1)

                    for n in range(8 + 1):
                        if n < 8:
                            exp(n)
                        if n >= 1:
                            fetch(n - 1)
                    for hh in range(2):
                        act.wait_ge(sem("c_mo_mm"), 2 * i + (hh + 1))
                        nc.scalar.activation(mo_hi[:, ds(2 * i + hh, 1), :], bank[6 + hh][:], ACT.Copy).then_inc(sem("c_mo_hi"), 1)
                ring("mla", 2, body)

            def merge2_epi():
                def body(i, u, nxt):
                    nxt(u, 1)
                    act.wait_ge(mm_done, u + 1)
                    act.wait_ge(banks_free, u)
                    act.wait_ge(sem("merged2"), i)
                    own.step(nc.scalar.activation(nt[:, 0, :], bank[0][:], ACT.Sigmoid))
                    nc.scalar.activation(nt[:, 1, :], bank[1][:], ACT.Sigmoid).then_inc(banks_free, 1)
                    nxt(u, 2)
                    act.wait_ge(sem("mixed2"), i + 1)
                    nc.scalar.activation(m2_hi[:, ds(i, 1), :], nt[:, 2, :], ACT.Copy).then_inc(sem("m2_hi_ready"), 1)
                ring("merge2", 2, body, 1)

            def out2():
                out_units("out2", 2)

            def mlp():
                u = U0["ple_in"]

                def copies(half):
                    act.wait_ge(mm_done, u + half + 1)
                    for n in range(4):
                        if n == 3:
                            act.wait_ge(sem("p_copied"), 3 * half + 3)
                        nc.scalar.activation(aret[:, 4 * half + n, :], bank[n][:], ACT.Copy
                                             ).then_inc(sem("p_copied") if n < 3 else banks_free, 1)

                split(u + 1)
                act.wait_ge(banks_free, u)
                norm(2, lambda: copies(0), {1: lambda: split(u + 2), 3: lambda: copies(1)})

                def body(i, u, nxt):
                    for k in range(4):
                        nxt(u, k + 1)
                        act.wait_ge(mm_done, u + k + 1)
                        act.wait_ge(banks_free, u + k)
                        for n in range(2):
                            act.wait_ge(sem("mlp_squared"), 8 * i + max(2 * k + n - 1, 0))
                            ins = nc.scalar.activation(nt[:, n, :], bank[2 * (k % 2) + n][:], ACT.Relu)
                            ins.then_inc(sem("mlp_relu"), 1)
                        act.wait_ge(sem("mlp_relu"), 8 * i + (2 * k + 2))
                        own.step(nc.scalar.activation(small[:, 20:21], eps[:], ACT.Copy))
                        nc.scalar.activation(small[:, 21:22], eps[:], ACT.Copy).then_inc(banks_free, 1)
                        for n in range(2):
                            act.wait_ge(sem("mlp_squared"), 8 * i + (2 * k + n + 1))
                            nc.scalar.activation(u_hi[:, 2 * k + n, :], nt[:, 4 + n, :], ACT.Copy).then_inc(sem("mlp_hi"), 1)
                    for k in range(4, 8):
                        nxt(u, k + 1)
                        if k > 4 and isinstance(i, int):
                            act.wait_ge(banks_free, u + k)
                            norm_squares(3, 2 * k - 10, 2 * k - 8)
                ring("mlp", 8, body, 4)

            def ple():
                act.wait_ge(banks_free, U0["ple"])
                norm(3)
                def body(i, u, nxt):
                    for slot in range(2):
                        nxt(u, slot + 1)
                        act.wait_ge(mm_done, u + slot + 1)
                        act.wait_ge(sem("x_done"), 4 * i)
                        own.step(nc.scalar.activation(nt[:, 2 * slot, :], bank[2 * slot][:], ACT.Sigmoid))
                        nc.scalar.activation(nt[:, 2 * slot + 1, :], bank[2 * slot + 1][:], ACT.Sigmoid).then_inc(banks_free, 1)
                ring("ple", 2, body, 2)
                for t in range(QT):
                    act.wait_ge(sem("out_mm"), t + 1)
                    nc.scalar.activation(out_sb[:, t, 0:512], bank[4 + t][:], ACT.Copy).then_inc(sem("out_left"), 1)
                for t in range(0, QT, 2):
                    act.wait_ge(sem("out_mm"), QT + t + 1)
                    nc.scalar.activation(out_sb[:, t, 512:D], bank[4 + t][:], ACT.Copy).then_inc(sem("out_even"), 1)

            prologue()
            index()
            topk()
            values()
            qk()
            attn_a()
            attn_b()
            turn_y()
            merge_epi()
            out1()
            norm2()
            ff()
            norm_mix()
            retention()
            latent()
            mla()
            merge2_epi()
            out2()
            mlp()
            ple()

        @block.vector
        def _(dve):
            own = Count(dve, sem("dve_steps"))
            v = nc.vector

            def split(u, slot=None, width=None):
                if isinstance(u, int):
                    if u >= len(WIDTH):
                        return
                    slot, width = u % 2, WIDTH[u]
                dve.wait_ge(hi_done, u + 1)
                v.tensor_tensor(w_lo[:, slot, 0:width], raw[:, slot, 0:width],
                                w_hi[:, slot, 0:width].bitcast(F32), ALU.subtract).then_inc(lo_done, 1)

            def ring(name, per, body, count=0):
                u0, n = U0[name], len(dict(STAGES)[name]) // per
                widths = WIDTH[u0:u0 + per]
                if n > 1:
                    with dve.Fori(0, n - 1) as i:
                        own.enter(i, count)
                        body(i, u0 + per * i, lambda u, k: split(u + k, k % 2, (widths + widths[:1])[k]))
                    own.leave(n - 1)
                body(n - 1, u0 + per * (n - 1), lambda u, k: split(u + k))

            def prologue():
                v.memset(eps[:], EPS).then_inc(sem("eps_ready"), 1)
                dve.wait_ge(sem("x_std"), 1)
                own.step(v.reciprocal(small[:, 0:4], small[:, 4:8]))
                for t in range(QT):
                    v.tensor_scalar(x_n[:, t, :], x_in[:, t, :], small[:, t:t + 1], None, ALU.mult
                                    ).then_inc(sem("x_n_ready"), 1)
                dve.wait_ge(sem("vectors_in"), 16 * 17)
                for n in range(2):
                    own.step(v.tensor_tensor(vrows_l(n), lrow[0:1, 128 * n:128 * n + 64],
                                             lrow[0:1, 128 * n + 64:128 * n + 128], ALU.mult))
                    v.reduce_sum(lsum[0:1, n:n + 1], vrows_l(n), axis=AX).then_inc(sem("lambda_dots"), 1)
                dve.wait_ge(sem("silu_exp"), 1)
                own.step(v.tensor_scalar(cs[:, KD:2 * KD], cs[:, 0:KD], 1.0, None, ALU.add))
                own.step(v.reciprocal(cs[:, 0:KD], cs[:, KD:2 * KD]))
                own.step(v.tensor_tensor(cs[:, 2 * KD:3 * KD], cs[:, 0:KD], vT[:, 0:KD], ALU.mult))
                dve.wait_ge(sem("lambda_exp"), 1)
                own.step(v.tensor_tensor(lsum[0:1, 5:6], lsum[0:1, 2:3], lsum[0:1, 3:4], ALU.subtract))
                v.tensor_scalar(lsum[0:1, 4:5], lsum[0:1, 5:6], LAMBDA_INIT, None, ALU.add
                                ).then_inc(sem("lambda_sum"), 1)
                for k, w in enumerate(ada_in1):
                    dve.wait_ge(sem(f"ada_in{k}"), 16)
                    scale = cs[:, 2 * KD + k:2 * KD + k + 1]
                    if k == 0:
                        ins = v.tensor_scalar(ada[:], w, scale, None, ALU.mult)
                    else:
                        dve.wait_ge(sem("ada_free"), k)
                        ins = v.scalar_tensor_tensor(ada[:], w, scale, ada[:], ALU.mult, ALU.add)
                    ins.then_inc(sem("ada_free"), 1)
                split(0)
                split(1)
                dve.wait_ge(sem("lambda_mm"), 1)
                own.step(v.tensor_scalar(minus_lam[:], bank[5][:, 0:1], -1.0, None, ALU.mult))
                make_h1()
                v.tensor_scalar(vT[:, VROWS["qn_a"]:VROWS["qn_a"] + 1], vcol("qn_a"), D_A ** -0.5, None, ALU.mult
                                ).then_inc(own.sem, 1)
                own.total += 1
                v.tensor_scalar(vT[:, VROWS["qn_b"]:VROWS["qn_b"] + 1], vcol("qn_b"), D_A ** -0.5, None, ALU.mult
                                ).then_inc(own.sem, 1)
                own.total += 1
                own.step(v.tensor_scalar(vT[:, VROWS["subln"]:VROWS["subln"] + 1], vcol("subln"), 1.0 - LAMBDA_INIT,
                                         None, ALU.mult))

            def vrows_l(n):
                return h_t[0:1, n, 0:64]

            def make_h1():
                dve.wait_ge(sem("ada_mm"), 1)
                own.step(v.tensor_tensor(modc[:, 0:16], bank[6][:, 0:16], vT[:, VROWS["b_ada"]:VROWS["b_ada"] + 16], ALU.add))
                own.step(v.tensor_scalar(gs1[:], SC1, 1.0, None, ALU.add))
                own.step(v.tensor_tensor(gs1[:], gs1[:], vT[:, VROWS["norm1_g"]:VROWS["norm1_g"] + KD], ALU.mult))
                for f in range(KD):
                    dve.wait_ge(sem("x_mm"), KD + f + 1)
                    if f >= 2:
                        dve.wait_ge(sem("h_made"), f - 1)
                    v.tensor_scalar(h_t[:, f % 2, :], bank[f % 4][:], gs1[:, f:f + 1], modc[:, f:f + 1],
                                    ALU.mult, ALU.add).then_inc(sem("h_t_ready"), 1)
                    if f:
                        h_rest(0, f - 1, h_t)
                h_rest(0, KD - 1, h_t)

            def h_rest(first, f, tmp):
                dve.wait_ge(sem("h_hi_ready"), first + f + 1)
                v.tensor_tensor(h_lo[:, f, :], tmp[:, f % 2, :], h_hi[:, f, :].bitcast(F32), ALU.subtract
                                ).then_inc(sem("h_made"), 1)

            def index():
                split(U0["index"] + 2)
                split(U0["values"] + 1)

            def values():
                u = U0["values"]
                index_scores()
                rounds(1, 16)
                split(u + 2)
                rounds(2, 8)
                split(u + 3)
                rounds(2, 8)
                split(u + 4)
                rounds(3, TOPK // 8 - 12)
                dve.wait_ge(sem("dist_ready"), QT)
                own.step(v.tensor_copy(dist_a[:, 0, 0:P], dist_b[:, 0, 0:P]))
                selected(1)
                selected(2)

            def qk():
                def body(i, u, nxt):
                    for slot in range(2):
                        nxt(u, slot + 1)
                        if not isinstance(i, int):
                            rounds(3, 2)
                        for n, (dst, g) in enumerate((((qaT, "qn_a"), (kaT, "kn_a")), ((qbT, "qn_b"), (kbT, "kn_b")))[slot]):
                            c = 2 * slot + n
                            dve.wait_ge(sem("qk_std"), 4 * i + (c + 1))
                            own.step(v.reciprocal(t3[:, n, :], t2[:, n, :]))
                            ins = v.scalar_tensor_tensor(dst[:, ds(i, 1), :], bank[c][:], vcol(g), t3[:, n, :],
                                                         ALU.mult, ALU.mult)
                            if n == 0:
                                own.step(ins)
                        ins.then_inc(banks_free, 1)
                ring("qk", 2, body, 14)

            def index_scores():
                dve.wait_ge(sem("index_ready"), 2)
                g = 0
                for t in range(QT):
                    w = (t + 1) * P
                    for hh in range(H_I):
                        dve.wait_ge(sem("logits_read"), g + 1)
                        if hh == 0:
                            ins = v.tensor_scalar(dist_a[:, t, 0:w], t1[:, g % 2, 0:w], wi[:, t, 0:1], None, ALU.mult)
                        else:
                            ins = v.scalar_tensor_tensor(dist_a[:, t, 0:w], t1[:, g % 2, 0:w], wi[:, t, hh:hh + 1],
                                                         dist_a[:, t, 0:w], ALU.mult, ALU.add)
                        ins.then_inc(sem("logits_added"), 1)
                        g += 1
                        dve.wait_ge(sem("logits_added"), g)
                    own.step(v.memset(dist_a[0:64, t, w - 64:w], INADMISSIBLE))

            def rounds(t, n):
                w = (t + 1) * P
                for _ in range(n):
                    if own.loop:
                        dve.sem_inc(sem("rounds_seen"), 1)
                    own.step(v.max(top8[:], dist_a[:, t, 0:w]))
                    if own.loop:
                        dve.sem_inc(sem("rounds_seen"), 1)
                    own.step(v.match_replace(out=dist_a[:, t, 0:w], in_to_replace=top8[:], in_values=dist_a[:, t, 0:w],
                                             imm_value=TAKEN))

            def selected(t):
                w = (t + 1) * P
                own.step(v.tensor_scalar(dist_a[:, t, 0:w], dist_a[:, t, 0:w], TAKEN, FAR, ALU.is_gt, ALU.mult))
                own.step(v.tensor_tensor(dist_a[:, t, 0:w], dist_a[:, t, 0:w], dist_b[:, t, 0:w], ALU.add))

            def topk():
                selected(3)

            def attn_a():
                with dve.Fori(0, 2) as i:
                    own.enter(i, 16)

                    def bias(n):
                        head, t = divmod(n, QT)
                        w = (t + 1) * P
                        dve.wait_ge(sem("a_scores"), 16 * i + (n + 1))
                        dve.wait_ge(sem("a_turned"), 16 * i + max(n - 1, 0))
                        v.scalar_tensor_tensor(t1[:, n % 2, 0:w], dist_a[:, t, 0:w], slope[:, ds(4 * i + head, 1)],
                                               bank[2 + n % 4][:, 0:w], ALU.mult, ALU.add).then_inc(sem("a_biased"), 1)
                        dve.wait_ge(sem("a_biased"), 16 * i + (n + 1))
                        v.tensor_reduce(stat[:, n % 8:n % 8 + 1], t1[:, n % 2, 0:w], axis=AX, op=ALU.max, negate=True
                                        ).then_inc(sem("a_max"), 1)

                    def out_(n):
                        head, t = divmod(n, QT)
                        dve.wait_ge(sem("a_exp"), 16 * i + (n + 1))
                        own.step(v.reciprocal(stat[:, 16 + n % 8:17 + n % 8], stat[:, 8 + n % 8:9 + n % 8]))
                        dve.wait_ge(sem("a_weighed"), 16 * i + (n + 1))
                        v.tensor_scalar(y_a[:, t, ds(2 * P * i + head * D_A, D_A)], bank[n % 2][:, 0:D_A],
                                        stat[:, 16 + n % 8:17 + n % 8], None, ALU.mult).then_inc(sem("a_out"), 1)

                    for n in range(16 + 2):
                        if n < 16:
                            bias(n)
                        if n >= 2:
                            out_(n - 2)
                own.leave(2)

            def attn_b():
                with dve.Fori(0, 2) as i:
                    own.enter(i, 16)

                    def bias(k):
                        head, t = divmod(k, QT)
                        w = (t + 1) * P
                        for m in range(2):
                            n = 2 * t + m
                            dve.wait_ge(sem("b_scores"), 16 * i + (2 * k + m + 1))
                            dve.wait_ge(sem("b_turned"), 8 * i + max(k - 1, 0))
                            p = dist_a[:, 2 * (t % 2) + m, 0:w]
                            v.scalar_tensor_tensor(p, dist_b[:, t, 0:w], slope[:, ds(2 * i + (H_A + head), 1)],
                                                   bank[2 + 2 * (t % 2) + m][:, 0:w], ALU.mult, ALU.add
                                                   ).then_inc(sem("b_biased"), 1)
                            dve.wait_ge(sem("b_biased"), 16 * i + (2 * k + m + 1))
                            v.tensor_reduce(stat[:, n:n + 1], p, axis=AX, op=ALU.max, negate=True
                                            ).then_inc(sem("b_max"), 1)

                    def mix(k):
                        t = k % QT
                        w = (t + 1) * P
                        c = 16 + 2 * t
                        dve.wait_ge(sem("b_exp"), 16 * i + (2 * k + 2))
                        own.step(v.reciprocal(stat[:, c:c + 2], stat[:, c - 8:c - 6]))
                        own.step(v.scalar_tensor_tensor(stat[:, 24 + t:25 + t], stat[:, c + 1:c + 2], minus_lam[:],
                                                        stat[:, c - 8:c - 7], ALU.mult, ALU.mult))
                        p0, p1 = (dist_a[:, 2 * (t % 2) + m, 0:w] for m in range(2))
                        v.scalar_tensor_tensor(p0, p1, stat[:, 24 + t:25 + t], p0, ALU.mult, ALU.add
                                               ).then_inc(sem("b_mixed"), 1)

                    def out_(k):
                        head, t = divmod(k, QT)
                        dve.wait_ge(sem("b_weighed"), 8 * i + (k + 1))
                        v.tensor_scalar(y_b[:, t, ds(2 * P * i + head * P, P)], bank[t % 2][:, 0:P],
                                        stat[:, 16 + 2 * t:17 + 2 * t], None, ALU.mult).then_inc(sem("b_out"), 1)

                    for n in range(2 * QT + 2):
                        if n < 2 * QT:
                            bias(n)
                        if 0 <= n - 1 < 2 * QT:
                            mix(n - 1)
                        if n >= 2:
                            out_(n - 2)
                own.leave(2)

            def turn_y():
                dve.wait_ge(sem("y_b_std"), 1)
                own.step(v.reciprocal(stat[:, 16:32], stat[:, 0:16]))
                for n in range(16):
                    blk = y_b[:, n % 4, (n // 4) * P:(n // 4) * P + P]
                    v.tensor_scalar(blk, blk, stat[:, 16 + n:17 + n], None, ALU.mult).then_inc(sem("y_b_scaled"), 1)
                for f in range(8):
                    dve.wait_ge(sem("y_hi_ready"), f + 1)
                    if f < 4:
                        ins = v.tensor_tensor(y_lo[:, f, :], bank[f % 4][:], y_hi[:, f, :].bitcast(F32), ALU.subtract)
                    else:
                        ins = v.scalar_tensor_tensor(y_lo[:, f, :], bank[f % 4][:], vcol("subln"), y_hi[:, f, :].bitcast(F32),
                                                     ALU.mult, ALU.subtract)
                    ins.then_inc(sem("y_made"), 1)

            def merge_epi():
                dve.wait_ge(sem("ada_clear"), 1)

                def body(i, u, nxt):
                    for n in range(2):
                        nxt(u, n + 1)
                        dve.wait_ge(sem(f"ada_in{n}"), 16 * i + 32)
                        dve.wait_ge(sem("ada_free"), 2 * i + (KD - 1 + n))
                        v.scalar_tensor_tensor(ada2[:, n, :], ada_in2[n], cs[:, ds(i + 2 * KD, 1)], ada2[:, n, :],
                                               ALU.mult, ALU.add).then_inc(sem("ada_free"), 1)
                    dve.wait_ge(mm_done, u + 2)
                    dve.wait_ge(banks_free, u + 1)
                    own.step(v.tensor_tensor(mt[:, 0, :], bank[2][:], mt[:, 0, :], ALU.mult))
                    own.step(v.tensor_tensor(mt[:, 1, :], bank[3][:], mt[:, 1, :], ALU.mult))
                    v.tensor_tensor(mt[:, 2, :], mt[:, 0, :], mt[:, 1, :], ALU.add).then_inc(sem("mixed"), 1)
                    v.memset(small[:, 18:19], 0.0).then_inc(banks_free, 1)
                    dve.wait_ge(sem("m_hi_ready"), i + 1)
                    v.tensor_tensor(m_lo[:, ds(i, 1), :], mt[:, ds(2, 1), :], m_hi[:, ds(i, 1), :].bitcast(F32), ALU.subtract
                                    ).then_inc(sem("merged"), 1)
                ring("merge", 2, body, 2)

            def add_gated(i, u, nxt, gate, per_unit):
                for slot in range(2):
                    nxt(u, slot + 1)
                    dve.wait_ge(mm_done, u + slot + 1)
                    for n in range(per_unit):
                        f = ds(2 * per_unit * i + (per_unit * slot + n), 1)
                        ins = v.scalar_tensor_tensor(xT[:, f, :], bank[2 * slot + n][:], gate[:, f], xT[:, f, :],
                                                     ALU.mult, ALU.add)
                        if n < per_unit - 1:
                            own.step(ins)
                    ins.then_inc(banks_free, 1)

            def modulation(b, tiles, count):
                dve.wait_ge(sem("ada_mm"), count)
                lo, hi = tiles[0], tiles[-1] + 1
                at = VROWS["b_ada"]
                own.step(v.tensor_tensor(modc[:, lo:hi], bank[b][:, lo - 2 * KD:hi - 2 * KD], vT[:, at + lo:at + hi], ALU.add))

            def out1():
                modulation(5, range(2 * KD, 3 * KD), 2)
                ring("out1", 2, lambda i, u, nxt: add_gated(i, u, nxt, GT1, 2), 2)

            def norm(q, gains, shift=None, then=None):
                dve.wait_ge(sem("norm_std"), q + 1)
                own.step(v.reciprocal(nt[:, 3, :], nt[:, 2, :]))
                norm_tiles(q, gains, shift, then)

            def norm_tiles(q, gains, shift=None, then=None):
                for f in range(KD):
                    if f >= 2:
                        dve.wait_ge(sem("h_made"), KD * (q + 1) + f - 1)
                    ins = v.scalar_tensor_tensor(nt[:, 4 + f % 2, :], xT[:, f, :], gains[:, f:f + 1], nt[:, 3, :],
                                                 ALU.mult, ALU.mult)
                    if shift is not None:
                        own.step(ins)
                        ins = v.tensor_scalar(nt[:, 4 + f % 2, :], nt[:, 4 + f % 2, :], shift[:, f:f + 1], None, ALU.add)
                    ins.then_inc(sem("h_t_ready"), 1)
                    if f:
                        rest(q, f - 1)
                    if then and f in then:
                        then[f]()
                rest(q, KD - 1)

            def rest(q, f):
                dve.wait_ge(sem("h_hi_ready"), KD * (q + 1) + f + 1)
                v.tensor_tensor(h_lo[:, f, :], nt[:, 4 + f % 2, :], h_hi[:, f, :].bitcast(F32), ALU.subtract
                                ).then_inc(sem("h_made"), 1)

            def norm2():
                dve.wait_ge(sem("norm_std"), 1)
                own.step(v.reciprocal(nt[:, 3, :], nt[:, 2, :]))
                modulation(6, range(3 * KD, 5 * KD), 3)
                own.step(v.tensor_scalar(gs2[:], SC2, 1.0, None, ALU.add))
                own.step(v.tensor_tensor(gs2[:], gs2[:], vT[:, VROWS["norm2_g"]:VROWS["norm2_g"] + KD], ALU.mult))
                norm_tiles(0, gs2, SH2)
                modulation(7, range(5 * KD, 6 * KD), 4)

            def ff():
                at = 0
                for part, n in (("a", 12), ("b", 10)):
                    def epi(i, u, nxt, at=at):
                        for slot in range(2):
                            nxt(u, slot + 1)
                            dve.wait_ge(sem("ff_sigmoid"), 2 * i + (at + slot + 1))
                            own.step(v.tensor_tensor(ft[:, 2, :], bank[2 * slot][:], ft[:, 0, :], ALU.mult))
                            v.tensor_tensor(ft[:, 1, :], bank[2 * slot + 1][:], ft[:, 2, :], ALU.mult
                                            ).then_inc(sem("ff_t_ready"), 1)
                            dve.wait_ge(sem("ff_t_ready"), 2 * i + (at + slot + 1))
                            v.memset(small[:, 19:20], 0.0).then_inc(banks_free, 1)
                            dve.wait_ge(sem("ff_hi_ready"), 2 * i + (at + slot + 1))
                            v.tensor_tensor(g_lo[:, ds(2 * i + slot, 1), :], ft[:, ds(1, 1), :],
                                            g_hi[:, ds(2 * i + slot, 1), :].bitcast(F32), ALU.subtract).then_inc(sem("hidden"), 1)
                    ring("ff1" + part, 2, epi, 2)
                    at += n
                    if part == "a":
                        angles(0)
                    ring("ff2" + part, 2, lambda i, u, nxt: add_gated(i, u, nxt, GT2, 1))
                    if part == "a":
                        angles(1)

            def angles(s):
                two_pi = 2.0 * math.pi
                c1 = 6.28125
                c2 = float(np.float32(two_pi - c1).view(np.uint32).__and__(np.uint32(0xFFFFF000)).view(np.float32))
                c3 = two_pi - c1 - c2
                magic = 1.5 * 2.0 ** 23
                edge = float(np.nextafter(np.float32(math.pi), np.float32(0)))
                dve.wait_ge(sem("positions_in"), 32)
                a, k, x, y = (nt[:, n, :] for n in range(4))
                own.step(v.tensor_copy(a, pos_i[:]))
                own.step(v.tensor_scalar(a, a, consts[:, s:s + 1], None, ALU.mult))
                own.step(v.tensor_scalar(k, a, 1.0 / two_pi, magic, ALU.mult, ALU.add))
                own.step(v.tensor_scalar(k, k, magic, None, ALU.subtract))
                own.step(v.scalar_tensor_tensor(x, k, -c1, a, ALU.mult, ALU.add))
                own.step(v.scalar_tensor_tensor(x, k, -c2, x, ALU.mult, ALU.add))
                own.step(v.scalar_tensor_tensor(x, k, -c3, x, ALU.mult, ALU.add))
                own.step(v.tensor_scalar(y, x, math.pi / 2, None, ALU.add))
                own.step(v.tensor_scalar(k, y, math.pi, -two_pi, ALU.is_gt, ALU.mult))
                own.step(v.tensor_tensor(y, y, k, ALU.add))
                if s:
                    dve.wait_ge(sem("trig_ready"), 2)
                v.tensor_scalar(nt[:, 4, :], y, edge, -edge, ALU.min, ALU.max).then_inc(sem("angles"), 1)
                v.tensor_scalar(nt[:, 5, :], x, edge, -edge, ALU.min, ALU.max).then_inc(sem("angles"), 1)

            def norm_mix():
                norm(1, vT[:, VROWS["norm_mix"]:VROWS["norm_mix"] + KD])

            def rope_tile(dst, x1, x2, cos, sin):
                own.step(v.tensor_tensor(rt[:, 0, :], x1, cos, ALU.mult))
                own.step(v.tensor_tensor(rt[:, 1, :], x2, sin, ALU.mult))
                own.step(v.tensor_tensor(rt[:, 2, :], x2, cos, ALU.mult))
                own.step(v.tensor_tensor(rt[:, 3, :], x1, sin, ALU.mult))
                v.tensor_tensor(dst[:, 0, :], rt[:, 0, :], rt[:, 1, :], ALU.subtract).then_inc(banks_free, 1)
                v.tensor_tensor(dst[:, 1, :], rt[:, 2, :], rt[:, 3, :], ALU.add).then_inc(sem("r_rope"), 1)

            def retention():
                cos, sin = trigs[:, 0, :], trigs[:, 1, :]
                dve.wait_ge(sem("aret_clear"), 1)

                def body(i, u, nxt):
                    for k, dst in enumerate((rqT, rkT)):
                        nxt(u, k + 1)
                        dve.wait_ge(mm_done, u + k + 1)
                        dve.wait_ge(sem("r_scores"), 4 * i)
                        rope_tile(dst, bank[2 * k][:], bank[2 * k + 1][:], cos, sin)
                        dve.wait_ge(sem("r_rope"), 2 * i + (k + 1))
                        dve.wait_ge(banks_free, u + k + 1)
                    nxt(u, 3)
                    nxt(u, 4)
                    dve.wait_ge(sem("r_table"), i + 1)
                    for j in range(QT):
                        dve.wait_ge(sem("r_scores"), 4 * i + (j + 1))
                        w = S - j * P
                        v.scalar_tensor_tensor(rs_t[:, j, 0:w], bank[4 + j][:, 0:w], R_QK ** -0.5, etab[:, 0:w],
                                               ALU.mult, ALU.mult).then_inc(sem("r_decayed"), 1)
                    nxt(u, 5)
                    dve.wait_ge(banks_free, u + 4)
                    for n in range(2):
                        dve.wait_ge(sem("r_sigmoid"), 4 * i + (n + 1))
                        ins = v.tensor_tensor(sg[:, n, :], bank[n][:], sg[:, n, :], ALU.mult)
                        if n == 0:
                            own.step(ins)
                    ins.then_inc(banks_free, 1)
                    nxt(u, 6)
                    dve.wait_ge(sem("r_squares"), 4 * i + 4)
                    for vt in range(2):
                        gate_tile(i, vt)
                    dve.wait_ge(sem("r_std"), i + 1)
                    own.step(v.reciprocal(nt[:, 3, :], nt[:, 2, :]))
                    for vt in range(2):
                        v.tensor_tensor(nt[:, 4 + vt, :], rt[:, vt, :], nt[:, 3, :], ALU.mult).then_inc(sem("r_gated"), 1)
                    y_lo_tile(i, 0)
                    y_lo_tile(i, 1)
                    for vt in range(2, 4):
                        own.step(v.scalar_tensor_tensor(rt[:, vt, :], bank[4 + vt][:],
                                                        vT[:, ds(4 * i + (VROWS["ret_norm"] + vt), 1)], nt[:, 3, :],
                                                        ALU.mult, ALU.mult))
                    for vt in range(2, 4):
                        dve.wait_ge(sem("r_sigmoid"), 4 * i + (vt + 1))
                        own.step(v.tensor_tensor(sg[:, vt, :], bank[vt][:], sg[:, vt, :], ALU.mult))
                        v.tensor_tensor(nt[:, 2 + vt, :], rt[:, vt, :], sg[:, vt, :], ALU.mult).then_inc(sem("r_gated"), 1)
                    v.memset(small[:, 24:25], 0.0).then_inc(banks_free, 1)
                    dve.wait_ge(banks_free, u + 6)
                    y_lo_tile(i, 2)
                    y_lo_tile(i, 3)
                    nxt(u, 7)
                    for half in range(2):
                        dve.wait_ge(mm_done, u + (7 + half))
                        for n in range(4):
                            f = 4 * half + n
                            ins = v.tensor_tensor(aret[:, f, :], bank[f][:], aret[:, f, :], ALU.add)
                            if n < 3:
                                own.step(ins)
                        ins.then_inc(banks_free, 1)
                        if half == 0:
                            nxt(u, 8)
                    if not isinstance(i, int):
                        dve.wait_ge(banks_free, u + 8)

                def gate_tile(i, vt):
                    own.step(v.scalar_tensor_tensor(rt[:, vt, :], bank[4 + vt][:],
                                                    vT[:, ds(4 * i + (VROWS["ret_norm"] + vt), 1)], sg[:, vt, :],
                                                    ALU.mult, ALU.mult))

                def y_lo_tile(i, vt):
                    dve.wait_ge(sem("r_y_hi"), 4 * i + (vt + 1))
                    v.tensor_tensor(yr_lo[:, vt, :], nt[:, 4 + vt % 2, :], yr_hi[:, vt, :].bitcast(F32), ALU.subtract
                                    ).then_inc(sem("r_y"), 1)
                    dve.wait_ge(sem("r_y"), 4 * i + (vt + 1))
                ring("retention", 8, body, 22)

            def latent():
                u = U0["latent"]
                for k in range(3):
                    split(u + k + 1)

                def scaled(tiles, at, which):
                    dve.wait_ge(sem("l_std"), which + 1)
                    own.step(v.reciprocal(trigs[:, which, :], trigs[:, which, :]))
                    for n, f in enumerate(tiles):
                        if n >= 2:
                            rest(tiles[n - 2], at + n - 2)
                        name, g = ("q_lat", f) if f < 3 else ("kv_lat", f - 3)
                        v.scalar_tensor_tensor(lat_tmp[:, (at + n) % 2, :], lat_t[:, f, :], vcol(name, g),
                                               trigs[:, which, :], ALU.mult, ALU.mult).then_inc(sem("l_t"), 1)
                    for n in range(len(tiles) - 2, len(tiles)):
                        rest(tiles[n], at + n)

                def rest(f, n):
                    dve.wait_ge(sem("l_hi"), n + 1)
                    v.tensor_tensor(lat_lo[:, f, :], lat_tmp[:, n % 2, :], lat_hi[:, f, :].bitcast(F32), ALU.subtract
                                    ).then_inc(sem("l_made"), 1)
                    dve.wait_ge(sem("l_made"), n + 1)

                scaled((3, 4), 0, 0)
                split(u + 4)
                dve.wait_ge(banks_free, u + 4)
                v.tensor_scalar(krT, krr[:], vcol("k_rope"), None, ALU.mult).then_inc(sem("l_kr"), 1)
                dve.wait_ge(sem("l_added"), 6)
                v.tensor_copy(stat[:, 32:36], bank[6][:, 0:4]).then_inc(sem("l_kr_sums"), 1)
                scaled((0, 1, 2), 2, 1)
                dve.wait_ge(sem("l_kr_sums"), 1)
                dve.wait_ge(sem("l_turned"), 1)
                own.step(v.tensor_tensor(lat_tmp[:, 0, :], bank[7][:], trigs[:, 3, :], ALU.mult))
                own.step(v.tensor_tensor(lat_tmp[:, 1, :], krT, trigs[:, 2, :], ALU.mult))
                v.tensor_tensor(krr[:], lat_tmp[:, 0, :], lat_tmp[:, 1, :], ALU.add).then_inc(sem("l_krr"), 1)
                dve.wait_ge(sem("l_krr"), 1)

            def mla():
                for hh in range(2):
                    own.step(v.memset(kr2[64 - 64 * hh:128 - 64 * hh, hh, :], 0.0))

                def body(i, u, nxt):
                    nxt(u, 1)
                    dve.wait_ge(sem("c_sums"), 2 * i + 1)
                    own.step(v.tensor_copy(stat[:, 0:8], bank[7][:, 0:8]))
                    by = stat[:, 0:8].rearrange("p (t c) -> p c t", c=2)
                    own.step(v.tensor_tensor(by[:, 0, :], by[:, 0, :], stat[:, 32:36], ALU.add))
                    v.tensor_tensor(by[:, 1, :], by[:, 1, :], stat[:, 32:36], ALU.add).then_inc(sem("c_sums_out"), 1)
                    dve.wait_ge(sem("c_std"), 2 * i + 1)
                    own.step(v.reciprocal(cst[:, 0:8], stat[:, 16:24]))
                    for hh in range(2):
                        for t in range(QT):
                            if t == QT - 1:
                                own.settle()
                            ins = v.tensor_scalar(kw[:, 4 * hh + t, :], ones[:], cst[:, 2 * t + hh:2 * t + hh + 1], None, ALU.mult)
                            if t < QT - 1:
                                own.inc(ins)
                        ins.then_inc(sem("c_wide"), 1)
                    dve.wait_ge(sem("c_turned_q"), i + 1)
                    own.step(v.tensor_tensor(qr[:], bank[5][:], trigs[:, 3, :], ALU.mult))
                    own.step(v.tensor_tensor(qrg, qrg, trigs[:, 2, :], ALU.mult))
                    own.step(v.tensor_tensor(qr[:], qr[:], qrg, ALU.add))
                    for hh in range(2):
                        lo = 64 * hh
                        dve.wait_ge(sem("c_kinv_out"), 2 * i + (hh + 1))
                        own.step(v.scalar_tensor_tensor(kn[:, hh, :], bank[3 + hh][:], vcol("k_nope"), nt[:, 3 + hh, :],
                                                        ALU.mult, ALU.mult))
                        own.step(v.tensor_tensor(kr2[lo:lo + 64, hh, :], krr[lo:lo + 64, :], nt[lo:lo + 64, 3 + hh, :], ALU.mult))
                    dve.wait_ge(sem("c_qn"), 2 * i + 2)
                    v.memset(small[:, 22:23], 0.0).then_inc(banks_free, 2)
                    dve.wait_ge(sem("c_sums"), 2 * i + 2)
                    v.tensor_copy(stat[:, 8:16], bank[2][:, 0:8]).then_inc(sem("c_sums_out"), 1)
                    dve.wait_ge(sem("c_std"), 2 * i + 2)
                    own.step(v.reciprocal(cst[:, 8:16], stat[:, 24:32]))
                    own.step(v.tensor_scalar(cst[:, 8:16], cst[:, 8:16], 192.0 ** -0.5, None, ALU.mult))
                    nxt(u, 2)

                    def peak(n):
                        hh, t = divmod(n, QT)
                        w = (t + 1) * P
                        dve.wait_ge(sem("c_scores"), 8 * i + (n + 1))
                        own.step(v.tensor_tensor(bank[SCORE_BANKS[n % 4]][:, t * P:w], bank[SCORE_BANKS[n % 4]][:, t * P:w], tri[:], ALU.add))
                        own.step(v.tensor_reduce(cst[:, 16 + n:17 + n], bank[SCORE_BANKS[n % 4]][:, 0:w], axis=AX, op=ALU.max, negate=True))
                        v.tensor_tensor(cst[:, 24 + n:25 + n], cst[:, 16 + n:17 + n], cst[:, 8 + 2 * t + hh:9 + 2 * t + hh],
                                        ALU.mult).then_inc(sem("c_max"), 1)

                    def out_(n):
                        hh, t = divmod(n, QT)
                        dve.wait_ge(sem("c_exp"), 8 * i + (n + 1))
                        own.step(v.reciprocal(cst[:, 40 + n:41 + n], cst[:, 32 + n:33 + n]))
                        dve.wait_ge(sem("c_weighed"), 8 * i + (n + 1))
                        v.tensor_scalar(mo_t[:, t, hh * P:hh * P + P], bank[4 + n % 2][:, 0:P], cst[:, 40 + n:41 + n], None,
                                        ALU.mult).then_inc(sem("c_out"), 1)

                    for n in range(8 + 2):
                        if n < 8:
                            peak(n)
                        if n >= 2:
                            out_(n - 2)
                    for hh in range(2):
                        dve.wait_ge(sem("c_mo_hi"), 2 * i + (hh + 1))
                        v.tensor_tensor(mo_lo[:, ds(2 * i + hh, 1), :], bank[6 + hh][:].unsqueeze(1),
                                        mo_hi[:, ds(2 * i + hh, 1), :].bitcast(F32), ALU.subtract).then_inc(sem("c_mo"), 1)
                ring("mla", 2, body, 42)

            def merge2_epi():
                def body(i, u, nxt):
                    nxt(u, 1)
                    nxt(u, 2)
                    dve.wait_ge(mm_done, u + 2)
                    dve.wait_ge(banks_free, u + 1)
                    own.step(v.tensor_tensor(nt[:, 3, :], bank[2][:], nt[:, 1, :], ALU.mult))
                    own.step(v.tensor_tensor(nt[:, ds(4, 1), :], aret[:, ds(i, 1), :], nt[:, ds(0, 1), :], ALU.mult))
                    v.tensor_tensor(nt[:, 2, :], nt[:, 3, :], nt[:, 4, :], ALU.add).then_inc(sem("mixed2"), 1)
                    v.memset(small[:, 23:24], 0.0).then_inc(banks_free, 1)
                    dve.wait_ge(sem("m2_hi_ready"), i + 1)
                    v.tensor_tensor(m2_lo[:, ds(i, 1), :], nt[:, ds(2, 1), :], m2_hi[:, ds(i, 1), :].bitcast(F32), ALU.subtract
                                    ).then_inc(sem("merged2"), 1)
                ring("merge2", 2, body, 2)

            def out2():
                def body(i, u, nxt):
                    for slot in range(2):
                        nxt(u, slot + 1)
                        if slot == 0 and isinstance(i, int) and i == 1:
                            for n in range(2):
                                dve.wait_ge(sem("p_hi_ready"), n + 1)
                                v.tensor_tensor(p_lo[:, n, :], bank[5 + n][:], p_hi[:, n, :].bitcast(F32), ALU.subtract
                                                ).then_inc(sem("p_made"), 1)
                        dve.wait_ge(mm_done, u + slot + 1)
                        for n in range(2):
                            f = ds(4 * i + (2 * slot + n), 1)
                            ins = v.tensor_tensor(xT[:, f, :], bank[2 * slot + n][:].unsqueeze(1), xT[:, f, :], ALU.add)
                            if n == 0:
                                own.step(ins)
                        ins.then_inc(banks_free, 1)
                ring("out2", 2, body, 2)

            def mlp():
                u = U0["ple_in"]
                split(u + 1)
                norm(2, vT[:, VROWS["norm_mlp"]:VROWS["norm_mlp"] + KD], None, {2: lambda: split(u + 2)})

                def body(i, u, nxt):
                    for k in range(4):
                        nxt(u, k + 1)
                        for n in range(2):
                            dve.wait_ge(sem("mlp_relu"), 8 * i + (2 * k + n + 1))
                            dve.wait_ge(sem("mlp_made"), 8 * i + max(2 * k + n - 1, 0))
                            v.tensor_tensor(nt[:, 4 + n, :], nt[:, n, :], nt[:, n, :], ALU.mult).then_inc(sem("mlp_squared"), 1)
                        for n in range(2):
                            dve.wait_ge(sem("mlp_hi"), 8 * i + (2 * k + n + 1))
                            v.tensor_tensor(u_lo[:, 2 * k + n, :], nt[:, 4 + n, :], u_hi[:, 2 * k + n, :].bitcast(F32), ALU.subtract
                                            ).then_inc(sem("mlp_made"), 1)
                    for k in range(4):
                        nxt(u, 4 + k + 1)
                        dve.wait_ge(mm_done, u + (5 + k))
                        dve.wait_ge(banks_free, u + (4 + k))
                        for n in range(2):
                            f = 2 * k + n
                            ins = v.tensor_tensor(xT[:, f, :], bank[2 * (k % 2) + n][:], xT[:, f, :], ALU.add)
                            if n == 0:
                                own.step(ins)
                        ins.then_inc(banks_free, 1)
                    dve.wait_ge(banks_free, u + 8)
                ring("mlp", 8, body, 4)

            def ple():
                norm(3, vT[:, VROWS["norm_ple"]:VROWS["norm_ple"] + KD])

                def body(i, u, nxt):
                    for slot in range(2):
                        nxt(u, slot + 1)
                        dve.wait_ge(banks_free, u + slot + 1)
                        for n in range(2):
                            k, f = 2 * slot + n, ds(4 * i + (2 * slot + n), 1)
                            own.step(v.tensor_tensor(nt[:, ds(4 + n, 1), :], nt[:, ds(k, 1), :], aret[:, f, :], ALU.mult))
                            v.tensor_tensor(xT[:, f, :], nt[:, ds(4 + n, 1), :], xT[:, f, :], ALU.add).then_inc(sem("x_done"), 1)
                            dve.wait_ge(sem("x_done"), 4 * i + (k + 1))
                ring("ple", 2, body, 4)
                for t in range(1, QT, 2):
                    dve.wait_ge(sem("out_mm"), QT + t + 1)
                    v.tensor_copy(out_sb[:, t, 512:D], bank[4 + t][:]).then_inc(sem("out_odd"), 1)

            prologue()
            index()
            values()
            qk()
            topk()
            attn_a()
            attn_b()
            turn_y()
            merge_epi()
            out1()
            norm2()
            ff()
            norm_mix()
            retention()
            latent()
            mla()
            merge2_epi()
            out2()
            mlp()
            ple()


NAMES = ['x', 'c', 'w_ada', 'b_ada', 'norm1_g', 'w_in', 'qn_a', 'kn_a', 'qn_b', 'kn_b', 'lam_q1', 'lam_k1',
         'lam_q2', 'lam_k2', 'subln_g', 'w_up_a', 'w_up_b', 'w_o', 'norm2_g', 'w_ff1', 'w_ff3', 'w_ff2',
         'p_2', 'positions_2', 'norm_mix_2', 'w_in_2', 'ret_norm_2', 'q_lat_norm_2', 'kv_lat_norm_2',
         'w_uq_2', 'w_ukv_2', 'q_norm_2', 'k_norm_2', 'w_br_2', 'w_bm_2', 'w_o_2', 'norm_mlp_2', 'w_up_2',
         'w_down_2', 'norm_ple_2', 'w_ple_gate_2', 'w_ple_2']


def shape_constants():
    p = np.arange(P, dtype=np.float32)
    table = np.zeros((P, 8), np.float32)
    table[:, 0] = np.float32(10000.0) ** (-p / np.float32(128))
    table[:, 1] = np.float32(10000.0) ** (-(p % 32) / np.float32(32))
    table[:, 2:2 + R_H] = np.log1p(-np.exp2(-5.0 - np.arange(R_H, dtype=np.float32)))
    return table


def kernel(**inputs):
    import concourse.bacc as bacc
    from concourse.bass_utils import run_bass_kernel_spmd

    nc = bacc.Bacc("TRN2", target_bir_lowering=False, num_devices=1)
    arrays, aps = {}, {}
    for name in NAMES:
        a = np.ascontiguousarray(inputs[name])
        arrays[f"in_{name}"] = a
        aps[name] = nc.dram_tensor(f"in_{name}", a.shape, mybir.dt.from_np(a.dtype), kind="ExternalInput").ap()
    arrays["in_shape_constants"] = shape_constants()
    aps["shape_constants"] = nc.dram_tensor("in_shape_constants", (P, 8), F32, kind="ExternalInput").ap()
    out = nc.dram_tensor("out", (1, S, D), F32, kind="ExternalOutput").ap()
    two_layers(nc, aps, out)
    r = run_bass_kernel_spmd(nc, [arrays], core_ids=[0])
    return r.results[0]["out"]
```
